# Optimizing a Trainium2 kernel written in Bass

```python
import math
import jax, jax.numpy as jnp
from jax import lax
import numpy as np

D_MODEL = 1024
BATCH = 1
SEQ = 1024
DEPTH = 1
DEC_BATCH = 1
DEC_SEQ = 512
PAST_LEN = 128

GRID_W = 64
N_Q_HEADS = 8
N_KV_HEADS = 2
HEAD_DIM = 64
GQA_GROUP = N_Q_HEADS // N_KV_HEADS
ROPE_HALF = HEAD_DIM // 2
ROPE_THETA = 10000.0
Q_BLOCK = 128
N_DN_HEADS = 4
DN_HEAD_DIM = 128
DN_CONV_K = 3
DN_CHUNK = 64
D_FF = 4 * D_MODEL
EPS = 1e-6

ATT_Q = N_Q_HEADS * HEAD_DIM
ATT_KV = N_KV_HEADS * HEAD_DIM
DN_W = N_DN_HEADS * DN_HEAD_DIM
PART_SIZES = [ATT_Q, ATT_KV, ATT_KV, 3 * DN_W, DN_W, 2 * N_DN_HEADS, 2 * N_DN_HEADS, 2 * D_MODEL]
PROJ_WIDTH = sum(PART_SIZES)
SPLIT_IDX = [int(v) for v in np.cumsum(PART_SIZES[:-1])]

kernel_name = "hybrid_gqa_gdn_bidir_encoder"

def rms_norm(x, g):
    xf = x.astype(jnp.float32)
    y = xf * lax.rsqrt(jnp.mean(xf * xf, axis=-1, keepdims=True) + EPS) * g.astype(jnp.float32)
    return y.astype(x.dtype)

def axial_rope_tables(T):
    rows = T // GRID_W
    row_ids = jnp.repeat(jnp.arange(rows, dtype=jnp.float32), GRID_W)
    col_ids = jnp.tile(jnp.arange(GRID_W, dtype=jnp.float32), rows)
    inv_freq = ROPE_THETA ** (-jnp.arange(0, ROPE_HALF, 2, dtype=jnp.float32) / ROPE_HALF)
    ang_r = row_ids[:, None] * inv_freq
    ang_c = col_ids[:, None] * inv_freq
    return jnp.cos(ang_r), jnp.sin(ang_r), jnp.cos(ang_c), jnp.sin(ang_c)

def rope_rotate(x, cos, sin):
    m = x.shape[-1] // 2
    x1, x2 = x[..., :m], x[..., m:]
    c, s = cos[:, None, :], sin[:, None, :]
    return jnp.concatenate([x1 * c - x2 * s, x2 * c + x1 * s], axis=-1)

def apply_axial_rope(x, tables):
    cos_r, sin_r, cos_c, sin_c = tables
    xf = x.astype(jnp.float32)
    out = jnp.concatenate([rope_rotate(xf[..., :ROPE_HALF], cos_r, sin_r),
                           rope_rotate(xf[..., ROPE_HALF:], cos_c, sin_c)], axis=-1)
    return out.astype(x.dtype)

def blocked_gqa_attention(q, k, v):
    B, T = q.shape[0], q.shape[1]
    nb = T // Q_BLOCK
    scale = HEAD_DIM ** -0.5
    qb = q.reshape(B, nb, Q_BLOCK, N_KV_HEADS, GQA_GROUP, HEAD_DIM).transpose(1, 0, 2, 3, 4, 5)

    def one_block(q_blk):
        s = jnp.einsum('bqkgd,bskd->bkgqs', q_blk, k).astype(jnp.float32) * scale
        p = jax.nn.softmax(s, axis=-1).astype(v.dtype)
        return jnp.einsum('bkgqs,bskd->bqkgd', p, v)

    o = lax.map(one_block, qb)
    return o.transpose(1, 0, 2, 3, 4, 5).reshape(B, T, ATT_Q)

def gated_delta_rule_chunked(q, k, v, g, beta):
    B, T, H, DK = q.shape
    DV = v.shape[-1]
    n = T // DN_CHUNK

    def chunks(x):
        return x.reshape(B, n, DN_CHUNK, H, x.shape[-1]).transpose(1, 0, 3, 2, 4)

    qc = chunks(q) * (DK ** -0.5)
    kc = chunks(k)
    vc = chunks(v)
    gc = jnp.cumsum(chunks(g[..., None])[..., 0], axis=-1)
    bc = chunks(beta[..., None])[..., 0]
    idx = jnp.arange(DN_CHUNK)
    incl = idx[:, None] >= idx[None, :]
    strict = idx[:, None] > idx[None, :]
    decay = jnp.exp(jnp.where(incl, gc[..., :, None] - gc[..., None, :], -jnp.inf))
    kk = jnp.einsum('nbhcd,nbhed->nbhce', kc, kc)
    lower = jnp.where(strict, bc[..., :, None] * kk * decay, 0.0)
    eye = jnp.eye(DN_CHUNK, dtype=jnp.float32)
    tinv = lax.linalg.triangular_solve(lower + eye, jnp.broadcast_to(eye, lower.shape),
                                       left_side=True, lower=True, unit_diagonal=True)
    u = tinv @ (vc * bc[..., None])
    w = tinv @ (kc * (bc * jnp.exp(gc))[..., None])
    qk = jnp.einsum('nbhcd,nbhed->nbhce', qc, kc) * decay
    q_dec = qc * jnp.exp(gc)[..., None]
    g_last = gc[..., -1]
    k_dec = kc * jnp.exp(g_last[..., None] - gc)[..., None]

    def step(state, xs):
        u_i, w_i, qk_i, q_i, k_i, gl_i = xs
        v_new = u_i - w_i @ state
        o_i = q_i @ state + qk_i @ v_new
        state = state * jnp.exp(gl_i)[..., None, None] + jnp.einsum('bhcd,bhce->bhde', k_i, v_new)
        return state, o_i

    state0 = jnp.zeros((B, H, DK, DV), jnp.float32)
    _, o = lax.scan(step, state0, (u, w, qk, q_dec, k_dec, g_last))
    return o.transpose(1, 0, 3, 2, 4).reshape(B, T, H, DV)

def l2_normalise(x):
    return x * lax.rsqrt(jnp.sum(x * x, axis=-1, keepdims=True) + EPS)

def token_mixer(h, w_in, q_norm_g, k_norm_g, conv_w, A_log, dt_bias, dn_norm_g,
                w_attn_branch, w_dn_branch, w_out):
    B, T, _ = h.shape
    proj = h @ w_in
    aq, ak, av, dqkv, dz, dbeta, da, gates = jnp.split(proj, SPLIT_IDX, axis=-1)

    tables = axial_rope_tables(T)
    aq = apply_axial_rope(rms_norm(aq.reshape(B, T, N_Q_HEADS, HEAD_DIM), q_norm_g), tables)
    ak = apply_axial_rope(rms_norm(ak.reshape(B, T, N_KV_HEADS, HEAD_DIM), k_norm_g), tables)
    av = av.reshape(B, T, N_KV_HEADS, HEAD_DIM)
    attn_out = blocked_gqa_attention(aq, ak, av)

    pad = DN_CONV_K // 2
    dqkv = lax.conv_general_dilated(dqkv, conv_w[:, None, :], window_strides=(1,),
                                    padding=((pad, pad),), dimension_numbers=('NWC', 'WIO', 'NWC'),
                                    feature_group_count=3 * DN_W)
    dqkv = jax.nn.silu(dqkv).astype(jnp.float32)
    dq, dk, dv = jnp.split(dqkv, 3, axis=-1)
    dq = l2_normalise(dq.reshape(B, T, N_DN_HEADS, DN_HEAD_DIM))
    dk = l2_normalise(dk.reshape(B, T, N_DN_HEADS, DN_HEAD_DIM))
    dv = dv.reshape(B, T, N_DN_HEADS, DN_HEAD_DIM)
    beta = jax.nn.sigmoid(dbeta.astype(jnp.float32)).reshape(B, T, 2, N_DN_HEADS)
    g = -jnp.exp(A_log.astype(jnp.float32)) * jax.nn.softplus(
        da.astype(jnp.float32).reshape(B, T, 2, N_DN_HEADS) + dt_bias.astype(jnp.float32))
    flip = lambda a: a[:, ::-1]
    o_fwd = gated_delta_rule_chunked(dq, dk, dv, g[:, :, 0], beta[:, :, 0])
    o_bwd = flip(gated_delta_rule_chunked(flip(dq), flip(dk), flip(dv),
                                          flip(g[:, :, 1]), flip(beta[:, :, 1])))
    o = o_fwd + o_bwd
    z = jax.nn.silu(dz.astype(jnp.float32).reshape(B, T, N_DN_HEADS, DN_HEAD_DIM))
    dn_out = (rms_norm(o, dn_norm_g) * z).reshape(B, T, DN_W).astype(h.dtype)

    g_a, g_b = jnp.split(gates, 2, axis=-1)
    merged = jax.nn.sigmoid(g_a) * (attn_out @ w_attn_branch) + jax.nn.sigmoid(g_b) * (dn_out @ w_dn_branch)
    return merged @ w_out

def trunk(x, ln1_pre_g, w_in, attn_q_norm_g, attn_k_norm_g, dn_conv_w, dn_A_log, dn_dt_bias,
          dn_out_norm_g, w_attn_branch, w_dn_branch, w_out, ln1_post_g, ln2_pre_g,
          w_ff_in, w_ff_out, ln2_post_g):
    for l in range(DEPTH):
        mix = token_mixer(rms_norm(x, ln1_pre_g[l]), w_in[l], attn_q_norm_g[l], attn_k_norm_g[l],
                          dn_conv_w[l], dn_A_log[l], dn_dt_bias[l], dn_out_norm_g[l],
                          w_attn_branch[l], w_dn_branch[l], w_out[l])
        x = x + rms_norm(mix, ln1_post_g[l])
        hid = jnp.square(jax.nn.relu(rms_norm(x, ln2_pre_g[l]) @ w_ff_in[l]))
        x = x + rms_norm(hid @ w_ff_out[l], ln2_post_g[l])
    return x

def setup_inputs(seed: int = 0) -> dict:
    key = jax.random.key(seed)
    ks = jax.random.split(key, 20)
    f32 = jnp.float32

    def nrm(k, shape, fan_in):
        return jax.random.normal(k, shape, f32) * fan_in ** -0.5

    def gain(k, shape):
        return 1.0 + 0.05 * jax.random.normal(k, shape, f32)

    dt = jnp.exp(jax.random.uniform(ks[8], (DEPTH, 2, N_DN_HEADS), f32,
                                    minval=math.log(1e-3), maxval=math.log(1e-1)))
    return {
        "x_prompt": jax.random.normal(ks[0], (BATCH, SEQ, D_MODEL), f32),
        "x_sample": jax.random.normal(ks[1], (DEC_BATCH, DEC_SEQ, D_MODEL), f32),
        "ln1_pre_g": gain(ks[2], (DEPTH, D_MODEL)),
        "w_in": nrm(ks[3], (DEPTH, D_MODEL, PROJ_WIDTH), D_MODEL),
        "attn_q_norm_g": gain(ks[4], (DEPTH, HEAD_DIM)),
        "attn_k_norm_g": gain(ks[5], (DEPTH, HEAD_DIM)),
        "dn_conv_w": nrm(ks[6], (DEPTH, DN_CONV_K, 3 * DN_W), DN_CONV_K),
        "dn_A_log": jnp.log(jax.random.uniform(ks[7], (DEPTH, 2, N_DN_HEADS), f32, minval=1.0, maxval=16.0)),
        "dn_dt_bias": dt + jnp.log(-jnp.expm1(-dt)),
        "dn_out_norm_g": gain(ks[9], (DEPTH, DN_HEAD_DIM)),
        "w_attn_branch": nrm(ks[10], (DEPTH, ATT_Q, D_MODEL), ATT_Q),
        "w_dn_branch": nrm(ks[11], (DEPTH, DN_W, D_MODEL), DN_W),
        "w_out": nrm(ks[12], (DEPTH, D_MODEL, D_MODEL), D_MODEL),
        "ln1_post_g": gain(ks[13], (DEPTH, D_MODEL)),
        "ln2_pre_g": gain(ks[14], (DEPTH, D_MODEL)),
        "w_ff_in": nrm(ks[15], (DEPTH, D_MODEL, D_FF), D_MODEL),
        "w_ff_out": nrm(ks[16], (DEPTH, D_FF, D_MODEL), D_FF),
        "ln2_post_g": gain(ks[17], (DEPTH, D_MODEL)),
    }

def reference(x_prompt, x_sample, ln1_pre_g, w_in, attn_q_norm_g, attn_k_norm_g, dn_conv_w,
              dn_A_log, dn_dt_bias, dn_out_norm_g, w_attn_branch, w_dn_branch, w_out,
              ln1_post_g, ln2_pre_g, w_ff_in, w_ff_out, ln2_post_g):
    y_prompt = trunk(x_prompt, ln1_pre_g, w_in, attn_q_norm_g, attn_k_norm_g, dn_conv_w, dn_A_log,
                     dn_dt_bias, dn_out_norm_g, w_attn_branch, w_dn_branch, w_out, ln1_post_g,
                     ln2_pre_g, w_ff_in, w_ff_out, ln2_post_g)
    y_sample = trunk(x_sample, ln1_pre_g, w_in, attn_q_norm_g, attn_k_norm_g, dn_conv_w, dn_A_log,
                     dn_dt_bias, dn_out_norm_g, w_attn_branch, w_dn_branch, w_out, ln1_post_g,
                     ln2_pre_g, w_ff_in, w_ff_out, ln2_post_g)
    return (y_prompt, y_sample)


_drawn_inputs = setup_inputs


def setup_inputs(seed=0):
    import zlib

    import numpy as np

    out = dict(_drawn_inputs(seed))
    spreads = {}
    factors = {'attn_q_norm_g': 8.0, 'attn_k_norm_g': 8.0}
    for name, (base, spread) in spreads.items():
        noise = np.random.default_rng([zlib.crc32(name.encode()), seed]).standard_normal(out[name].shape)
        drawn = base * np.exp(spread * noise) if base else spread * noise
        out[name] = __import__('jax').numpy.asarray(drawn.astype(out[name].dtype))
    for name, factor in factors.items():
        out[name] = (out[name] * factor).astype(out[name].dtype)
    return out
```

```python
from contextlib import ExitStack

import concourse.bass as bass
from concourse import mybir
import numpy as np

F32 = mybir.dt.float32
F32R = mybir.dt.float32r
ACT = mybir.ActivationFunctionType
ALU = mybir.AluOpType
AX = mybir.AxisListType

P = 128
D = 1024
KD = D // P
T0, T1 = 1024, 512
TOK = T0 + T1
NT = TOK // P
SEQS = [(0, T0 // P), (T0 // P, T1 // P)]
NG = TOK // 512
GRID_W = 64
NQH, NKVH, HD = 8, 2, 64
NH, DH = 4, 128
DNW = NH * DH
DFF = 4 * D
EPS = 1e-6
QKV_W = NQH * HD + 2 * NKVH * HD
DQKV_COL = QKV_W
DZ_COL = DQKV_COL + 3 * DNW
BA_COL = DZ_COL + DNW
GATE_COL = BA_COL + 4 * NH
PROJ_W = GATE_COL + 2 * D


def f32(ap):
    return ap.bitcast(F32)


def along(ap, axis, n):
    a = ap.unsqueeze(axis)
    shape = list(a.shape)
    shape[axis] = n
    return a.to_broadcast(shape)


def hold(pool, passed, sem, value):
    pool.wait_ge(sem, value)
    pool.sem_inc(passed, 1)


class Core:

    def __init__(self, nc, ctx, phase):
        self.nc, self.ctx, self.phase = nc, ctx, phase
        self.sems = []

    def sb(self, name, shape, dt=F32):
        return self.ctx.enter_context(self.nc.sbuf_tensor(name, shape, dt))

    def ps(self, name, shape):
        return self.ctx.enter_context(self.nc.psum_tensor(name, shape, F32))

    def sem(self, name):
        s = self.nc.alloc_semaphore(f"{self.phase}_{name}")
        self.sems.append(s)
        return s

    def sems2(self, name):
        return [self.sem(f"{name}{u}") for u in range(2)]


def end_phase(nc, core):
    nc.clear_and_free_semaphores(core.sems)
    nc.all_engine_barrier()


def split_matmuls(pe, out, pairs, n_k):
    for k in range(n_k):
        for first, (wi, xi) in enumerate(((0, 2), (0, 3), (1, 2))):
            for g, bank in enumerate(out):
                ops = pairs(k, g)
                mm = pe.matmul(bank, ops[wi], ops[xi], start=(k == 0 and first == 0),
                               stop=(k == n_k - 1 and first == 2))
    return mm


def uses(u, t, per):
    return (t + (2 - u)) * (per // 2)


def ahead(eng, n, stage1, stage2, early=None):
    def first(u, t):
        if early:
            early(u, t)
    stage1(0, 0)
    with eng.Fori(0, n // 2 - 1) as i:
        first(0, i * 2)
        stage1(1, i * 2 + 1)
        stage2(0, i * 2)
        first(1, i * 2 + 1)
        stage1(0, i * 2 + 2)
        stage2(1, i * 2 + 1)
    first(0, n - 2)
    stage1(1, n - 1)
    stage2(0, n - 2)
    first(1, n - 1)
    stage2(1, n - 1)


def project(nc, io):
    with ExitStack() as ctx:
        c = Core(nc, ctx, "project")
        ht_hi = c.sb("ht_hi", [P, KD, TOK], F32R)
        ht_lo = c.sb("ht_lo", [P, KD, TOK], F32R)
        xt = c.sb("xt", [P, 2, D])
        gain = c.sb("ln1_gain", [P, D])
        ident = c.sb("ident_a", [P, P])
        stat = c.sb("x_stat", [P, 2, 3])
        mhalf = c.sb("mhalf_a", [P, 1])
        raw = c.sb("win_raw", [P, 2, KD, P])
        whi = c.sb("win_hi", [P, 2, KD, P], F32R)
        wlo = c.sb("win_lo", [P, 2, KD, P], F32R)
        stage = c.sb("proj_stage", [P, 2, TOK])
        conv = c.sb("conv_out", [P, TOK])
        taps = c.sb("conv_taps", [P, 2, 3])
        xn = [stage[:, u, 0:D] for u in range(2)]
        acc = c.ps("proj_ps", [P, 2, NG, 512])
        xps = c.ps("xt_ps", [P, 2, 512])

        x_in = c.sems2("x_in")
        const_in, ss_done, ms_done, rstd_done = (c.sem(n) for n in ("const_in", "ss_done", "ms_done", "rstd_done"))
        xn_done, xt_done, hi_done, lo_done = (c.sem(n) for n in ("xn_done", "xt_done", "hi_done", "lo_done"))
        mhalf_done, passed = c.sem("mhalf_done"), c.sem("passed")
        w_in, w_hi, w_ready, acc_done = (c.sems2(n) for n in ("w_in", "w_hi", "w_ready", "acc_done"))
        acc_used, stage_done, stored = (c.sems2(n) for n in ("acc_used", "stage_done", "stored"))
        taps_in, conv_step, sig_done, silu_done = c.sems2("taps_in"), c.sem("conv_step"), c.sems2("sig_done"), c.sems2("silu_done")

        w_cols = io["w_in"].rearrange("(ko p) n -> p ko n", p=P)
        groups = [("plain", 0, QKV_W // 256, io["qkv_s"], 0),
                  ("conv", DQKV_COL, 3 * DNW // 256, io["dqkv_s"], 0),
                  ("silu", DZ_COL, DNW // 256, io["z_s"], 0),
                  ("ba", BA_COL, 0.5, io["ba_s"], 0),
                  ("gate", GATE_COL, 2 * D // 256, io["gate_s"], 0)]

        def tiles(eng, body, kinds=("plain", "conv", "silu", "ba", "gate"), start=0):
            done = [0, 0]
            for kind, col0, pairs, dst, row0 in groups:
                if kind not in kinds:
                    done = [d + (pairs if pairs != 0.5 else 1 - u) for u, d in enumerate(done)]
                    continue
                if pairs == 0.5:
                    body(0, done[0] + 1, kind, col0, dst, row0)
                    done[0] += 1
                    continue
                with eng.Fori(start if kind == "plain" else 0, pairs) as i:
                    for u in range(2):
                        body(u, i + done[u] + 1, kind, i * 256 + (col0 + u * P), dst, i * 256 + (row0 + u * P))
                done = [d + pairs for d in done]
            return done

        block = ctx.enter_context(nc.Block("project"))

        @block.sync
        def _(sp):
            sp.dma_start(gain[:], io["ln1_pre_g"][0].partition_broadcast(P)).then_inc(const_in, 16)
            sp.dma_start(ident[:], io["ident"]).then_inc(const_in, 16)
            def load(u, n, kind, col, dst, row):
                sp.wait_ge(w_ready[u], n)
                sp.dma_start(raw[:, u], w_cols[:, :, bass.ds(col, P)]).then_inc(w_in[u], 16)
                if kind == "conv":
                    sp.wait_ge(silu_done[u], n - QKV_W // 256)
                    sp.dma_start(taps[:, u, :], io["conv_w"][bass.ds(row, P), :]).then_inc(taps_in[u], 16)
            for u in range(2):
                load(u, 1, "plain", u * P, io["qkv_s"], 0)
            with sp.Fori(0, NT // 2) as i:
                for u in range(2):
                    sp.wait_ge(xn_done, i * 2 + (u + 1))
                    sp.dma_start(xt[:, u, :], io["x"][bass.ds(i * 256 + u * P, P), :]).then_inc(x_in[u], 16)
            tiles(sp, load, start=1)

        @block.gpsimd
        def _(pool):
            pool.memset(mhalf[:], -0.5).then_inc(mhalf_done, 1)
            for u in range(2):
                pool.sem_inc(w_ready[u], 1)
            pool.wait_ge(mhalf_done, 1)
            with pool.Fori(0, NT // 2) as i:
                for u in range(2):
                    t = i * 2 + u
                    hold(pool, passed, ss_done, t + 1)
                    pool.tensor_scalar(stat[:, u, 1:2], stat[:, u, 0:1], 1.0 / D, EPS, ALU.mult, ALU.add).then_inc(ms_done, 1)
                    pool.wait_ge(ms_done, t + 1)
                    pool.tensor_tensor(stat[:, u, 2:3], stat[:, u, 1:2], mhalf[:], ALU.pow).then_inc(rstd_done, 1)
            def split(u, n, kind, col, dst, row):
                pool.wait_ge(w_in[u], n * 16)
                hold(pool, passed, acc_done[u], n)
                pool.tensor_copy(whi[:, u], raw[:, u]).then_inc(w_hi[u], 1)
                pool.wait_ge(w_hi[u], n)
                pool.tensor_tensor(wlo[:, u], raw[:, u], f32(whi[:, u]), ALU.subtract).then_inc(w_ready[u], 1)
            tiles(pool, split)

        @block.tensor
        def _(pe):
            for u in range(2):
                pe.sem_inc(acc_done[u], 1)
            pe.wait_ge(const_in, 32)
            with pe.Fori(0, NT // 2) as i:
                for u in range(2):
                    t = i * 2 + u
                    pe.wait_ge(xn_done, t + 3)
                    for half in range(2):
                        pe.wait_ge(lo_done, t * 2 + (half + 1))
                        for k in range(4):
                            tr = pe.transpose(xps[:, half, k * P:(k + 1) * P], xn[u][:, (4 * half + k) * P:(4 * half + k + 1) * P], ident[:])
                        tr.then_inc(xt_done, 1)
            pe.wait_ge(lo_done, 2 * NT + 2)

            def products(u, n, kind, col, dst, row):
                pe.wait_ge(w_ready[u], n + 1)
                pe.wait_ge(acc_used[u], n)
                split_matmuls(pe, [acc[:, u, g] for g in range(NG)],
                              lambda k, g: (whi[:, u, k], wlo[:, u, k], ht_hi[:, k, g * 512:(g + 1) * 512],
                                            ht_lo[:, k, g * 512:(g + 1) * 512]), KD).then_inc(acc_done[u], 1)
            tiles(pe, products)

        @block.scalar
        def _(act):
            for u in range(2):
                act.sem_inc(acc_used[u], 1)
                act.sem_inc(stored[u], 16)

            def square(u, t):
                act.wait_ge(x_in[u], uses(u, t, 16))
                act.activation(acc[:, u, 0:2].rearrange("p g t -> p (g t)"), xt[:, u, :], ACT.Square, accum_out=stat[:, u, 0:1]).then_inc(ss_done, 1)

            def copy_hi(u, t):
                for half in range(2):
                    act.wait_ge(xt_done, t * 2 + (half + 1))
                    act.activation(ht_hi[:, 4 * half:4 * half + 4, bass.ds(t * P, P)],
                                   xps[:, half].rearrange("p (k t) -> p k t", k=4), ACT.Copy).then_inc(hi_done, 1)
            ahead(act, NT, square, copy_hi)

            def evacuate(u, n, kind, col, dst, row):
                act.wait_ge(acc_done[u], n + 1)
                act.wait_ge(stored[u], n * 16)
                banks = acc[:, u].rearrange("p g t -> p (g t)")
                if kind in ("plain", "ba", "conv", "silu"):
                    act.activation(stage[:, u], banks, ACT.Copy).then_inc(acc_used[u], 1)
                if kind == "gate":
                    act.activation(stage[:, u], banks, ACT.Sigmoid).then_inc(acc_used[u], 1)
                if kind == "conv":
                    act.wait_ge(conv_step, (n - QKV_W // 256 - 1) * 6 + 3 * u + 3)
                    act.activation(stage[:, u], conv[:], ACT.Sigmoid).then_inc(sig_done[u], 1)
                if kind == "silu":
                    act.wait_ge(acc_used[u], n + 1)
                    act.activation(conv[:], stage[:, u], ACT.Sigmoid).then_inc(sig_done[u], 1)
                if kind in ("conv", "silu"):
                    act.wait_ge(silu_done[u], n - QKV_W // 256 + 1)
                else:
                    act.wait_ge(acc_used[u], n + 1)
                if kind == "ba":
                    act.dma_start(dst, stage[0:4 * NH, u]).then_inc(stored[u], 16)
                else:
                    act.dma_start(dst[bass.ds(row, P), :], stage[:, u]).then_inc(stored[u], 16)
            done = tiles(act, evacuate)
            for u in range(2):
                act.wait_ge(stored[u], 16 * done[u] + 16)

        @block.vector
        def _(dve):
            for u in range(2):
                dve.sem_inc(silu_done[u], 1)
            dve.sem_inc(lo_done, 2)
            dve.sem_inc(xn_done, 2)
            dve.wait_ge(const_in, 32)

            def normalise(u, t):
                dve.wait_ge(rstd_done, t + 1)
                dve.scalar_tensor_tensor(xn[u], xt[:, u, :], stat[:, u, 2:3], gain[:], ALU.mult, ALU.mult).then_inc(xn_done, 1)

            def subtract_hi(u, t):
                for half in range(2):
                    dve.wait_ge(hi_done, t * 2 + (half + 1))
                    out = ht_lo[:, 4 * half:4 * half + 4, bass.ds(t * P, P)]
                    hi = f32(ht_hi[:, 4 * half:4 * half + 4, bass.ds(t * P, P)])
                    dve.tensor_tensor(out, xps[:, half].rearrange("p (k t) -> p k t", k=4), hi, ALU.subtract).then_inc(lo_done, 1)
            ahead(dve, NT, normalise, subtract_hi)

            def act_on(u, n, kind, col, dst, row):
                m = n - QKV_W // 256
                if kind == "conv":
                    x, s = stage[:, u], (m - 1) * 6 + 3 * u
                    dve.wait_ge(taps_in[u], m * 16)
                    dve.wait_ge(acc_used[u], n + 1)
                    dve.tensor_scalar(conv[:], x, taps[:, u, 1:2], None, ALU.mult).then_inc(conv_step, 1)
                    dve.wait_ge(conv_step, s + 1)
                    for a, b in ((0, T0), (T0, TOK)):
                        op = dve.scalar_tensor_tensor(conv[:, a + 1:b], x[:, a:b - 1], taps[:, u, 0:1],
                                                      conv[:, a + 1:b], ALU.mult, ALU.add)
                    op.then_inc(conv_step, 1)
                    dve.wait_ge(conv_step, s + 2)
                    for a, b in ((0, T0), (T0, TOK)):
                        op = dve.scalar_tensor_tensor(conv[:, a:b - 1], x[:, a + 1:b], taps[:, u, 2:3],
                                                      conv[:, a:b - 1], ALU.mult, ALU.add)
                    op.then_inc(conv_step, 1)
                if kind in ("conv", "silu"):
                    dve.wait_ge(sig_done[u], m)
                    dve.tensor_tensor(stage[:, u], stage[:, u], conv[:], ALU.mult).then_inc(silu_done[u], 1)
            tiles(dve, act_on, ("conv", "silu"))
    end_phase(nc, c)


def prepare(nc, io):
    B = 3
    NQK = NQH + NKVH
    QK = NQK * HD
    with ExitStack() as ctx:
        c = Core(nc, ctx, "prepare")
        feat = c.sb("feat", [P, B, 22, P])
        feat_ba = c.sb("feat_ba", [4 * NH, B, P])
        rope = c.sb("rope", [P, NT, 2, HD])
        qk = c.sb("qk_tok", [P, B, NQK, HD])
        qk_sq = c.sb("qk_sq", [P, B, NQK, HD])
        qk_g = c.sb("qk_gained", [P, B, NQK, HD])
        rot_a = c.sb("rot_a", [P, B, NQK, HD])
        rot_b = c.sb("rot_b", [P, B, NQK, HD])
        rstd = c.sb("qk_rstd", [P, B, 2, NQK])
        q_split = c.sb("q_split", [P, B, NQH, 2, HD], F32R)
        k_split = c.sb("k_split", [P, B, NKVH, 2, 2, HD], F32R)
        v_split = c.sb("v_split", [P, B, NKVH, 2, HD], F32R)
        dn_sq = c.sb("dn_sq", [P, B, 2 * NH, DH])
        dn_rs = c.sb("dn_rs", [P, B, 2, 2 * NH])
        dn_q = c.sb("dn_q", [P, B, DNW])
        pack = c.sb("dn_pack", [P, B, 5, DNW])
        qt = c.sb("q_t", [P, B, NQH, P])
        kt = c.sb("k_t", [P, B, 2 * NKVH, P])
        ba = c.sb("ba_tok", [P, NT, 4 * NH])
        gain = c.sb("qk_gain", [P, NQK, HD])
        ident = c.sb("ident_b", [P, P])
        mhalf = c.sb("mhalf_b", [P, NQK])
        gates = c.sb("dn_gates", [P, 6, NT, 2 * NH])
        alog = c.sb("alog_row", [P, 2, 2 * NH])
        dtb = c.sb("dtb_row", [P, 2 * NH])
        one = c.sb("one_b", [P, 1])
        ps = c.ps("prep_ps", [P, 8, 512])
        K_TOK, V_TOK, K_T, Q_T, Z_TOK = range(5)

        tile_in, stored = ([c.sem(f"{n}{u}") for u in range(B)] for n in ("tile_in", "p_stored"))
        names = ("const_in", "rope_in", "const_done", "passed", "qkv_turned", "dn_turned", "qkv_copied", "qk_squared", "dn_copied",
                 "v_lo_done", "qk_summed", "dn_summed", "qk_rms", "dn_rs_done", "qk_scaled", "dn_scaled", "qk_gained",
                 "rot_b_done", "rot_step", "split_done", "back_turned", "back_copied", "pool_step", "gate_step", "x_done")
        s = {n: c.sem(n) for n in names}

        def pipeline(eng, turn, scale, finish):
            turn(0, 0, 0)
            with eng.Fori(0, NT // B - 1) as i:
                for u in range(B):
                    scale(u, i * B + u, i)
                    turn((u + 1) % B, i * B + u + 1, i + (u + 1) // B)
                    finish(u, i * B + u, i)
            for t in range(NT - B, NT):
                scale(t % B, t, t // B)
                if t + 1 < NT:
                    turn((t + 1) % B, t + 1, (t + 1) // B)
                finish(t % B, t, t // B)

        def none(u, t, n):
            pass

        with nc.Block("prepare") as block:
            @block.sync
            def _(sp):
                for dst, src in ((gain[:, 0], "attn_q_norm_g"), (gain[:, NQH], "attn_k_norm_g")):
                    sp.dma_start(dst, io[src][0].partition_broadcast(P)).then_inc(s["const_in"], 16)
                sp.dma_start(ident[:], io["ident"]).then_inc(s["const_in"], 16)
                sp.dma_start(alog[:, 0], io["dn_A_log"].rearrange("a b -> (a b)").partition_broadcast(P)).then_inc(s["const_in"], 16)
                sp.dma_start(dtb[:], io["dn_dt_bias"].rearrange("a b -> (a b)").partition_broadcast(P)).then_inc(s["const_in"], 16)
                sp.dma_start(rope[:], io["rope"].rearrange("(t p) (a d) -> p t a d", p=P, a=2)).then_inc(s["rope_in"], 16)
                with sp.Fori(0, NT // B) as i:
                    for u in range(B):
                        tok = bass.ds(i * B * P + u * P, P)
                        sp.wait_ge(s["dn_turned"], i * B + (u + 1))
                        for a, b, src in ((0, 6, "qkv_s"), (6, 18, "dqkv_s"), (18, 22, "z_s")):
                            sp.dma_start(feat[:, u, a:b], io[src].rearrange("(n p) t -> p n t", p=P)[:, :, tok]).then_inc(tile_in[u], 16)
                        sp.dma_start(feat_ba[:, u], io["ba_s"][:, tok]).then_inc(tile_in[u], 16)

            @block.tensor
            def _(pe):
                pe.sem_inc(s["dn_turned"], B)
                pe.wait_ge(s["const_in"], 80)

                def turn(u, t, n):
                    pe.wait_ge(tile_in[u], n * 64 + 64)
                    pe.wait_ge(s["qkv_copied"], t + 1)
                    pe.wait_ge(s["v_lo_done"], t + 1)
                    for k in range(6):
                        pe.transpose(ps[:, k // 4, (k % 4) * P:(k % 4 + 1) * P], feat[:, u, k], ident[:])
                    pe.transpose(ps[:, 1, 256:256 + 4 * NH], feat_ba[:, u], ident[0:4 * NH, 0:4 * NH]).then_inc(s["qkv_turned"], 1)
                    pe.wait_ge(s["dn_copied"], t + 1)
                    pe.wait_ge(s["dn_scaled"], t + 1)
                    for k in range(16):
                        tr = pe.transpose(ps[:, 2 + k // 4, (k % 4) * P:(k % 4 + 1) * P], feat[:, u, 6 + k], ident[:])
                    tr.then_inc(s["dn_turned"], 1)

                def finish(u, t, n):
                    sources = [dn_q[:, u].rearrange("p (h d) -> p h d", h=NH),
                               pack[:, u, K_TOK].rearrange("p (h d) -> p h d", h=NH),
                               f32(q_split[:, u, 0:4]).rearrange("p h s d -> p h (s d)"),
                               f32(q_split[:, u, 4:8]).rearrange("p h s d -> p h (s d)"),
                               f32(k_split[:, u]).rearrange("p h s r d -> p (h s) (r d)")]
                    pe.wait_ge(s["dn_scaled"], t + 2)
                    for g, src in enumerate(sources):
                        if g == 2:
                            pe.wait_ge(s["split_done"], t + 1)
                        pe.wait_ge(s["back_copied"], t * 5 + max(g + 1, 2))
                        for k in range(4):
                            tr = pe.transpose(ps[:, 6 + g % 2, k * P:(k + 1) * P], src[:, k], ident[:])
                        tr.then_inc(s["back_turned"], 1)
                pipeline(pe, turn, none, finish)

            @block.scalar
            def _(act):
                for u in range(B):
                    act.sem_inc(stored[u], 64)
                for n in ("qkv_copied", "dn_copied"):
                    act.sem_inc(s[n], 1)
                act.sem_inc(s["back_copied"], 2)

                def turn(u, t, n):
                    act.wait_ge(s["qkv_turned"], t + 1)
                    act.wait_ge(stored[u], n * 64 + 64)
                    act.activation(qk[:, u, 0:NQH], ps[:, 0].rearrange("p (n d) -> p n d", d=HD), ACT.Copy)
                    act.activation(qk[:, u, NQH:NQK], ps[:, 1, 0:P].rearrange("p (n d) -> p n d", d=HD), ACT.Copy)
                    act.activation(v_split[:, u, :, 0], ps[:, 1, P:2 * P].rearrange("p (n d) -> p n d", d=HD), ACT.Copy)
                    act.activation(ba[:, bass.ds(t, 1), :].rearrange("p a n -> p (a n)"), ps[:, 1, 256:256 + 4 * NH], ACT.Copy).then_inc(s["qkv_copied"], 1)
                    act.wait_ge(s["qkv_copied"], t + 2)
                    act.activation(qk_sq[:, u], qk[:, u], ACT.Square).then_inc(s["qk_squared"], 1)
                    act.wait_ge(s["dn_turned"], t + (B + 1))
                    act.activation(dn_sq[:, u], ps[:, 2:4].rearrange("p b (n d) -> p (b n) d", d=DH), ACT.Square)
                    act.activation(pack[:, u, V_TOK], ps[:, 4], ACT.Copy)
                    act.activation(pack[:, u, Z_TOK], ps[:, 5], ACT.Copy).then_inc(s["dn_copied"], 1)

                def finish(u, t, n):
                    targets = [pack[:, u, Q_T].rearrange("p (h d) -> p h d", h=NH),
                               pack[:, u, K_T].rearrange("p (h d) -> p h d", h=NH), qt[:, u, 0:4], qt[:, u, 4:8], kt[:, u]]
                    for g, dst in enumerate(targets):
                        act.wait_ge(s["back_turned"], t * 5 + (g + 1))
                        act.activation(dst, ps[:, 6 + g % 2].rearrange("p (n d) -> p n d", n=4), ACT.Copy).then_inc(s["back_copied"], 1)
                    act.wait_ge(s["back_copied"], t * 5 + 7)
                    act.wait_ge(s["v_lo_done"], t + 2)
                    tok = bass.ds(t * P, P)
                    act.dma_start(io["q_s"][:, :, tok].rearrange("h p t -> p h t"), qt[:, u]).then_inc(stored[u], 16)
                    act.dma_start(io["k_s"][:, :, tok].rearrange("h p t -> p h t"), kt[:, u]).then_inc(stored[u], 16)
                    act.dma_start(io["v_s"][:, :, bass.ds(t, 1), :].rearrange("h p a d -> p h (a d)"),
                                  f32(v_split[:, u]).rearrange("p h s d -> p h (s d)")).then_inc(stored[u], 16)
                    act.dma_start(io["dn_s"][bass.ds(t, 1)].rearrange("a p n -> p (a n)"),
                                  pack[:, u].rearrange("p a n -> p (a n)")).then_inc(stored[u], 16)
                pipeline(act, turn, none, finish)
                for u in range(B):
                    act.wait_ge(stored[u], 64 * (NT // B + 1))
                BETA, G, X, E, L, R = range(6)
                act.activation(gates[:, BETA], ba[:, :, 0:2 * NH], ACT.Sigmoid).then_inc(s["gate_step"], 1)
                act.activation(alog[:, 1], alog[:, 0], ACT.Exp).then_inc(s["gate_step"], 1)
                act.wait_ge(s["x_done"], 1)
                act.activation(gates[:, E], gates[:, X], ACT.Abs).then_inc(s["gate_step"], 1)
                act.wait_ge(s["gate_step"], 3)
                act.activation(gates[:, L], gates[:, E], ACT.Exp, scale=-1.0).then_inc(s["gate_step"], 1)
                act.wait_ge(s["gate_step"], 4)
                act.activation(gates[:, E], gates[:, L], ACT.Ln, bias=one[:]).then_inc(s["gate_step"], 1)
                act.wait_ge(s["x_done"], 5)
                act.dma_start(io["bg_s"], gates[:, 0:2].rearrange("p a t n -> p (a t n)")).then_inc(stored[0], 16)
                act.wait_ge(stored[0], 64 * (NT // B + 1) + 16)

            @block.vector
            def _(dve):
                dve.sem_inc(s["v_lo_done"], 1)
                dve.sem_inc(s["dn_scaled"], 1)
                dve.wait_ge(s["rope_in"], 16)

                def turn(u, t, n):
                    dve.wait_ge(s["qkv_copied"], t + 2)
                    dve.tensor_tensor(v_split[:, u, :, 1], ps[:, 1, P:2 * P].rearrange("p (n d) -> p n d", d=HD),
                                      f32(v_split[:, u, :, 0]), ALU.subtract).then_inc(s["v_lo_done"], 1)
                    dve.wait_ge(s["qk_squared"], t + 1)
                    dve.tensor_reduce(rstd[:, u, 0], qk_sq[:, u], AX.X, ALU.add).then_inc(s["qk_summed"], 1)
                    dve.wait_ge(s["dn_copied"], t + 2)
                    dve.tensor_reduce(dn_rs[:, u, 0], dn_sq[:, u], AX.X, ALU.add).then_inc(s["dn_summed"], 1)

                def scale(u, t, n):
                    dve.wait_ge(s["qk_rms"], t + 1)
                    dve.tensor_tensor(qk[:, u], qk[:, u], along(rstd[:, u, 1], 2, HD), ALU.mult).then_inc(s["qk_scaled"], 1)
                    dve.wait_ge(s["dn_rs_done"], t + 1)
                    dve.tensor_tensor(dn_q[:, u].rearrange("p (h d) -> p h d", h=NH), ps[:, 2].rearrange("p (h d) -> p h d", h=NH),
                                      along(dn_rs[:, u, 1, 0:NH], 2, DH), ALU.mult)
                    dve.tensor_tensor(pack[:, u, K_TOK].rearrange("p (h d) -> p h d", h=NH), ps[:, 3].rearrange("p (h d) -> p h d", h=NH),
                                      along(dn_rs[:, u, 1, NH:2 * NH], 2, DH), ALU.mult).then_inc(s["dn_scaled"], 1)

                def finish(u, t, n):
                    dve.wait_ge(s["qk_gained"], t + 1)
                    dve.tensor_tensor(rot_a[:, u], qk_g[:, u], along(rope[:, bass.ds(t, 1), 0].rearrange("p a d -> p (a d)"), 1, NQK),
                                      ALU.mult).then_inc(s["rot_step"], 1)
                    dve.wait_ge(s["rot_b_done"], t + 1)
                    dve.wait_ge(s["rot_step"], t * 3 + 1)
                    dve.tensor_tensor(rot_a[:, u], rot_a[:, u], rot_b[:, u], ALU.add).then_inc(s["rot_step"], 1)
                    dve.wait_ge(s["rot_step"], t * 3 + 2)
                    k_rot = along(rot_a[:, u, NQH:NQK], 2, 2)
                    dve.tensor_copy(q_split[:, u, :, 0], rot_a[:, u, 0:NQH])
                    dve.tensor_copy(k_split[:, u, :, 0], k_rot).then_inc(s["rot_step"], 1)
                    dve.wait_ge(s["rot_step"], t * 3 + 3)
                    dve.tensor_tensor(q_split[:, u, :, 1], rot_a[:, u, 0:NQH], f32(q_split[:, u, :, 0]), ALU.subtract)
                    dve.tensor_tensor(k_split[:, u, :, 1], k_rot, f32(k_split[:, u, :, 0]), ALU.subtract).then_inc(s["split_done"], 1)
                pipeline(dve, turn, scale, finish)

            @block.gpsimd
            def _(pool):
                pool.memset(mhalf[:], -0.5)
                pool.memset(one[:], 1.0)
                pool.wait_ge(s["const_in"], 80)
                pool.wait_ge(s["rope_in"], 16)
                for h in range(1, NQH):
                    pool.tensor_copy(gain[:, h], gain[:, 0])
                pool.tensor_copy(gain[:, NQH + 1], gain[:, NQH]).then_inc(s["const_done"], 1)
                pool.wait_ge(s["const_done"], 1)
                pool.tensor_scalar(gain[:, 0:NQH], gain[:, 0:NQH], HD ** -0.5, None, ALU.mult).then_inc(s["const_done"], 1)
                pool.wait_ge(s["const_done"], 2)

                def turn(u, t, n):
                    hold(pool, s["passed"], s["qk_summed"], t + 1)
                    pool.tensor_scalar(rstd[:, u, 1], rstd[:, u, 0], 1.0 / HD, EPS, ALU.mult, ALU.add).then_inc(s["pool_step"], 1)
                    pool.wait_ge(s["pool_step"], t * 3 + 1)
                    pool.tensor_tensor(rstd[:, u, 1], rstd[:, u, 1], mhalf[:], ALU.pow).then_inc(s["qk_rms"], 1)
                    hold(pool, s["passed"], s["dn_summed"], t + 1)
                    pool.tensor_scalar(dn_rs[:, u, 1], dn_rs[:, u, 0], EPS, None, ALU.add).then_inc(s["pool_step"], 1)
                    pool.wait_ge(s["pool_step"], t * 3 + 2)
                    pool.tensor_tensor(dn_rs[:, u, 1], dn_rs[:, u, 1], mhalf[:, 0:2 * NH], ALU.pow).then_inc(s["pool_step"], 1)
                    hold(pool, s["passed"], s["pool_step"], t * 3 + 3)
                    pool.tensor_scalar(dn_rs[:, u, 1, 0:NH], dn_rs[:, u, 1, 0:NH], DH ** -0.5, None, ALU.mult).then_inc(s["dn_rs_done"], 1)

                def scale(u, t, n):
                    pool.wait_ge(s["qk_scaled"], t + 1)
                    pool.tensor_tensor(qk_g[:, u], qk[:, u], gain[:], ALU.mult).then_inc(s["qk_gained"], 1)
                    pool.wait_ge(s["qk_gained"], t + 1)
                    x = qk_g[:, u].rearrange("p n (h r j) -> p n h r j", h=2, r=2)
                    y = rot_b[:, u].rearrange("p n (h r j) -> p n h r j", h=2, r=2)
                    sin = rope[:, bass.ds(t, 1), 1].rearrange("p a (h r j) -> p (a h) r j", h=2, r=2)
                    for r in range(2):
                        op = pool.tensor_tensor(y[:, :, :, r], x[:, :, :, 1 - r], along(sin[:, :, r], 1, NQK), ALU.mult)
                    op.then_inc(s["rot_b_done"], 1)
                pipeline(pool, turn, scale, none)
                BETA, G, X, E, L, R = range(6)
                pool.wait_ge(s["qkv_copied"], NT + 1)
                pool.tensor_tensor(gates[:, X], ba[:, :, 2 * NH:4 * NH], along(dtb[:], 1, NT), ALU.add).then_inc(s["x_done"], 1)
                pool.wait_ge(s["x_done"], 1)
                pool.tensor_scalar(gates[:, R], gates[:, X], 0.0, None, ALU.max).then_inc(s["x_done"], 1)
                pool.wait_ge(s["gate_step"], 5)
                pool.wait_ge(s["x_done"], 2)
                pool.tensor_tensor(gates[:, R], gates[:, R], gates[:, E], ALU.add).then_inc(s["x_done"], 1)
                pool.tensor_scalar(alog[:, 1], alog[:, 1], -1.0, None, ALU.mult).then_inc(s["x_done"], 1)
                pool.wait_ge(s["x_done"], 4)
                pool.tensor_tensor(gates[:, G], gates[:, R], along(alog[:, 1], 1, NT), ALU.mult).then_inc(s["x_done"], 1)
    end_phase(nc, c)


def attend(nc, io):
    GROUPS = [(0, 0, T0 // P), (4, 0, T0 // P), (T0 // P, T0 // P, T1 // P)]
    NGR = 2 * len(GROUPS)
    group = [(u, *g) for u in range(2) for g in GROUPS]
    TILES = 4 * NGR
    first_key = [sum(g[3] for g in group[:n]) for n in range(NGR + 1)]
    KEYS = first_key[NGR]
    with ExitStack() as ctx:
        c = Core(nc, ctx, "attend")
        q = c.sb("q_head", [P, 2, TOK], F32R)
        k = c.sb("k_head", [P, 2, 2, TOK], F32R)
        v = c.sb("v_head", [P, 2, NT, P], F32R)
        probs = c.sb("probs", [P, 2, 4, T0])
        turned_hi = c.sb("probs_hi", [P, 2, 512], F32R)
        turned_lo = c.sb("probs_lo", [P, 2, 512], F32R)
        neg_max = c.sb("neg_max", [P, 2, 4])
        row_sum = c.sb("row_sum", [P, 3, 4])
        inv_sum = c.sb("inv_sum", [P, 2, 4])
        o_feat = c.sb("o_feat", [P, 2, 512])
        o_tok = c.sb("o_tok", [P, 2, 4, P])
        attn = c.sb("attn_tok", [P, NT, NQH, HD])
        ident = c.sb("ident_c", [P, P])
        score_ps = c.ps("score_ps", [P, 2, 2, 512])
        turn_ps = c.ps("turn_ps", [P, 2, 512])
        out_ps = c.ps("out_ps", [P, 2, 512])

        head_in, head_used = c.sems2("head_in"), c.sems2("head_used")
        names = ("ident_in", "scored", "maxed", "expd", "turned", "hi_done", "lo_done", "pv_done", "o_copied", "o_turned",
                 "inverted", "o_scaled", "o_added", "stored")
        s = {n: c.sem(n) for n in names}

        def schedule(score, keys, copy_out, turn_out, scale_out, lead=0):
            def do(f, *a):
                if f:
                    f(*a)

            def score_at(x):
                if x < TILES:
                    do(score, x // 4, x % 4)
            for x in range(lead):
                score_at(x)
            for j in range(4):
                score_at(j + lead)
            for n in range(NGR):
                per = group[n][3] // 4
                for j in range(4):
                    score_at(4 * n + 4 + j + lead)
                    for kt in range(j * per, (j + 1) * per):
                        do(keys, n, kt)
                    if n and j < 3:
                        do((copy_out, turn_out, scale_out)[j], n - 1)
            for f in (copy_out, turn_out, scale_out):
                do(f, NGR - 1)

        with nc.Block("attend") as block:
            @block.sync
            def _(sp):
                sp.dma_start(ident[:], io["ident"]).then_inc(s["ident_in"], 16)
                with sp.Fori(0, NKVH) as kv:
                    with sp.Fori(0, 2) as pair:
                        for u in range(2):
                            sp.wait_ge(head_used[u], kv * 2 + pair + 1)
                            sp.dma_start(f32(q[:, u]), io["q_s"][bass.ds(kv * 4 + pair * 2 + u, 1)].rearrange("a p t -> p (a t)")).then_inc(head_in[u], 16)
                            sp.dma_start(f32(k[:, u]), io["k_s"][bass.ds(kv * 2, 2)].rearrange("a p t -> p a t")).then_inc(head_in[u], 16)
                            sp.dma_start(f32(v[:, u]), io["v_s"][bass.ds(kv, 1)].rearrange("a p t d -> p (a t) d")).then_inc(head_in[u], 16)
                sp.wait_ge(s["o_added"], 4 * NGR + 2)
                sp.dma_start(io["at_s"], attn[:].rearrange("p t h d -> p (t h d)")).then_inc(s["stored"], 16)
                sp.wait_ge(s["stored"], 16)

            @block.tensor
            def _(pe):
                for u in range(2):
                    pe.sem_inc(head_used[u], 1)
                pe.sem_inc(s["pv_done"], 2)
                pe.wait_ge(s["ident_in"], 16)
                with pe.Fori(0, NQH // 2) as it:
                    def score(n, j):
                        u, q0, k0, nk = group[n]
                        if n % 3 == 0 and j == 0:
                            pe.wait_ge(head_in[u], it * 48 + 48)
                        pe.wait_ge(s["expd"], it * TILES + (4 * n + j + 1))
                        for b in range(nk // 4):
                            for half in range(2):
                                mm = pe.matmul(score_ps[:, j % 2, b], q[:, u, (q0 + j) * P:(q0 + j + 1) * P],
                                               k[:, u, half, (k0 + 4 * b) * P:(k0 + 4 * b + 4) * P], start=half == 0, stop=half == 1)
                        mm.then_inc(s["scored"], 1)

                    def product(n, kt):
                        u, q0, k0, nk = group[n]
                        m = first_key[n] + kt
                        pe.wait_ge(s["lo_done"], it * KEYS + (m + 3))
                        if kt == 0:
                            pe.wait_ge(s["o_scaled"], it * NGR + (n + 1))
                        for half, x in enumerate((turned_hi, turned_lo)):
                            mm = pe.matmul(out_ps[:, n % 2], v[:, u, k0 + kt], x[:, m % 2], start=kt == 0 and half == 0,
                                           stop=kt == nk - 1 and half == 1)
                        mm.then_inc(s["pv_done"], 1)
                        if n % 3 == 2 and kt == nk - 1:
                            pe.wait_ge(s["pv_done"], it * KEYS + (m + 3))
                            pe.sem_inc(head_used[u], 1)

                    def keys(n, kt):
                        u, q0, k0, nk = group[n]
                        m = first_key[n] + kt
                        if kt == 0:
                            pe.wait_ge(s["expd"], it * TILES + (4 * n + 6))
                        pe.wait_ge(s["lo_done"], it * KEYS + (m + 1))
                        for j in range(4):
                            tr = pe.transpose(turn_ps[:, m % 2, j * P:(j + 1) * P], probs[:, n % 2, j, kt * P:(kt + 1) * P], ident[:])
                        tr.then_inc(s["turned"], 1)
                        if kt:
                            product(n, kt - 1)
                        if kt == nk - 1:
                            product(n, kt)

                    def turn_out(n):
                        pe.wait_ge(s["o_copied"], it * NGR + (n + 1))
                        for j in range(4):
                            tr = pe.transpose(out_ps[:, n % 2, j * P:(j + 1) * P], o_feat[:, n % 2, j * P:(j + 1) * P], ident[:])
                        tr.then_inc(s["o_turned"], 1)
                    schedule(score, keys, None, turn_out, None, lead=1)

            @block.scalar
            def _(act):
                act.sem_inc(s["expd"], 2)
                with act.Fori(0, NQH // 2) as it:
                    def score(n, j):
                        u, q0, k0, nk = group[n]
                        act.wait_ge(s["maxed"], it * TILES + (4 * n + j + 1))
                        act.activation(probs[:, n % 2, j, 0:nk * P], score_ps[:, j % 2, 0:nk // 4].rearrange("p b t -> p (b t)"), ACT.Exp,
                                       bias=neg_max[:, n % 2, j:j + 1], accum_out=row_sum[:, n % 3, j:j + 1]).then_inc(s["expd"], 1)

                    def keys(n, kt):
                        m = first_key[n] + kt
                        act.wait_ge(s["turned"], it * KEYS + (m + 1))
                        act.wait_ge(s["pv_done"], it * KEYS + (m + 1))
                        act.activation(turned_hi[:, m % 2], turn_ps[:, m % 2], ACT.Copy).then_inc(s["hi_done"], 1)

                    def copy_out(n):
                        act.wait_ge(s["pv_done"], it * KEYS + (first_key[n + 1] + 2))
                        act.activation(o_feat[:, n % 2], out_ps[:, n % 2], ACT.Copy).then_inc(s["o_copied"], 1)
                    schedule(score, keys, copy_out, None, None)

            @block.vector
            def _(dve):
                dve.sem_inc(s["lo_done"], 2)
                dve.sem_inc(s["o_scaled"], 2)
                with dve.Fori(0, NQH // 2) as it:
                    def score(n, j):
                        u, q0, k0, nk = group[n]
                        dve.wait_ge(s["scored"], it * TILES + (4 * n + j + 1))
                        dve.tensor_reduce(neg_max[:, n % 2, j:j + 1], score_ps[:, j % 2, 0:nk // 4].rearrange("p b t -> p (b t)"),
                                          AX.X, ALU.max, negate=True).then_inc(s["maxed"], 1)

                    def keys(n, kt):
                        m = first_key[n] + kt
                        dve.wait_ge(s["hi_done"], it * KEYS + (m + 1))
                        dve.tensor_tensor(turned_lo[:, m % 2], turn_ps[:, m % 2], f32(turned_hi[:, m % 2]), ALU.subtract).then_inc(s["lo_done"], 1)

                    def scale_out(n):
                        dve.wait_ge(s["expd"], it * TILES + (4 * n + 6))
                        dve.reciprocal(inv_sum[:, n % 2], row_sum[:, n % 3]).then_inc(s["inverted"], 1)
                        dve.wait_ge(s["inverted"], it * NGR + (n + 1))
                        dve.wait_ge(s["o_turned"], it * NGR + (n + 1))
                        dve.wait_ge(s["o_added"], it * NGR + (n + 1))
                        dve.tensor_tensor(o_tok[:, n % 2], out_ps[:, n % 2].rearrange("p (j d) -> p j d", j=4),
                                          along(inv_sum[:, n % 2], 2, P), ALU.mult).then_inc(s["o_scaled"], 1)
                    schedule(score, keys, None, None, scale_out, lead=1)

            @block.gpsimd
            def _(pool):
                pool.sem_inc(s["o_added"], 2)
                with pool.Fori(0, NQH // 2) as it:
                    for n in range(NGR):
                        u, q0, k0, nk = group[n]
                        pool.wait_ge(s["o_scaled"], it * NGR + (n + 3))
                        pool.tensor_tensor(attn[:, q0:q0 + 4, bass.ds(it * 2 + u, 1), :].rearrange("p t a d -> p t (a d)"),
                                           o_tok[:, n % 2, :, 0:HD], o_tok[:, n % 2, :, HD:P], ALU.add).then_inc(s["o_added"], 1)
    end_phase(nc, c)


LEVELS = [2 ** n for n in range(1, 7)]
FWD, BWD = range(2)


def deltanet(nc, io):
    NM = 3 + len(LEVELS)
    INCL, STRICT, NEG_M1 = range(3)
    EGC, TAIL, TOTAL = range(3)
    K_TOK, V_TOK, K_T, Q_T = range(4)
    NL = len(LEVELS)
    with ExitStack() as ctx:
        c = Core(nc, ctx, "deltanet")
        masks = c.sb("masks", [P, 2, NM, P])
        ident = c.sb("ident_d", [P, P])
        ones = c.sb("ones_d", [P, P])
        bg = c.sb("bg", [P, 2, NT, 2 * NH])
        pack = c.sb("pack_in", [P, 2, 2, 4, DNW])
        out = c.sb("dn_out", [P, 2, 2, DNW])

        def work(name):
            return c.sb(name, [P, 2, NH, P])
        g_cut, decay, decay_m, decay_b, low_t, qk_d = (work(n) for n in ("g_cut", "decay", "decay_m", "decay_b", "low_t", "qk_d"))
        t_inv, r, x_m, k_dec, z, v_new, state, q_state = (work(n) for n in ("t_inv", "r_inv", "x_m", "k_dec", "z_in", "v_new", "state", "q_state"))
        small = c.sb("beta_g", [P, 2, 2, NH])
        exps = c.sb("g_exps", [P, 2, 3, NH])
        neg_egc = c.sb("neg_egc", [P, 2, NH])
        ps = c.ps("dn_ps", [P, 2, 4, 512])
        BA, BB, BC, BD = range(4)

        names = ("small_done", "cut_done", "gates_mm", "exp_done", "decay_m_done", "decay_b_done", "neg_done", "kk_mm", "qk_mm",
                 "low_done", "qk_done", "r_masked", "r_init", "turned", "t_init", "t_upd", "r_upd", "r_final", "x_mm", "x_done", "tx_mm",
                 "k_dec_done", "ks_mm", "qs_mm", "z_done", "q_state_done", "y_mm", "v_new_done", "o_mm", "ktv_mm", "state_scaled",
                 "state_ready", "out_done")
        s = {n: c.sems2(n) for n in names}
        pack_in, out_stored = ([c.sems2(f"{n}{d}_") for d in range(2)] for n in ("pack_in", "out_stored"))
        const_in, ones_done, passed = c.sem("const_in"), c.sem("ones_done"), c.sem("passed")

        def steps(eng, stages, before=None):
            for q, (base, n) in enumerate(SEQS):
                if before:
                    before(q, base)
                with eng.Fori(0, n // 2) as i:
                    for p in range(2):
                        for stage in stages:
                            for d in range(2):
                                tile = i * 2 + (base + p) if d == FWD else i * -2 + (base + n - 1 - p)
                                stage(d, p, i * 2 + (base + p), tile, q)

        with nc.Block("deltanet") as block:
            @block.sync
            def _(sp):
                sp.dma_start(masks[:].rearrange("p a m j -> p (a m j)"), io["masks"]).then_inc(const_in, 16)
                sp.dma_start(ident[:], io["ident"]).then_inc(const_in, 16)
                sp.dma_start(bg[:].rearrange("p a t n -> p (a t n)"), io["bg_s"]).then_inc(const_in, 16)
                for q, (base, n) in enumerate(SEQS):
                    def load(u, t):
                        for d in range(2):
                            sp.wait_ge(s["ktv_mm"][d], t + (base + 1))
                            tile = t + base if d == FWD else t * -1 + (base + n - 1)
                            sp.dma_start(pack[:, d, u].rearrange("p a n -> p (a n)"),
                                         io["dn_s"][bass.ds(tile, 1)].rearrange("a p n -> p (a n)")[:, 0:4 * DNW]).then_inc(pack_in[d][u], 16)

                    def store(u, t):
                        for d in range(2):
                            tile = t + base if d == FWD else t * -1 + (base + n - 1)
                            sp.wait_ge(s["out_done"][d], t + (base + 1))
                            sp.dma_start(io["do_s"][d][bass.ds(tile, 1)].rearrange("a p n -> p (a n)"), out[:, d, u]).then_inc(out_stored[d][u], 16)
                    ahead(sp, n, load, store)
                for d in range(2):
                    for u in range(2):
                        sp.wait_ge(out_stored[d][u], 16 * (NT // 2 + 1))

            @block.tensor
            def _(pe):
                pe.wait_ge(const_in, 48)
                pe.wait_ge(ones_done, 1)
                for d in range(2):
                    pe.sem_inc(s["ktv_mm"][d], 2)

                def heads(dst, lhs, rhs):
                    for h in range(NH):
                        mm = pe.matmul(dst[:, h * P:(h + 1) * P], lhs(h), rhs(h), start=True, stop=True)
                    return mm

                def block_of(a, d, p, which):
                    return lambda h: a[:, d, p, which, h * P:(h + 1) * P]

                def gates(d, p, g, tile, q):
                    pe.wait_ge(s["cut_done"][d], g + 1)
                    pe.wait_ge(s["q_state_done"][d], g + 1)
                    heads(ps[:, d, BA], lambda h: g_cut[:, d, h], lambda h: masks[:, d, INCL])
                    for n, lhs in enumerate((masks[:, d, INCL], masks[:, d, STRICT], ones[:])):
                        mm = pe.matmul(ps[:, d, BD, n * NH:(n + 1) * NH], lhs, small[:, d, 1], start=True, stop=True)
                    mm.then_inc(s["gates_mm"][d], 1)

                def key_products(d, p, g, tile, q):
                    pe.wait_ge(pack_in[d][p], uses(p, g, 16))
                    pe.wait_ge(s["state_ready"][d], g + (q + 1))
                    heads(ps[:, d, BB], block_of(pack, d, p, K_T), block_of(pack, d, p, K_T)).then_inc(s["kk_mm"][d], 1)
                    heads(ps[:, d, BC], block_of(pack, d, p, K_T), block_of(pack, d, p, Q_T)).then_inc(s["qk_mm"][d], 1)

                def turn(src, event):
                    def stage(d, p, g, tile, q):
                        event(d, g)
                        for h in range(NH):
                            tr = pe.transpose(ps[:, d, BA, h * P:(h + 1) * P], src[:, d, h], ident[:])
                        tr.then_inc(s["turned"][d], 1)
                    return stage

                def grow_x(n):
                    def stage(d, p, g, tile, q):
                        if n == 0:
                            pe.wait_ge(s["t_init"][d], g + 1)
                        else:
                            pe.wait_ge(s["t_upd"][d], g * (NL - 1) + n)
                        heads(ps[:, d, BB], lambda h: low_t[:, d, h], lambda h: t_inv[:, d, h]).then_inc(s["x_mm"][d], 1)
                    return stage

                def grow_t(n):
                    def stage(d, p, g, tile, q):
                        pe.wait_ge(s["x_done"][d], g * NL + (n + 1))
                        if n == 0:
                            pe.wait_ge(s["qk_done"][d], g + 1)
                        else:
                            pe.wait_ge(s["r_upd"][d], g * (NL - 1) + n)
                        if n < NL - 1:
                            heads(ps[:, d, BC], lambda h: r[:, d, h], lambda h: x_m[:, d, h]).then_inc(s["tx_mm"][d], 1)
                        else:
                            heads(ps[:, d, BC], lambda h: x_m[:, d, h], lambda h: r[:, d, h]).then_inc(s["tx_mm"][d], 1)
                    return stage

                def state_products(d, p, g, tile, q):
                    pe.wait_ge(s["state_ready"][d], g + (q + 1))
                    heads(ps[:, d, BB], block_of(pack, d, p, K_T), lambda h: state[:, d, h]).then_inc(s["ks_mm"][d], 1)
                    heads(ps[:, d, BD], block_of(pack, d, p, Q_T), lambda h: state[:, d, h]).then_inc(s["qs_mm"][d], 1)

                def solve(d, p, g, tile, q):
                    pe.wait_ge(s["r_final"][d], g + 1)
                    pe.wait_ge(s["z_done"][d], g + 1)
                    heads(ps[:, d, BC], lambda h: r[:, d, h], lambda h: z[:, d, h]).then_inc(s["y_mm"][d], 1)

                def new_products(d, p, g, tile, q):
                    pe.wait_ge(s["v_new_done"][d], g + 1)
                    pe.wait_ge(s["k_dec_done"][d], g + 1)
                    heads(ps[:, d, BB], lambda h: k_dec[:, d, h], lambda h: v_new[:, d, h]).then_inc(s["ktv_mm"][d], 1)
                    heads(ps[:, d, BA], lambda h: qk_d[:, d, h], lambda h: v_new[:, d, h]).then_inc(s["o_mm"][d], 1)

                stages = [gates, key_products, turn(r, lambda d, g: pe.wait_ge(s["r_init"][d], g + 1))]
                for n in range(NL):
                    stages += [grow_x(n), grow_t(n)]
                    if n < NL - 1:
                        stages.append(turn(t_inv, lambda d, g, n=n: pe.wait_ge(s["t_upd"][d], g * (NL - 1) + (n + 1))))
                stages += [state_products, solve, new_products]
                steps(pe, stages)

            @block.scalar
            def _(act):
                for d in range(2):
                    act.sem_inc(s["q_state_done"][d], 1)

                def exponentials(d, p, g, tile, q):
                    act.wait_ge(s["gates_mm"][d], g + 1)
                    act.activation(decay[:, d].rearrange("p h t -> p (h t)"), ps[:, d, BA], ACT.Exp)
                    act.activation(exps[:, d].rearrange("p a h -> p (a h)"), ps[:, d, BD, 0:3 * NH], ACT.Exp).then_inc(s["exp_done"][d], 1)

                def copy_turned(n):
                    def stage(d, p, g, tile, q):
                        act.wait_ge(s["turned"][d], g * NL + (n + 1))
                        dst, done = (t_inv, "t_init") if n == 0 else (r, "r_upd")
                        act.activation(dst[:, d].rearrange("p h t -> p (h t)"), ps[:, d, BA], ACT.Copy).then_inc(s[done][d], 1)
                    return stage

                def scale_q_state(d, p, g, tile, q):
                    act.wait_ge(s["qs_mm"][d], g + 1)
                    for h in range(NH):
                        op = act.activation(q_state[:, d, h], ps[:, d, BD, h * P:(h + 1) * P], ACT.Copy, scale=exps[:, d, EGC, h:h + 1])
                    op.then_inc(s["q_state_done"][d], 1)
                steps(act, [exponentials] + [copy_turned(n) for n in range(NL)] + [scale_q_state])

            @block.vector
            def _(dve):
                dve.wait_ge(const_in, 48)

                def take_gates(d, p, g, tile, q):
                    dve.tensor_copy(small[:, d], bg[:, :, bass.ds(tile, 1), d * NH:(d + 1) * NH].rearrange("p a t n -> p a (t n)")).then_inc(s["small_done"][d], 1)

                def decayed_products(d, p, g, tile, q):
                    dve.wait_ge(s["kk_mm"][d], g + 1)
                    dve.wait_ge(s["decay_b_done"][d], g + 1)
                    dve.tensor_tensor(low_t[:, d], ps[:, d, BB].rearrange("p (h t) -> p h t", h=NH), decay_b[:, d], ALU.mult).then_inc(s["low_done"][d], 1)
                    dve.wait_ge(s["qk_mm"][d], g + 1)
                    dve.tensor_tensor(qk_d[:, d], ps[:, d, BC].rearrange("p (h t) -> p h t", h=NH), decay_m[:, d], ALU.mult).then_inc(s["qk_done"][d], 1)

                def mask_x(n):
                    def stage(d, p, g, tile, q):
                        dve.wait_ge(s["x_mm"][d], g * NL + (n + 1))
                        dve.tensor_tensor(x_m[:, d], ps[:, d, BB].rearrange("p (h t) -> p h t", h=NH), along(masks[:, d, 3 + n], 1, NH),
                                          ALU.mult).then_inc(s["x_done"][d], 1)
                    return stage

                def subtract(n):
                    def stage(d, p, g, tile, q):
                        dve.wait_ge(s["tx_mm"][d], g * NL + (n + 1))
                        dst, done = (t_inv, "t_upd") if n < NL - 1 else (r, "r_final")
                        dve.tensor_tensor(dst[:, d], dst[:, d], ps[:, d, BC].rearrange("p (h t) -> p h t", h=NH), ALU.subtract).then_inc(s[done][d], 1)
                    return stage

                def make_z(d, p, g, tile, q):
                    dve.wait_ge(s["neg_done"][d], g + 1)
                    dve.wait_ge(s["ks_mm"][d], g + 1)
                    for h in range(NH):
                        op = dve.scalar_tensor_tensor(z[:, d, h], ps[:, d, BB, h * P:(h + 1) * P], neg_egc[:, d, h:h + 1],
                                                      pack[:, d, p, V_TOK, h * P:(h + 1) * P], ALU.mult, ALU.add)
                    op.then_inc(s["z_done"][d], 1)

                def make_v_new(d, p, g, tile, q):
                    dve.wait_ge(s["y_mm"][d], g + 1)
                    dve.tensor_tensor(v_new[:, d], ps[:, d, BC].rearrange("p (h t) -> p h t", h=NH), along(small[:, d, 0], 2, P),
                                      ALU.mult).then_inc(s["v_new_done"][d], 1)

                def update_state(d, p, g, tile, q):
                    dve.wait_ge(s["ktv_mm"][d], g + 3)
                    dve.wait_ge(s["state_scaled"][d], g + 1)
                    dve.tensor_tensor(state[:, d], state[:, d], ps[:, d, BB].rearrange("p (h t) -> p h t", h=NH), ALU.add).then_inc(s["state_ready"][d], 1)

                def outputs(d, p, g, tile, q):
                    dve.wait_ge(s["o_mm"][d], g + 1)
                    dve.wait_ge(s["q_state_done"][d], g + 2)
                    dve.wait_ge(out_stored[d][p], uses(p, g, 16))
                    dve.tensor_tensor(out[:, d, p], q_state[:, d].rearrange("p h t -> p (h t)"), ps[:, d, BA], ALU.add).then_inc(s["out_done"][d], 1)
                stages = [take_gates, decayed_products]
                for n in range(NL):
                    stages += [mask_x(n), subtract(n)]
                steps(dve, stages + [make_z, make_v_new, update_state, outputs])

            @block.gpsimd
            def _(pool):
                pool.memset(ones[:], 1.0).then_inc(ones_done, 1)
                for d in range(2):
                    for u in range(2):
                        pool.sem_inc(out_stored[d][u], 16)
                pool.wait_ge(const_in, 48)

                def clear_state(q, base):
                    for d in range(2):
                        if q:
                            pool.wait_ge(s["state_ready"][d], base + q)
                        pool.memset(state[:, d], 0.0).then_inc(s["state_ready"][d], 1)

                def cut_gates(d, p, g, tile, q):
                    pool.wait_ge(s["small_done"][d], g + 1)
                    pool.tensor_tensor(g_cut[:, d], along(masks[:, d, STRICT], 1, NH), along(small[:, d, 1], 2, P), ALU.mult).then_inc(s["cut_done"][d], 1)

                def mask_decay(d, p, g, tile, q):
                    pool.wait_ge(s["exp_done"][d], g + 1)
                    pool.tensor_tensor(decay_m[:, d], decay[:, d], along(masks[:, d, INCL], 1, NH), ALU.mult).then_inc(s["decay_m_done"][d], 1)
                    pool.wait_ge(s["decay_m_done"][d], g + 1)
                    pool.tensor_tensor(decay_b[:, d], decay_m[:, d], along(small[:, d, 0], 2, P), ALU.mult).then_inc(s["decay_b_done"][d], 1)

                def first_r(d, p, g, tile, q):
                    pool.wait_ge(s["low_done"][d], g + 1)
                    pool.tensor_tensor(r[:, d], low_t[:, d], along(masks[:, d, NEG_M1], 1, NH), ALU.mult).then_inc(s["r_masked"][d], 1)
                    pool.wait_ge(s["r_masked"][d], g + 1)
                    pool.tensor_tensor(r[:, d], r[:, d], along(ident[:], 1, NH), ALU.add).then_inc(s["r_init"][d], 1)

                def decay_keys(d, p, g, tile, q):
                    pool.wait_ge(pack_in[d][p], uses(p, g, 16))
                    pool.tensor_tensor(k_dec[:, d], pack[:, d, p, K_TOK].rearrange("p (h t) -> p h t", h=NH), along(exps[:, d, TAIL], 2, P),
                                       ALU.mult).then_inc(s["k_dec_done"][d], 1)
                    pool.tensor_scalar(neg_egc[:, d], exps[:, d, EGC], -1.0, None, ALU.mult).then_inc(s["neg_done"][d], 1)

                def scale_state(d, p, g, tile, q):
                    pool.wait_ge(s["qs_mm"][d], g + 1)
                    pool.tensor_tensor(state[:, d], state[:, d], along(exps[:, d, TOTAL], 2, P), ALU.mult).then_inc(s["state_scaled"][d], 1)
                steps(pool, [cut_gates, mask_decay, first_r, decay_keys, scale_state], clear_state)
    end_phase(nc, c)


def merge(nc, io):
    KB = NQH * HD // P
    with ExitStack() as ctx:
        c = Core(nc, ctx, "merge")
        x_hi = c.sb("branch_hi", [P, 2, KB, TOK], F32R)
        x_lo = c.sb("branch_lo", [P, 2, KB, TOK], F32R)
        dirs = c.sb("dn_dirs", [P, 2, 2, DNW])
        zt = c.sb("z_tok", [P, 2, DNW])
        at = c.sb("attn_in", [P, 2, DNW])
        osum = c.sb("dn_sum", [P, 2, NH, DH])
        osq = c.sb("dn_square", [P, 2, NH, DH])
        stat = c.sb("dn_stat", [P, 2, 3, NH])
        gain = c.sb("dn_gain", [P, DH])
        mhalf = c.sb("mhalf_e", [P, NH])
        ident = c.sb("ident_e", [P, P])
        raw = c.sb("wb_raw", [P, 2, 2, KB, P])
        whi = c.sb("wb_hi", [P, 2, 2, KB, P], F32R)
        wlo = c.sb("wb_lo", [P, 2, 2, KB, P], F32R)
        sig = c.sb("gate_sig", [P, 2, TOK])
        part = c.sb("branch_out", [P, 2, 2, TOK])
        turn_ps = c.ps("branch_turn", [P, 2, 512])
        acc = c.ps("branch_ps", [P, 2, NG, 512])

        tile_in, dirs_in = c.sems2("tile_in"), c.sems2("dirs_in")
        names = ("const_in", "mhalf_done", "passed", "summed", "squared", "reduced", "ms_done", "rstd_done", "normed", "gained",
                 "gated", "turned", "hi_done", "lo_done")
        s = {n: c.sem(n) for n in names}
        w_in, w_hi, w_ready, stored, added, sig_in, acc_done, acc_used = (c.sems2(n) for n in (
            "w_in", "w_hi", "w_ready", "stored", "added", "sig_in", "acc_done", "acc_used"))

        with nc.Block("merge") as block:
            @block.sync
            def _(sp):
                sp.dma_start(gain[:], io["dn_out_norm_g"][0].partition_broadcast(P)).then_inc(s["const_in"], 16)
                sp.dma_start(ident[:], io["ident"]).then_inc(s["const_in"], 16)

                def load_weights(u, i):
                    sp.wait_ge(w_ready[u], i + 1)
                    for b, w in enumerate(("w_attn_branch", "w_dn_branch")):
                        sp.dma_start(raw[:, u, b], io[w].rearrange("(k p) n -> p k n", p=P)[:, :, bass.ds(i * 256 + u * P, P)]).then_inc(w_in[u], 16)

                def load_gates(u, i):
                    for b in range(2):
                        sp.wait_ge(acc_used[b], i * 2 + (u + 1))
                        sp.dma_start(sig[:, b], io["gate_s"][bass.ds(i * 256 + (u * P + b * D), P), :]).then_inc(sig_in[b], 16)

                with sp.Fori(0, NT // 2) as i:
                    for u in range(2):
                        row = bass.ds(i * 2 + u, 1)
                        sp.wait_ge(s["summed"], i * 2 + (u + 1))
                        for d in range(2):
                            sp.dma_start(dirs[:, u, d], io["do_s"][d][row].rearrange("a p n -> p (a n)")).then_inc(dirs_in[u], 16)
                        sp.wait_ge(s["turned"], i * 2 + (u + 1))
                        sp.dma_start(zt[:, u], io["dn_s"][row].rearrange("a p n -> p (a n)")[:, 4 * DNW:5 * DNW]).then_inc(tile_in[u], 16)
                        sp.dma_start(at[:, u], io["at_s"][:, bass.ds(i * (2 * DNW) + u * DNW, DNW)]).then_inc(tile_in[u], 16)
                for u in range(2):
                    load_weights(u, 0)
                with sp.Fori(0, KD // 2 - 1) as i:
                    for u in range(2):
                        load_gates(u, i)
                        load_weights(u, i + 1)
                for u in range(2):
                    load_gates(u, KD // 2 - 1)

            @block.gpsimd
            def _(pool):
                for u in range(2):
                    pool.sem_inc(w_ready[u], 1)
                pool.memset(mhalf[:], -0.5).then_inc(s["mhalf_done"], 1)
                pool.wait_ge(s["mhalf_done"], 1)
                pool.wait_ge(s["const_in"], 32)

                def root(u, t):
                    hold(pool, s["passed"], s["reduced"], t + 1)
                    pool.tensor_scalar(stat[:, u, 1], stat[:, u, 0], 1.0 / DH, EPS, ALU.mult, ALU.add).then_inc(s["ms_done"], 1)
                    pool.wait_ge(s["ms_done"], t + 1)
                    pool.tensor_tensor(stat[:, u, 2], stat[:, u, 1], mhalf[:], ALU.pow).then_inc(s["rstd_done"], 1)
                    pool.wait_ge(tile_in[u], uses(u, t, 32))
                    zh = zt[:, u].rearrange("p (h d) -> p h d", h=NH)
                    pool.tensor_tensor(zh, zh, along(gain[:], 1, NH), ALU.mult).then_inc(s["gained"], 1)
                ahead(pool, NT, root, lambda u, t: None)

                def split(u, i):
                    pool.wait_ge(w_in[u], i * 32 + 32)
                    hold(pool, s["passed"], acc_done[u], i * 2 + 2)
                    pool.tensor_copy(whi[:, u], raw[:, u]).then_inc(w_hi[u], 1)
                    pool.wait_ge(w_hi[u], i + 1)
                    pool.tensor_tensor(wlo[:, u], raw[:, u], f32(whi[:, u]), ALU.subtract).then_inc(w_ready[u], 1)
                with pool.Fori(0, KD // 2) as i:
                    for u in range(2):
                        split(u, i)

            @block.tensor
            def _(pe):
                for u in range(2):
                    pe.sem_inc(acc_done[u], 2)
                pe.sem_inc(s["turned"], 2)
                pe.wait_ge(s["const_in"], 32)
                with pe.Fori(0, NT // 2) as i:
                    for u in range(2):
                        t = i * 2 + u
                        pe.wait_ge(s["lo_done"], t + 2)
                        pe.wait_ge(tile_in[u], i * 32 + 32)
                        for k in range(KB):
                            pe.transpose(turn_ps[:, 0, k * P:(k + 1) * P], at[:, u, k * P:(k + 1) * P], ident[:])
                        pe.wait_ge(s["gated"], t + 1)
                        for k in range(KB):
                            tr = pe.transpose(turn_ps[:, 1, k * P:(k + 1) * P], osum[:, u, k], ident[:])
                        tr.then_inc(s["turned"], 1)
                pe.wait_ge(s["lo_done"], NT + 2)
                with pe.Fori(0, KD // 2) as i:
                    for u in range(2):
                        pe.wait_ge(w_ready[u], i + 2)
                        for b in range(2):
                            pe.wait_ge(acc_used[b], i * 2 + (u + 1))
                            split_matmuls(pe, [acc[:, b, g] for g in range(NG)],
                                          lambda k, g: (whi[:, u, b, k], wlo[:, u, b, k], x_hi[:, b, k, g * 512:(g + 1) * 512],
                                                        x_lo[:, b, k, g * 512:(g + 1) * 512]), KB).then_inc(acc_done[u], 1)

            @block.scalar
            def _(act):
                for u in range(2):
                    act.sem_inc(stored[u], 16)

                def square(u, t):
                    act.wait_ge(s["summed"], t + 3)
                    act.activation(osq[:, u], osum[:, u], ACT.Square).then_inc(s["squared"], 1)

                def copy_hi(u, t):
                    act.wait_ge(s["turned"], t + 3)
                    act.activation(x_hi[:, :, :, bass.ds(t * P, P)].rearrange("p b k t -> p (b k) t"),
                                   turn_ps[:].rearrange("p b (k t) -> p (b k) t", k=KB), ACT.Copy).then_inc(s["hi_done"], 1)
                ahead(act, NT, square, copy_hi)
                with act.Fori(0, KD // 2) as i:
                    for u in range(2):
                        act.wait_ge(added[u], i + 1)
                        act.dma_start(io["m_s"][:, :, bass.ds(i * 2 + u, 1), :].rearrange("t p a j -> p t (a j)"),
                                      part[:, u, 0].rearrange("p (t j) -> p t j", j=P)).then_inc(stored[u], 16)
                for u in range(2):
                    act.wait_ge(stored[u], 16 * (KD // 2 + 1))

            @block.vector
            def _(dve):
                dve.sem_inc(s["lo_done"], 2)
                dve.sem_inc(s["summed"], 2)
                for b in range(2):
                    dve.sem_inc(acc_used[b], 1)

                def sum_directions(u, t):
                    dve.wait_ge(dirs_in[u], uses(u, t, 32))
                    dve.wait_ge(s["turned"], t + 1)
                    dve.tensor_tensor(osum[:, u].rearrange("p h d -> p (h d)"), dirs[:, u, 0], dirs[:, u, 1], ALU.add).then_inc(s["summed"], 1)
                    dve.wait_ge(s["squared"], t + 1)
                    dve.tensor_reduce(stat[:, u, 0], osq[:, u], AX.X, ALU.add).then_inc(s["reduced"], 1)

                def norm_and_gate(u, t):
                    dve.wait_ge(s["rstd_done"], t + 1)
                    dve.tensor_tensor(osum[:, u], osum[:, u], along(stat[:, u, 2], 2, DH), ALU.mult).then_inc(s["normed"], 1)
                    dve.wait_ge(s["gained"], t + 1)
                    dve.wait_ge(s["normed"], t + 1)
                    dve.tensor_tensor(osum[:, u].rearrange("p h d -> p (h d)"), osum[:, u].rearrange("p h d -> p (h d)"), zt[:, u],
                                      ALU.mult).then_inc(s["gated"], 1)

                def subtract_hi(u, t):
                    dve.wait_ge(s["hi_done"], t + 1)
                    tok = bass.ds(t * P, P)
                    dve.tensor_tensor(x_lo[:, :, :, tok].rearrange("p b k t -> p (b k) t"), turn_ps[:].rearrange("p b (k t) -> p (b k) t", k=KB),
                                      f32(x_hi[:, :, :, tok]).rearrange("p b k t -> p (b k) t"), ALU.subtract).then_inc(s["lo_done"], 1)
                ahead(dve, NT, sum_directions, subtract_hi, norm_and_gate)
                with dve.Fori(0, KD // 2) as i:
                    for u in range(2):
                        for b in range(2):
                            dve.wait_ge(acc_done[u], i * 2 + (b + 3))
                            dve.wait_ge(sig_in[b], i * 32 + (u * 16 + 16))
                            if b == 0:
                                dve.wait_ge(stored[u], i * 16 + 16)
                            dve.tensor_tensor(part[:, u, b], acc[:, b].rearrange("p g t -> p (g t)"), sig[:, b], ALU.mult).then_inc(acc_used[b], 1)
                        for b in range(2):
                            dve.wait_ge(acc_used[b], i * 2 + (u + 2))
                        dve.tensor_tensor(part[:, u, 0], part[:, u, 0], part[:, u, 1], ALU.add).then_inc(added[u], 1)
    end_phase(nc, c)


def mix_out(nc, io):
    with ExitStack() as ctx:
        c = Core(nc, ctx, "mix")
        whi = c.sb("wo_hi", [P, KD, D], F32R)
        wlo = c.sb("wo_lo", [P, KD, D], F32R)
        raw = c.sb("wo_raw", [P, 2, D])
        mt = c.sb("merged_in", [P, 2, KD, P])
        mhi = c.sb("merged_hi", [P, 2, KD, P], F32R)
        mlo = c.sb("merged_lo", [P, 2, KD, P], F32R)
        xt = c.sb("x_res", [P, 2, D])
        h = c.sb("h_tok", [P, 2, D])
        hn = c.sb("h_normed", [P, 2, D])
        junk = c.sb("squares_f", [P, 2, D])
        ht = c.sb("h_turned", [P, 2, KD, P])
        gains = c.sb("gains_f", [P, 2, D])
        stat = c.sb("stat_f", [P, 2, 2, 3])
        mhalf = c.sb("mhalf_f", [P, 1])
        ident = c.sb("ident_f", [P, P])
        acc = c.ps("mix_ps", [P, 2, 2, 512])
        turn_ps = c.ps("h_turn", [P, 2, 2, 512])
        tile_in, stored, raw_in = c.sems2("tile_in"), c.sems2("stored"), c.sems2("raw_in")
        names = ("const_in", "mhalf_done", "passed", "w_hi", "w_lo", "m_hi", "m_lo", "products", "post_sq", "post_ms", "post_rstd",
                 "post_normed", "h_done", "pre_sq", "pre_ms", "pre_rstd", "pre_normed", "turned", "copied")
        s = {n: c.sem(n) for n in names}

        with nc.Block("mix_out") as block:
            @block.sync
            def _(sp):
                sp.dma_start(gains[:, 0], io["ln1_post_g"][0].partition_broadcast(P)).then_inc(s["const_in"], 16)
                sp.dma_start(gains[:, 1], io["ln2_pre_g"][0].partition_broadcast(P)).then_inc(s["const_in"], 16)
                sp.dma_start(ident[:], io["ident"]).then_inc(s["const_in"], 16)
                for k in range(KD):
                    if k >= 2:
                        sp.wait_ge(s["w_lo"], k - 1)
                    sp.dma_start(raw[:, k % 2], io["w_out"][k * P:(k + 1) * P, :]).then_inc(raw_in[k % 2], 16)
                with sp.Fori(0, NT // 2) as i:
                    for u in range(2):
                        sp.wait_ge(s["h_done"], i * 2 + (u + 1))
                        sp.dma_start(mt[:, u].rearrange("p k t -> p (k t)"), io["m_s"][bass.ds(i * 2 + u, 1)].rearrange("a p k t -> p (a k t)")).then_inc(tile_in[u], 16)
                        sp.dma_start(xt[:, u], io["x"][bass.ds(i * 256 + u * P, P), :]).then_inc(tile_in[u], 16)

            @block.gpsimd
            def _(pool):
                pool.sem_inc(s["products"], 2)
                pool.memset(mhalf[:], -0.5).then_inc(s["mhalf_done"], 1)
                pool.wait_ge(s["mhalf_done"], 1)

                def split(u, t):
                    pool.wait_ge(tile_in[u], uses(u, t, 32))
                    hold(pool, s["passed"], s["products"], t + 1)
                    pool.tensor_copy(mhi[:, u], mt[:, u]).then_inc(s["m_hi"], 1)
                    pool.wait_ge(s["m_hi"], t + 1)
                    pool.tensor_tensor(mlo[:, u], mt[:, u], f32(mhi[:, u]), ALU.subtract).then_inc(s["m_lo"], 1)

                def norms(u, t):
                    for n, name in enumerate(("post", "pre")):
                        hold(pool, s["passed"], s[name + "_sq"], t + 1)
                        pool.tensor_scalar(stat[:, u, n, 1:2], stat[:, u, n, 0:1], 1.0 / D, EPS, ALU.mult, ALU.add).then_inc(s[name + "_ms"], 1)
                        pool.wait_ge(s[name + "_ms"], t + 1)
                        pool.tensor_tensor(stat[:, u, n, 2:3], stat[:, u, n, 1:2], mhalf[:], ALU.pow).then_inc(s[name + "_rstd"], 1)
                ahead(pool, NT, split, norms)

            @block.tensor
            def _(pe):
                pe.wait_ge(s["const_in"], 48)

                def products(u, t):
                    pe.wait_ge(s["m_lo"], t + 1)
                    pe.wait_ge(s["post_normed"], t + 1)
                    for k in range(KD):
                        if isinstance(t, int) and t == 0:
                            pe.wait_ge(s["w_lo"], k + 1)
                        for first, (x, w) in enumerate(((mhi, whi), (mhi, wlo), (mlo, whi))):
                            for b in range(2):
                                mm = pe.matmul(acc[:, u, b], x[:, u, k], w[:, k, b * 512:(b + 1) * 512], start=k == 0 and first == 0,
                                               stop=k == KD - 1 and first == 2)
                    mm.then_inc(s["products"], 1)

                def turn(u, t):
                    pe.wait_ge(s["pre_normed"], t + 1)
                    pe.wait_ge(s["copied"], t + 1)
                    for k in range(KD):
                        tr = pe.transpose(turn_ps[:, u, k // 4, (k % 4) * P:(k % 4 + 1) * P], hn[:, u, k * P:(k + 1) * P], ident[:])
                    tr.then_inc(s["turned"], 1)
                ahead(pe, NT, products, turn)

            @block.scalar
            def _(act):
                for u in range(2):
                    act.sem_inc(stored[u], 32)
                act.sem_inc(s["copied"], 2)
                for k in range(KD):
                    act.wait_ge(raw_in[k % 2], 16 * (k // 2 + 1))
                    act.activation(whi[:, k], raw[:, k % 2], ACT.Copy).then_inc(s["w_hi"], 1)

                def squares(u, t):
                    act.wait_ge(s["products"], t + 3)
                    act.activation(junk[:, 0], acc[:, u].rearrange("p b n -> p (b n)"), ACT.Square, accum_out=stat[:, u, 0, 0:1]).then_inc(s["post_sq"], 1)
                    act.wait_ge(s["h_done"], t + 3)
                    act.activation(junk[:, 1], h[:, u], ACT.Square, accum_out=stat[:, u, 1, 0:1]).then_inc(s["pre_sq"], 1)

                def store(u, t):
                    act.wait_ge(s["turned"], t + 1)
                    act.wait_ge(stored[u], uses(u, t, 32))
                    act.activation(ht[:, u].rearrange("p k t -> p (k t)"), turn_ps[:, u].rearrange("p b n -> p (b n)"), ACT.Copy).then_inc(s["copied"], 1)
                    act.wait_ge(s["copied"], t + 3)
                    act.dma_start(io["ht_s"][:, :, bass.ds(t * P, P)].rearrange("k p t -> p k t"), ht[:, u]).then_inc(stored[u], 16)
                    act.dma_start(io["h_s"][bass.ds(t * P, P), :], h[:, u]).then_inc(stored[u], 16)
                ahead(act, NT, squares, store)
                for u in range(2):
                    act.wait_ge(stored[u], 32 * (NT // 2 + 1))

            @block.vector
            def _(dve):
                dve.sem_inc(s["h_done"], 2)
                dve.sem_inc(s["post_normed"], 2)
                for k in range(KD):
                    dve.wait_ge(s["w_hi"], k + 1)
                    dve.tensor_tensor(wlo[:, k], raw[:, k % 2], f32(whi[:, k]), ALU.subtract).then_inc(s["w_lo"], 1)
                dve.wait_ge(s["const_in"], 48)
                with dve.Fori(0, NT // 2) as i:
                    for u in range(2):
                        t = i * 2 + u
                        dve.wait_ge(s["post_rstd"], t + 1)
                        dve.wait_ge(stored[u], i * 32 + 32)
                        dve.scalar_tensor_tensor(h[:, u], acc[:, u].rearrange("p b n -> p (b n)"), stat[:, u, 0, 2:3], gains[:, 0],
                                                 ALU.mult, ALU.mult).then_inc(s["post_normed"], 1)
                        dve.wait_ge(s["post_normed"], t + 3)
                        dve.tensor_tensor(h[:, u], h[:, u], xt[:, u], ALU.add).then_inc(s["h_done"], 1)
                        dve.wait_ge(s["pre_rstd"], t + 1)
                        dve.scalar_tensor_tensor(hn[:, u], h[:, u], stat[:, u, 1, 2:3], gains[:, 1], ALU.mult, ALU.mult).then_inc(s["pre_normed"], 1)
    end_phase(nc, c)


def ff_in(nc, io):
    with ExitStack() as ctx:
        c = Core(nc, ctx, "ff_in")
        x_hi = c.sb("ffx_hi", [P, KD, TOK], F32R)
        x_lo = c.sb("ffx_lo", [P, KD, TOK], F32R)
        xraw = c.sb("ffx_raw", [P, 2, TOK])
        raw = c.sb("w1_raw", [P, 2, KD, P])
        whi = c.sb("w1_hi", [P, 2, KD, P], F32R)
        wlo = c.sb("w1_lo", [P, 2, KD, P], F32R)
        stage = c.sb("ff_stage", [P, 2, TOK])
        acc = c.ps("ff_ps", [P, 2, NG, 512])
        names = ("passed", "x_hi", "x_lo")
        s = {n: c.sem(n) for n in names}
        x_in, w_in, w_hi, w_ready, acc_done, acc_used, squared, stored = (c.sems2(n) for n in (
            "x_in", "w_in", "w_hi", "w_ready", "acc_done", "acc_used", "squared", "stored"))

        with nc.Block("ff_in") as block:
            @block.sync
            def _(sp):
                for k in range(KD):
                    if k >= 2:
                        sp.wait_ge(s["x_lo"], k - 1)
                    sp.dma_start(xraw[:, k % 2], io["ht_s"][k]).then_inc(x_in[k % 2], 16)
                with sp.Fori(0, DFF // 256) as i:
                    for u in range(2):
                        sp.wait_ge(w_ready[u], i + 1)
                        sp.dma_start(raw[:, u], io["w_ff_in"].rearrange("(k p) n -> p k n", p=P)[:, :, bass.ds(i * 256 + u * P, P)]).then_inc(w_in[u], 16)

            @block.gpsimd
            def _(pool):
                for u in range(2):
                    pool.sem_inc(w_ready[u], 1)
                with pool.Fori(0, DFF // 256) as i:
                    for u in range(2):
                        pool.wait_ge(w_in[u], i * 16 + 16)
                        hold(pool, s["passed"], acc_done[u], i + 1)
                        pool.tensor_copy(whi[:, u], raw[:, u]).then_inc(w_hi[u], 1)
                        pool.wait_ge(w_hi[u], i + 1)
                        pool.tensor_tensor(wlo[:, u], raw[:, u], f32(whi[:, u]), ALU.subtract).then_inc(w_ready[u], 1)

            @block.tensor
            def _(pe):
                for u in range(2):
                    pe.sem_inc(acc_done[u], 1)
                pe.wait_ge(s["x_lo"], KD)
                with pe.Fori(0, DFF // 256) as i:
                    for u in range(2):
                        pe.wait_ge(w_ready[u], i + 2)
                        pe.wait_ge(acc_used[u], i + 1)
                        split_matmuls(pe, [acc[:, u, g] for g in range(NG)],
                                      lambda k, g: (whi[:, u, k], wlo[:, u, k], x_hi[:, k, g * 512:(g + 1) * 512],
                                                    x_lo[:, k, g * 512:(g + 1) * 512]), KD).then_inc(acc_done[u], 1)

            @block.scalar
            def _(act):
                for u in range(2):
                    act.sem_inc(acc_used[u], 1)
                    act.sem_inc(stored[u], 16)
                for k in range(KD):
                    act.wait_ge(x_in[k % 2], 16 * (k // 2 + 1))
                    act.activation(x_hi[:, k], xraw[:, k % 2], ACT.Copy).then_inc(s["x_hi"], 1)
                with act.Fori(0, DFF // 256) as i:
                    for u in range(2):
                        act.wait_ge(acc_done[u], i + 2)
                        act.wait_ge(stored[u], i * 16 + 16)
                        act.activation(stage[:, u], acc[:, u].rearrange("p g t -> p (g t)"), ACT.Relu).then_inc(acc_used[u], 1)
                        act.wait_ge(acc_used[u], i + 2)
                        act.activation(stage[:, u], stage[:, u], ACT.Square).then_inc(squared[u], 1)
                        act.wait_ge(squared[u], i + 1)
                        act.dma_start(io["hid_s"][:, :, bass.ds(i * 2 + u, 1), :].rearrange("t p a j -> p t (a j)"),
                                      stage[:, u].rearrange("p (t j) -> p t j", j=P)).then_inc(stored[u], 16)
                for u in range(2):
                    act.wait_ge(stored[u], 16 * (DFF // 256 + 1))

            @block.vector
            def _(dve):
                for k in range(KD):
                    dve.wait_ge(s["x_hi"], k + 1)
                    dve.tensor_tensor(x_lo[:, k], xraw[:, k % 2], f32(x_hi[:, k]), ALU.subtract).then_inc(s["x_lo"], 1)
    end_phase(nc, c)


def ff_out(nc, io):
    KF = DFF // P
    HC = D // 2
    WCH = KF // 4
    CHUNKS = WCH + 2 * NT
    with ExitStack() as ctx:
        c = Core(nc, ctx, "ff_out")
        whi = c.sb("w2_hi", [P, KF, HC], F32R)
        wlo = c.sb("w2_lo", [P, KF, HC], F32R)
        raw = c.sb("ff_raw", [P, 2, 4 * HC])
        hhi = c.sb("hid_hi", [P, 2, KF // 2, P], F32R)
        hlo = c.sb("hid_lo", [P, 2, KF // 2, P], F32R)
        y0 = c.sb("y_half", [P, 2, HC])
        h = c.sb("h_in", [P, 2, D])
        out = c.sb("y_out", [P, D])
        junk = c.sb("squares_g", [P, 2, HC])
        gain = c.sb("gain_g", [P, D])
        stat = c.sb("stat_g", [P, 2, 4])
        mhalf = c.sb("mhalf_g", [P, 1])
        acc = c.ps("y_ps", [P, 2, 512])
        raw_in, y_stored, h_in = c.sems2("raw_in"), c.sems2("y_stored"), c.sems2("h_in")
        names = ("const_in", "mhalf_done", "passed", "hi_done", "lo_done", "products", "y_copied", "squared", "sum_done", "ms_done",
                 "rstd_done", "acc_used", "normed", "added", "out_stored")
        s = {n: c.sem(n) for n in names}

        with nc.Block("ff_out") as block:
            @block.sync
            def _(sp):
                sp.dma_start(gain[:], io["ln2_post_g"][0].partition_broadcast(P)).then_inc(s["const_in"], 16)
                for half in range(2):
                    base = half * CHUNKS
                    for n in range(WCH):
                        sp.wait_ge(s["lo_done"], base + n + 1)
                        sp.dma_start(raw[:, n % 2].rearrange("p (k j) -> p k j", k=4),
                                     io["w_ff_out"].rearrange("(k p) n -> p k n", p=P)[:, 4 * n:4 * n + 4, half * HC:(half + 1) * HC]).then_inc(raw_in[n % 2], 16)
                    if half:
                        for u in range(2):
                            sp.wait_ge(y_stored[u], 16 * (NT // 2 + 1))
                    with sp.Fori(0, NT // 2) as i:
                        for u in range(2):
                            t = i * 2 + u
                            if half:
                                sp.wait_ge(s["added"], t + 1)
                                sp.dma_start(y0[:, u], io["y0_s"][bass.ds(t * P, P), :]).then_inc(h_in[u], 16)
                                sp.dma_start(h[:, u], io["h_s"][bass.ds(t * P, P), :]).then_inc(h_in[u], 16)
                            for kh in range(2):
                                sp.wait_ge(s["lo_done"], t * 2 + (base + WCH + kh + 1))
                                sp.dma_start(raw[:, kh].rearrange("p (k j) -> p k j", j=P),
                                             io["hid_s"][bass.ds(t, 1)].rearrange("a p k j -> p (a k) j")[:, kh * KF // 2:(kh + 1) * KF // 2, :]).then_inc(raw_in[kh], 16)

            @block.tensor
            def _(pe):
                pe.sem_inc(s["products"], 2)
                for half in range(2):
                    with pe.Fori(0, NT // 2) as i:
                        for u in range(2):
                            t = i * 2 + u
                            pe.wait_ge(s["acc_used"], t + (half * NT + 1))
                            for kh in range(2):
                                pe.wait_ge(s["lo_done"], t * 2 + (half * CHUNKS + WCH + kh + 3))
                                for k in range(KF // 2):
                                    w = kh * KF // 2 + k
                                    for first, (x, y) in enumerate(((hhi, whi), (hhi, wlo), (hlo, whi))):
                                        mm = pe.matmul(acc[:, u], x[:, kh, k], y[:, w], start=w == 0 and first == 0, stop=w == KF - 1 and first == 2)
                                mm.then_inc(s["products"], 1)

            @block.scalar
            def _(act):
                for u in range(2):
                    act.sem_inc(y_stored[u], 16)
                act.sem_inc(s["out_stored"], 16)
                for half in range(2):
                    base = half * CHUNKS
                    for n in range(WCH):
                        act.wait_ge(raw_in[n % 2], ((base + n) // 2 + 1) * 16)
                        if half:
                            act.wait_ge(s["products"], 2 * NT + (1 if n < WCH // 2 else 2))
                        act.activation(whi[:, 4 * n:4 * n + 4].rearrange("p k j -> p (k j)"), raw[:, n % 2], ACT.Copy).then_inc(s["hi_done"], 1)

                    def hidden(u, t):
                        for kh in range(2):
                            act.wait_ge(raw_in[kh], (t + (half * CHUNKS // 2 + WCH // 2 + 1)) * 16)
                            act.wait_ge(s["products"], t * 2 + (half * 2 * NT + kh + 1))
                            act.activation(hhi[:, kh].rearrange("p k j -> p (k j)"), raw[:, kh], ACT.Copy).then_inc(s["hi_done"], 1)

                    def keep(u, t):
                        act.wait_ge(s["products"], t * 2 + 4)
                        act.wait_ge(y_stored[u], uses(u, t, 16))
                        act.activation(y0[:, u], acc[:, u], ACT.Copy).then_inc(s["acc_used"], 1)
                        act.wait_ge(s["acc_used"], t + 3)
                        act.dma_start(io["y0_s"][bass.ds(t * P, P), :], y0[:, u]).then_inc(y_stored[u], 16)

                    def finish(u, t):
                        act.wait_ge(s["products"], t * 2 + (2 * NT + 4))
                        act.activation(junk[:, 0], acc[:, u], ACT.Square, accum_out=stat[:, u, 0:1])
                        act.wait_ge(h_in[u], uses(u, t, 32))
                        act.activation(junk[:, 1], y0[:, u], ACT.Square, accum_out=stat[:, u, 1:2]).then_inc(s["squared"], 1)
                        act.wait_ge(s["added"], t + 3)
                        act.dma_start(io["y"][bass.ds(t * P, P), :], out[:]).then_inc(s["out_stored"], 16)
                    ahead(act, NT, hidden, finish if half else keep)
                act.wait_ge(s["out_stored"], 16 * (NT + 1))

            @block.vector
            def _(dve):
                dve.sem_inc(s["lo_done"], 2)
                dve.sem_inc(s["acc_used"], 2)
                dve.sem_inc(s["added"], 2)
                dve.wait_ge(s["const_in"], 16)
                for half in range(2):
                    base = half * CHUNKS
                    for n in range(WCH):
                        dve.wait_ge(s["hi_done"], base + n + 1)
                        dve.tensor_tensor(wlo[:, 4 * n:4 * n + 4].rearrange("p k j -> p (k j)"), raw[:, n % 2],
                                          f32(whi[:, 4 * n:4 * n + 4]).rearrange("p k j -> p (k j)"), ALU.subtract).then_inc(s["lo_done"], 1)

                    def hidden(u, t):
                        for kh in range(2):
                            dve.wait_ge(s["hi_done"], t * 2 + (half * CHUNKS + WCH + kh + 1))
                            dve.tensor_tensor(hlo[:, kh].rearrange("p k j -> p (k j)"), raw[:, kh],
                                              f32(hhi[:, kh]).rearrange("p k j -> p (k j)"), ALU.subtract).then_inc(s["lo_done"], 1)

                    def finish(u, t):
                        dve.wait_ge(s["rstd_done"], t + 1)
                        dve.wait_ge(s["out_stored"], t * 16 + 16)
                        dve.scalar_tensor_tensor(out[:, 0:HC], y0[:, u], stat[:, u, 3:4], gain[:, 0:HC], ALU.mult, ALU.mult).then_inc(s["normed"], 1)
                        dve.scalar_tensor_tensor(out[:, HC:D], acc[:, u], stat[:, u, 3:4], gain[:, HC:D], ALU.mult, ALU.mult).then_inc(s["acc_used"], 1)
                        dve.wait_ge(s["normed"], t + 1)
                        dve.wait_ge(s["acc_used"], t + (NT + 3))
                        dve.tensor_tensor(out[:], out[:], h[:, u], ALU.add).then_inc(s["added"], 1)
                    ahead(dve, NT, hidden, finish if half else lambda u, t: None)

            @block.gpsimd
            def _(pool):
                pool.memset(mhalf[:], -0.5).then_inc(s["mhalf_done"], 1)
                pool.wait_ge(s["mhalf_done"], 1)
                with pool.Fori(0, NT // 2) as i:
                    for u in range(2):
                        t = i * 2 + u
                        pool.wait_ge(s["squared"], t + 1)
                        pool.tensor_tensor(stat[:, u, 2:3], stat[:, u, 0:1], stat[:, u, 1:2], ALU.add).then_inc(s["sum_done"], 1)
                        hold(pool, s["passed"], s["sum_done"], t + 1)
                        pool.tensor_scalar(stat[:, u, 2:3], stat[:, u, 2:3], 1.0 / D, EPS, ALU.mult, ALU.add).then_inc(s["ms_done"], 1)
                        pool.wait_ge(s["ms_done"], t + 1)
                        pool.tensor_tensor(stat[:, u, 3:4], stat[:, u, 2:3], mhalf[:], ALU.pow).then_inc(s["rstd_done"], 1)
    end_phase(nc, c)


PHASES = [project, prepare, attend, deltanet, merge, mix_out, ff_in, ff_out]
SCRATCH = {"qkv_s": (QKV_W, TOK), "dqkv_s": (3 * DNW, TOK), "z_s": (DNW, TOK), "ba_s": (4 * NH, TOK),
           "gate_s": (2 * D, TOK), "q_s": (NQH, P, TOK), "k_s": (2 * NKVH, P, TOK), "v_s": (NKVH, P, NT, P),
           "dn_s": (NT, P, 5 * DNW), "bg_s": (P, 2 * NT * 2 * NH), "at_s": (P, NT * NQH * HD), "do_s": (2, NT, P, DNW),
           "m_s": (NT, P, KD, P), "h_s": (TOK, D), "ht_s": (KD, P, TOK), "hid_s": (NT, P, DFF // P, P), "y0_s": (TOK, D // 2)}


def program(nc, io):
    for phase in PHASES:
        phase(nc, io)


def constants():
    tok = np.concatenate([np.arange(T0), np.arange(T1)]).astype(np.float32)
    inv = (np.float32(10000.0) ** (-np.arange(0, 32, 2, dtype=np.float32) / np.float32(32))).astype(np.float32)
    angles = [np.floor(tok / GRID_W)[:, None] * inv, (tok % GRID_W)[:, None] * inv]
    cos = np.concatenate([np.cos(a) for a in angles for _ in range(2)], 1)
    sin = np.concatenate([sign * np.sin(a) for a in angles for sign in (-1, 1)], 1)
    a, b = np.arange(P)[:, None], np.arange(P)[None]
    level = {w: (a // (2 * w) == b // (2 * w)) & (a % (2 * w) >= w) & (b % (2 * w) < w) for w in [1] + LEVELS}
    fwd = [a <= b, a > b, -1.0 * level[1].T] + [level[w] for w in LEVELS]
    bwd = [a >= b, a < b, -1.0 * level[1]] + [level[w].T for w in LEVELS]
    masks = np.stack([np.asarray(m, np.float32) for m in fwd + bwd], 1).reshape(P, -1)
    return {"masks": masks, "ident": np.eye(P, dtype=np.float32), "rope": np.concatenate([cos, sin], 1).astype(np.float32)}


def kernel(**inputs):
    import concourse.bacc as bacc
    from concourse.bass_utils import run_bass_kernel_spmd

    nc = bacc.Bacc("TRN2", target_bir_lowering=False, num_devices=1)
    arrays = {k: np.ascontiguousarray(v) for k, v in inputs.items() if k not in ("x_prompt", "x_sample", "dn_conv_w")}
    arrays = {k: v[0] if v.shape[0] == 1 and v.ndim == 3 else v for k, v in arrays.items()}
    arrays["x"] = np.concatenate([np.asarray(inputs["x_prompt"])[0], np.asarray(inputs["x_sample"])[0]])
    arrays["conv_w"] = np.ascontiguousarray(np.asarray(inputs["dn_conv_w"])[0].T)
    arrays |= constants()
    io = {k: nc.dram_tensor(f"in_{k}", v.shape, F32, kind="ExternalInput").ap() for k, v in arrays.items()}
    for k, shape in SCRATCH.items():
        io[k] = nc.dram_tensor(f"s_{k}", shape, F32, kind="Internal").ap()
    io["y"] = nc.dram_tensor("y", (TOK, D), F32, kind="ExternalOutput").ap()
    program(nc, io)
    r = run_bass_kernel_spmd(nc, [{f"in_{k}": v for k, v in arrays.items()}], core_ids=[0]).results[0]
    return r["y"][None, :T0], r["y"][None, T0:]
```

```python
from contextlib import ExitStack

import concourse.bass as bass
from concourse import mybir
import numpy as np

F32 = mybir.dt.float32
F32R = mybir.dt.float32r
ACT = mybir.ActivationFunctionType
ALU = mybir.AluOpType
AX = mybir.AxisListType

P = 128
D = 1024
KD = D // P
T0, T1 = 1024, 512
TOK = T0 + T1
NT = TOK // P
SEQS = [(0, T0 // P), (T0 // P, T1 // P)]
NG = TOK // 512
GRID_W = 64
NQH, NKVH, HD = 8, 2, 64
NH, DH = 4, 128
DNW = NH * DH
DFF = 4 * D
EPS = 1e-6
QKV_W = NQH * HD + 2 * NKVH * HD
DQKV_COL = QKV_W
DZ_COL = DQKV_COL + 3 * DNW
BA_COL = DZ_COL + DNW
GATE_COL = BA_COL + 4 * NH
PROJ_W = GATE_COL + 2 * D


def f32(ap):
    return ap.bitcast(F32)


def along(ap, axis, n):
    a = ap.unsqueeze(axis)
    shape = list(a.shape)
    shape[axis] = n
    return a.to_broadcast(shape)


def hold(pool, passed, sem, value):
    pool.wait_ge(sem, value)
    pool.sem_inc(passed, 1)


class Core:

    def __init__(self, nc, ctx, phase):
        self.nc, self.ctx, self.phase = nc, ctx, phase
        self.sems = []

    def sb(self, name, shape, dt=F32):
        return self.ctx.enter_context(self.nc.sbuf_tensor(name, shape, dt))

    def ps(self, name, shape):
        return self.ctx.enter_context(self.nc.psum_tensor(name, shape, F32))

    def sem(self, name):
        s = self.nc.alloc_semaphore(f"{self.phase}_{name}")
        self.sems.append(s)
        return s

    def sems2(self, name):
        return [self.sem(f"{name}{u}") for u in range(2)]


def end_phase(nc, core):
    nc.clear_and_free_semaphores(core.sems)
    nc.all_engine_barrier()


def split_matmuls(pe, out, pairs, n_k, ahead_of_k=None):
    for k in range(n_k):
        if ahead_of_k:
            ahead_of_k(k)
        for first, (wi, xi) in enumerate(((0, 2), (0, 3), (1, 2))):
            for g, bank in enumerate(out):
                ops = pairs(k, g)
                mm = pe.matmul(bank, ops[wi], ops[xi], start=(k == 0 and first == 0),
                               stop=(k == n_k - 1 and first == 2))
    return mm


def uses(u, t, per):
    return (t + (2 - u)) * (per // 2)


def ahead(eng, n, stage1, stage2, early=None):
    def first(u, t):
        if early:
            early(u, t)
    stage1(0, 0)
    with eng.Fori(0, n // 2 - 1) as i:
        first(0, i * 2)
        stage1(1, i * 2 + 1)
        stage2(0, i * 2)
        first(1, i * 2 + 1)
        stage1(0, i * 2 + 2)
        stage2(1, i * 2 + 1)
    first(0, n - 2)
    stage1(1, n - 1)
    stage2(0, n - 2)
    first(1, n - 1)
    stage2(1, n - 1)


def project(nc, io):
    with ExitStack() as ctx:
        c = Core(nc, ctx, "project")
        ht_hi = c.sb("ht_hi", [P, KD, TOK], F32R)
        ht_lo = c.sb("ht_lo", [P, KD, TOK], F32R)
        xt = c.sb("xt", [P, 2, D])
        gain = c.sb("ln1_gain", [P, D])
        ident = c.sb("ident_a", [P, P])
        stat = c.sb("x_stat", [P, 2, 3])
        mhalf = c.sb("mhalf_a", [P, 1])
        raw = c.sb("win_raw", [P, 2, KD, P])
        whi = c.sb("win_hi", [P, 2, KD, P], F32R)
        wlo = c.sb("win_lo", [P, 2, KD, P], F32R)
        stage = c.sb("proj_stage", [P, 2, TOK])
        conv = c.sb("conv_out", [P, TOK])
        taps = c.sb("conv_taps", [P, 2, 3])
        xn = [stage[:, u, 0:D] for u in range(2)]
        acc = c.ps("proj_ps", [P, 2, NG, 512])
        xps = c.ps("xt_ps", [P, 2, 512])

        x_in = c.sems2("x_in")
        const_in, ss_done, ms_done, rstd_done = (c.sem(n) for n in ("const_in", "ss_done", "ms_done", "rstd_done"))
        xn_done, xt_done, hi_done, lo_done = (c.sem(n) for n in ("xn_done", "xt_done", "hi_done", "lo_done"))
        mhalf_done, passed = c.sem("mhalf_done"), c.sem("passed")
        w_in, w_hi, w_ready, acc_done = (c.sems2(n) for n in ("w_in", "w_hi", "w_ready", "acc_done"))
        acc_used, stage_done, stored = (c.sems2(n) for n in ("acc_used", "stage_done", "stored"))
        taps_in, conv_step, sig_done, silu_done = c.sems2("taps_in"), c.sem("conv_step"), c.sems2("sig_done"), c.sems2("silu_done")

        w_cols = io["w_in"].rearrange("(ko p) n -> p ko n", p=P)
        groups = [("plain", 0, QKV_W // 256, io["qkv_s"], 0),
                  ("conv", DQKV_COL, 3 * DNW // 256, io["dqkv_s"], 0),
                  ("silu", DZ_COL, DNW // 256, io["z_s"], 0),
                  ("ba", BA_COL, 0.5, io["ba_s"], 0),
                  ("gate", GATE_COL, 2 * D // 256, io["gate_s"], 0)]

        def tiles(eng, body, kinds=("plain", "conv", "silu", "ba", "gate"), start=0):
            done = [0, 0]
            for kind, col0, pairs, dst, row0 in groups:
                if kind not in kinds:
                    done = [d + (pairs if pairs != 0.5 else 1 - u) for u, d in enumerate(done)]
                    continue
                if pairs == 0.5:
                    body(0, done[0] + 1, kind, col0, dst, row0)
                    done[0] += 1
                    continue
                with eng.Fori(start if kind == "plain" else 0, pairs) as i:
                    for u in range(2):
                        body(u, i + done[u] + 1, kind, i * 256 + (col0 + u * P), dst, i * 256 + (row0 + u * P))
                done = [d + pairs for d in done]
            return done

        block = ctx.enter_context(nc.Block("project"))

        @block.sync
        def _(sp):
            sp.dma_start(gain[:], io["ln1_pre_g"][0].partition_broadcast(P)).then_inc(const_in, 16)
            sp.dma_start(ident[:], io["ident"]).then_inc(const_in, 16)
            def load(u, n, kind, col, dst, row):
                sp.wait_ge(w_ready[u], n)
                sp.dma_start(raw[:, u], w_cols[:, :, bass.ds(col, P)]).then_inc(w_in[u], 16)
                if kind == "conv":
                    sp.wait_ge(silu_done[u], n - QKV_W // 256)
                    sp.dma_start(taps[:, u, :], io["conv_w"][bass.ds(row, P), :]).then_inc(taps_in[u], 16)
            for u in range(2):
                load(u, 1, "plain", u * P, io["qkv_s"], 0)
            with sp.Fori(0, NT // 2) as i:
                for u in range(2):
                    sp.wait_ge(xn_done, i * 2 + (u + 1))
                    sp.dma_start(xt[:, u, :], io["x"][bass.ds(i * 256 + u * P, P), :]).then_inc(x_in[u], 16)
            tiles(sp, load, start=1)

        @block.gpsimd
        def _(pool):
            pool.memset(mhalf[:], -0.5).then_inc(mhalf_done, 1)
            for u in range(2):
                pool.sem_inc(w_ready[u], 1)
            pool.wait_ge(mhalf_done, 1)
            with pool.Fori(0, NT // 2) as i:
                for u in range(2):
                    t = i * 2 + u
                    hold(pool, passed, ss_done, t + 1)
                    pool.tensor_scalar(stat[:, u, 1:2], stat[:, u, 0:1], 1.0 / D, EPS, ALU.mult, ALU.add).then_inc(ms_done, 1)
                    pool.wait_ge(ms_done, t + 1)
                    pool.tensor_tensor(stat[:, u, 2:3], stat[:, u, 1:2], mhalf[:], ALU.pow).then_inc(rstd_done, 1)
            def split(u, n, kind, col, dst, row):
                pool.wait_ge(w_in[u], n * 16)
                hold(pool, passed, acc_done[u], n)
                pool.tensor_copy(whi[:, u], raw[:, u]).then_inc(w_hi[u], 1)
                pool.wait_ge(w_hi[u], n)
                pool.tensor_tensor(wlo[:, u], raw[:, u], f32(whi[:, u]), ALU.subtract).then_inc(w_ready[u], 1)
            tiles(pool, split)

        @block.tensor
        def _(pe):
            for u in range(2):
                pe.sem_inc(acc_done[u], 1)
            pe.wait_ge(const_in, 32)
            with pe.Fori(0, NT // 2) as i:
                for u in range(2):
                    t = i * 2 + u
                    pe.wait_ge(xn_done, t + 3)
                    for half in range(2):
                        pe.wait_ge(lo_done, t * 2 + (half + 1))
                        for k in range(4):
                            tr = pe.transpose(xps[:, half, k * P:(k + 1) * P], xn[u][:, (4 * half + k) * P:(4 * half + k + 1) * P], ident[:])
                        tr.then_inc(xt_done, 1)
            pe.wait_ge(lo_done, 2 * NT + 2)

            def products(u, n, kind, col, dst, row):
                pe.wait_ge(w_ready[u], n + 1)
                pe.wait_ge(acc_used[u], n)
                split_matmuls(pe, [acc[:, u, g] for g in range(NG)],
                              lambda k, g: (whi[:, u, k], wlo[:, u, k], ht_hi[:, k, g * 512:(g + 1) * 512],
                                            ht_lo[:, k, g * 512:(g + 1) * 512]), KD).then_inc(acc_done[u], 1)
            tiles(pe, products)

        @block.scalar
        def _(act):
            for u in range(2):
                act.sem_inc(acc_used[u], 1)
                act.sem_inc(stored[u], 16)

            def square(u, t):
                act.wait_ge(x_in[u], uses(u, t, 16))
                act.activation(acc[:, u, 0:2].rearrange("p g t -> p (g t)"), xt[:, u, :], ACT.Square, accum_out=stat[:, u, 0:1]).then_inc(ss_done, 1)

            def copy_hi(u, t):
                for half in range(2):
                    act.wait_ge(xt_done, t * 2 + (half + 1))
                    act.activation(ht_hi[:, 4 * half:4 * half + 4, bass.ds(t * P, P)],
                                   xps[:, half].rearrange("p (k t) -> p k t", k=4), ACT.Copy).then_inc(hi_done, 1)
            ahead(act, NT, square, copy_hi)

            def evacuate(u, n, kind, col, dst, row):
                act.wait_ge(acc_done[u], n + 1)
                act.wait_ge(stored[u], n * 16)
                banks = acc[:, u].rearrange("p g t -> p (g t)")
                if kind in ("plain", "ba", "conv", "silu"):
                    act.activation(stage[:, u], banks, ACT.Copy).then_inc(acc_used[u], 1)
                if kind == "gate":
                    act.activation(stage[:, u], banks, ACT.Sigmoid).then_inc(acc_used[u], 1)
                if kind == "conv":
                    act.wait_ge(conv_step, (n - QKV_W // 256 - 1) * 6 + 3 * u + 3)
                    act.activation(stage[:, u], conv[:], ACT.Sigmoid).then_inc(sig_done[u], 1)
                if kind == "silu":
                    act.wait_ge(acc_used[u], n + 1)
                    act.activation(conv[:], stage[:, u], ACT.Sigmoid).then_inc(sig_done[u], 1)
                if kind in ("conv", "silu"):
                    act.wait_ge(silu_done[u], n - QKV_W // 256 + 1)
                else:
                    act.wait_ge(acc_used[u], n + 1)
                if kind == "ba":
                    act.dma_start(dst, stage[0:4 * NH, u]).then_inc(stored[u], 16)
                else:
                    act.dma_start(dst[bass.ds(row, P), :], stage[:, u]).then_inc(stored[u], 16)
            done = tiles(act, evacuate)
            for u in range(2):
                act.wait_ge(stored[u], 16 * done[u] + 16)

        @block.vector
        def _(dve):
            for u in range(2):
                dve.sem_inc(silu_done[u], 1)
            dve.sem_inc(lo_done, 2)
            dve.sem_inc(xn_done, 2)
            dve.wait_ge(const_in, 32)

            def normalise(u, t):
                dve.wait_ge(rstd_done, t + 1)
                dve.scalar_tensor_tensor(xn[u], xt[:, u, :], stat[:, u, 2:3], gain[:], ALU.mult, ALU.mult).then_inc(xn_done, 1)

            def subtract_hi(u, t):
                for half in range(2):
                    dve.wait_ge(hi_done, t * 2 + (half + 1))
                    out = ht_lo[:, 4 * half:4 * half + 4, bass.ds(t * P, P)]
                    hi = f32(ht_hi[:, 4 * half:4 * half + 4, bass.ds(t * P, P)])
                    dve.tensor_tensor(out, xps[:, half].rearrange("p (k t) -> p k t", k=4), hi, ALU.subtract).then_inc(lo_done, 1)
            ahead(dve, NT, normalise, subtract_hi)

            def act_on(u, n, kind, col, dst, row):
                m = n - QKV_W // 256
                if kind == "conv":
                    x, s = stage[:, u], (m - 1) * 6 + 3 * u
                    dve.wait_ge(taps_in[u], m * 16)
                    dve.wait_ge(acc_used[u], n + 1)
                    dve.tensor_scalar(conv[:], x, taps[:, u, 1:2], None, ALU.mult).then_inc(conv_step, 1)
                    dve.wait_ge(conv_step, s + 1)
                    for a, b in ((0, T0), (T0, TOK)):
                        op = dve.scalar_tensor_tensor(conv[:, a + 1:b], x[:, a:b - 1], taps[:, u, 0:1],
                                                      conv[:, a + 1:b], ALU.mult, ALU.add)
                    op.then_inc(conv_step, 1)
                    dve.wait_ge(conv_step, s + 2)
                    for a, b in ((0, T0), (T0, TOK)):
                        op = dve.scalar_tensor_tensor(conv[:, a:b - 1], x[:, a + 1:b], taps[:, u, 2:3],
                                                      conv[:, a:b - 1], ALU.mult, ALU.add)
                    op.then_inc(conv_step, 1)
                if kind in ("conv", "silu"):
                    dve.wait_ge(sig_done[u], m)
                    dve.tensor_tensor(stage[:, u], stage[:, u], conv[:], ALU.mult).then_inc(silu_done[u], 1)
            tiles(dve, act_on, ("conv", "silu"))
    end_phase(nc, c)


def prepare(nc, io):
    B = 3
    NQK = NQH + NKVH
    QK = NQK * HD
    with ExitStack() as ctx:
        c = Core(nc, ctx, "prepare")
        feat = c.sb("feat", [P, B, 22, P])
        feat_ba = c.sb("feat_ba", [4 * NH, B, P])
        rope = c.sb("rope", [P, NT, 2, HD])
        qk = c.sb("qk_tok", [P, B, NQK, HD])
        qk_sq = c.sb("qk_sq", [P, B, NQK, HD])
        qk_g = c.sb("qk_gained", [P, B, NQK, HD])
        rot_a = c.sb("rot_a", [P, B, NQK, HD])
        rot_b = c.sb("rot_b", [P, B, NQK, HD])
        rstd = c.sb("qk_rstd", [P, B, 2, NQK])
        q_split = c.sb("q_split", [P, B, NQH, 2, HD], F32R)
        k_split = c.sb("k_split", [P, B, NKVH, 2, 2, HD], F32R)
        v_split = c.sb("v_split", [P, B, NKVH, 2, HD], F32R)
        dn_sq = c.sb("dn_sq", [P, B, 2 * NH, DH])
        dn_rs = c.sb("dn_rs", [P, B, 2, 2 * NH])
        dn_q = c.sb("dn_q", [P, B, DNW])
        pack = c.sb("dn_pack", [P, B, 5, DNW])
        qt = c.sb("q_t", [P, B, NQH, P])
        kt = c.sb("k_t", [P, B, 2 * NKVH, P])
        ba = c.sb("ba_tok", [P, NT, 4 * NH])
        gain = c.sb("qk_gain", [P, NQK, HD])
        ident = c.sb("ident_b", [P, P])
        mhalf = c.sb("mhalf_b", [P, NQK])
        gates = c.sb("dn_gates", [P, 6, NT, 2 * NH])
        alog = c.sb("alog_row", [P, 2, 2 * NH])
        dtb = c.sb("dtb_row", [P, 2 * NH])
        one = c.sb("one_b", [P, 1])
        ps = c.ps("prep_ps", [P, 8, 512])
        K_TOK, V_TOK, K_T, Q_T, Z_TOK = range(5)

        tile_in, stored = ([c.sem(f"{n}{u}") for u in range(B)] for n in ("tile_in", "p_stored"))
        names = ("const_in", "rope_in", "const_done", "passed", "qkv_turned", "dn_turned", "qkv_copied", "qk_squared", "dn_copied",
                 "v_lo_done", "qk_summed", "dn_summed", "qk_rms", "dn_rs_done", "qk_scaled", "dn_scaled", "qk_gained",
                 "rot_b_done", "rot_step", "split_done", "back_turned", "back_copied", "pool_step", "gate_step", "x_done")
        s = {n: c.sem(n) for n in names}

        def pipeline(eng, turn, scale, finish):
            turn(0, 0, 0)
            with eng.Fori(0, NT // B - 1) as i:
                for u in range(B):
                    scale(u, i * B + u, i)
                    turn((u + 1) % B, i * B + u + 1, i + (u + 1) // B)
                    finish(u, i * B + u, i)
            for t in range(NT - B, NT):
                scale(t % B, t, t // B)
                if t + 1 < NT:
                    turn((t + 1) % B, t + 1, (t + 1) // B)
                finish(t % B, t, t // B)

        def none(u, t, n):
            pass

        with nc.Block("prepare") as block:
            @block.sync
            def _(sp):
                for dst, src in ((gain[:, 0], "attn_q_norm_g"), (gain[:, NQH], "attn_k_norm_g")):
                    sp.dma_start(dst, io[src][0].partition_broadcast(P)).then_inc(s["const_in"], 16)
                sp.dma_start(ident[:], io["ident"]).then_inc(s["const_in"], 16)
                sp.dma_start(alog[:, 0], io["dn_A_log"].rearrange("a b -> (a b)").partition_broadcast(P)).then_inc(s["const_in"], 16)
                sp.dma_start(dtb[:], io["dn_dt_bias"].rearrange("a b -> (a b)").partition_broadcast(P)).then_inc(s["const_in"], 16)
                sp.dma_start(rope[:], io["rope"].rearrange("(t p) (a d) -> p t a d", p=P, a=2)).then_inc(s["rope_in"], 16)
                with sp.Fori(0, NT // B) as i:
                    for u in range(B):
                        tok = bass.ds(i * B * P + u * P, P)
                        sp.wait_ge(s["dn_turned"], i * B + (u + 1))
                        for a, b, src in ((0, 6, "qkv_s"), (6, 18, "dqkv_s"), (18, 22, "z_s")):
                            sp.dma_start(feat[:, u, a:b], io[src].rearrange("(n p) t -> p n t", p=P)[:, :, tok]).then_inc(tile_in[u], 16)
                        sp.dma_start(feat_ba[:, u], io["ba_s"][:, tok]).then_inc(tile_in[u], 16)

            @block.tensor
            def _(pe):
                pe.sem_inc(s["dn_turned"], B)
                pe.wait_ge(s["const_in"], 80)

                def turn(u, t, n):
                    pe.wait_ge(tile_in[u], n * 64 + 64)
                    pe.wait_ge(s["qkv_copied"], t + 1)
                    pe.wait_ge(s["v_lo_done"], t + 1)
                    for k in range(6):
                        pe.transpose(ps[:, k // 4, (k % 4) * P:(k % 4 + 1) * P], feat[:, u, k], ident[:])
                    pe.transpose(ps[:, 1, 256:256 + 4 * NH], feat_ba[:, u], ident[0:4 * NH, 0:4 * NH]).then_inc(s["qkv_turned"], 1)
                    pe.wait_ge(s["dn_copied"], t + 1)
                    pe.wait_ge(s["dn_scaled"], t + 1)
                    for k in range(16):
                        tr = pe.transpose(ps[:, 2 + k // 4, (k % 4) * P:(k % 4 + 1) * P], feat[:, u, 6 + k], ident[:])
                    tr.then_inc(s["dn_turned"], 1)

                def finish(u, t, n):
                    sources = [dn_q[:, u].rearrange("p (h d) -> p h d", h=NH),
                               pack[:, u, K_TOK].rearrange("p (h d) -> p h d", h=NH),
                               f32(q_split[:, u, 0:4]).rearrange("p h s d -> p h (s d)"),
                               f32(q_split[:, u, 4:8]).rearrange("p h s d -> p h (s d)"),
                               f32(k_split[:, u]).rearrange("p h s r d -> p (h s) (r d)")]
                    pe.wait_ge(s["dn_scaled"], t + 2)
                    for g, src in enumerate(sources):
                        if g == 2:
                            pe.wait_ge(s["split_done"], t + 1)
                        pe.wait_ge(s["back_copied"], t * 5 + max(g + 1, 2))
                        for k in range(4):
                            tr = pe.transpose(ps[:, 6 + g % 2, k * P:(k + 1) * P], src[:, k], ident[:])
                        tr.then_inc(s["back_turned"], 1)
                pipeline(pe, turn, none, finish)

            @block.scalar
            def _(act):
                for u in range(B):
                    act.sem_inc(stored[u], 64)
                for n in ("qkv_copied", "dn_copied"):
                    act.sem_inc(s[n], 1)
                act.sem_inc(s["back_copied"], 2)

                def turn(u, t, n):
                    act.wait_ge(s["qkv_turned"], t + 1)
                    act.wait_ge(stored[u], n * 64 + 64)
                    act.activation(qk[:, u, 0:NQH], ps[:, 0].rearrange("p (n d) -> p n d", d=HD), ACT.Copy)
                    act.activation(qk[:, u, NQH:NQK], ps[:, 1, 0:P].rearrange("p (n d) -> p n d", d=HD), ACT.Copy)
                    act.activation(v_split[:, u, :, 0], ps[:, 1, P:2 * P].rearrange("p (n d) -> p n d", d=HD), ACT.Copy)
                    act.activation(ba[:, bass.ds(t, 1), :].rearrange("p a n -> p (a n)"), ps[:, 1, 256:256 + 4 * NH], ACT.Copy).then_inc(s["qkv_copied"], 1)
                    act.wait_ge(s["qkv_copied"], t + 2)
                    act.activation(qk_sq[:, u], qk[:, u], ACT.Square).then_inc(s["qk_squared"], 1)
                    act.wait_ge(s["dn_turned"], t + (B + 1))
                    act.activation(dn_sq[:, u], ps[:, 2:4].rearrange("p b (n d) -> p (b n) d", d=DH), ACT.Square)
                    act.activation(pack[:, u, V_TOK], ps[:, 4], ACT.Copy)
                    act.activation(pack[:, u, Z_TOK], ps[:, 5], ACT.Copy).then_inc(s["dn_copied"], 1)

                def finish(u, t, n):
                    targets = [pack[:, u, Q_T].rearrange("p (h d) -> p h d", h=NH),
                               pack[:, u, K_T].rearrange("p (h d) -> p h d", h=NH), qt[:, u, 0:4], qt[:, u, 4:8], kt[:, u]]
                    for g, dst in enumerate(targets):
                        act.wait_ge(s["back_turned"], t * 5 + (g + 1))
                        act.activation(dst, ps[:, 6 + g % 2].rearrange("p (n d) -> p n d", n=4), ACT.Copy).then_inc(s["back_copied"], 1)
                    act.wait_ge(s["back_copied"], t * 5 + 7)
                    act.wait_ge(s["v_lo_done"], t + 2)
                    tok = bass.ds(t * P, P)
                    act.dma_start(io["q_s"][:, :, tok].rearrange("h p t -> p h t"), qt[:, u]).then_inc(stored[u], 16)
                    act.dma_start(io["k_s"][:, :, tok].rearrange("h p t -> p h t"), kt[:, u]).then_inc(stored[u], 16)
                    act.dma_start(io["v_s"][:, :, bass.ds(t, 1), :].rearrange("h p a d -> p h (a d)"),
                                  f32(v_split[:, u]).rearrange("p h s d -> p h (s d)")).then_inc(stored[u], 16)
                    act.dma_start(io["dn_s"][bass.ds(t, 1)].rearrange("a p n -> p (a n)"),
                                  pack[:, u].rearrange("p a n -> p (a n)")).then_inc(stored[u], 16)
                pipeline(act, turn, none, finish)
                for u in range(B):
                    act.wait_ge(stored[u], 64 * (NT // B + 1))
                BETA, G, X, E, L, R = range(6)
                act.activation(gates[:, BETA], ba[:, :, 0:2 * NH], ACT.Sigmoid).then_inc(s["gate_step"], 1)
                act.activation(alog[:, 1], alog[:, 0], ACT.Exp).then_inc(s["gate_step"], 1)
                act.wait_ge(s["x_done"], 1)
                act.activation(gates[:, E], gates[:, X], ACT.Abs).then_inc(s["gate_step"], 1)
                act.wait_ge(s["gate_step"], 3)
                act.activation(gates[:, L], gates[:, E], ACT.Exp, scale=-1.0).then_inc(s["gate_step"], 1)
                act.wait_ge(s["gate_step"], 4)
                act.activation(gates[:, E], gates[:, L], ACT.Ln, bias=one[:]).then_inc(s["gate_step"], 1)
                act.wait_ge(s["x_done"], 5)
                act.dma_start(io["bg_s"], gates[:, 0:2].rearrange("p a t n -> p (a t n)")).then_inc(stored[0], 16)
                act.wait_ge(stored[0], 64 * (NT // B + 1) + 16)

            @block.vector
            def _(dve):
                dve.sem_inc(s["v_lo_done"], 1)
                dve.sem_inc(s["dn_scaled"], 1)
                dve.wait_ge(s["rope_in"], 16)

                def turn(u, t, n):
                    dve.wait_ge(s["qkv_copied"], t + 2)
                    dve.tensor_tensor(v_split[:, u, :, 1], ps[:, 1, P:2 * P].rearrange("p (n d) -> p n d", d=HD),
                                      f32(v_split[:, u, :, 0]), ALU.subtract).then_inc(s["v_lo_done"], 1)
                    dve.wait_ge(s["qk_squared"], t + 1)
                    dve.tensor_reduce(rstd[:, u, 0], qk_sq[:, u], AX.X, ALU.add).then_inc(s["qk_summed"], 1)
                    dve.wait_ge(s["dn_copied"], t + 2)
                    dve.tensor_reduce(dn_rs[:, u, 0], dn_sq[:, u], AX.X, ALU.add).then_inc(s["dn_summed"], 1)

                def scale(u, t, n):
                    dve.wait_ge(s["qk_rms"], t + 1)
                    dve.tensor_tensor(qk[:, u], qk[:, u], along(rstd[:, u, 1], 2, HD), ALU.mult).then_inc(s["qk_scaled"], 1)
                    dve.wait_ge(s["dn_rs_done"], t + 1)
                    dve.tensor_tensor(dn_q[:, u].rearrange("p (h d) -> p h d", h=NH), ps[:, 2].rearrange("p (h d) -> p h d", h=NH),
                                      along(dn_rs[:, u, 1, 0:NH], 2, DH), ALU.mult)
                    dve.tensor_tensor(pack[:, u, K_TOK].rearrange("p (h d) -> p h d", h=NH), ps[:, 3].rearrange("p (h d) -> p h d", h=NH),
                                      along(dn_rs[:, u, 1, NH:2 * NH], 2, DH), ALU.mult).then_inc(s["dn_scaled"], 1)

                def finish(u, t, n):
                    dve.wait_ge(s["qk_gained"], t + 1)
                    dve.tensor_tensor(rot_a[:, u], qk_g[:, u], along(rope[:, bass.ds(t, 1), 0].rearrange("p a d -> p (a d)"), 1, NQK),
                                      ALU.mult).then_inc(s["rot_step"], 1)
                    dve.wait_ge(s["rot_b_done"], t + 1)
                    dve.wait_ge(s["rot_step"], t * 3 + 1)
                    dve.tensor_tensor(rot_a[:, u], rot_a[:, u], rot_b[:, u], ALU.add).then_inc(s["rot_step"], 1)
                    dve.wait_ge(s["rot_step"], t * 3 + 2)
                    k_rot = along(rot_a[:, u, NQH:NQK], 2, 2)
                    dve.tensor_copy(q_split[:, u, :, 0], rot_a[:, u, 0:NQH])
                    dve.tensor_copy(k_split[:, u, :, 0], k_rot).then_inc(s["rot_step"], 1)
                    dve.wait_ge(s["rot_step"], t * 3 + 3)
                    dve.tensor_tensor(q_split[:, u, :, 1], rot_a[:, u, 0:NQH], f32(q_split[:, u, :, 0]), ALU.subtract)
                    dve.tensor_tensor(k_split[:, u, :, 1], k_rot, f32(k_split[:, u, :, 0]), ALU.subtract).then_inc(s["split_done"], 1)
                pipeline(dve, turn, scale, finish)

            @block.gpsimd
            def _(pool):
                pool.memset(mhalf[:], -0.5)
                pool.memset(one[:], 1.0)
                pool.wait_ge(s["const_in"], 80)
                pool.wait_ge(s["rope_in"], 16)
                for h in range(1, NQH):
                    pool.tensor_copy(gain[:, h], gain[:, 0])
                pool.tensor_copy(gain[:, NQH + 1], gain[:, NQH]).then_inc(s["const_done"], 1)
                pool.wait_ge(s["const_done"], 1)
                pool.tensor_scalar(gain[:, 0:NQH], gain[:, 0:NQH], HD ** -0.5, None, ALU.mult).then_inc(s["const_done"], 1)
                pool.wait_ge(s["const_done"], 2)

                def turn(u, t, n):
                    hold(pool, s["passed"], s["qk_summed"], t + 1)
                    pool.tensor_scalar(rstd[:, u, 1], rstd[:, u, 0], 1.0 / HD, EPS, ALU.mult, ALU.add).then_inc(s["pool_step"], 1)
                    pool.wait_ge(s["pool_step"], t * 3 + 1)
                    pool.tensor_tensor(rstd[:, u, 1], rstd[:, u, 1], mhalf[:], ALU.pow).then_inc(s["qk_rms"], 1)
                    hold(pool, s["passed"], s["dn_summed"], t + 1)
                    pool.tensor_scalar(dn_rs[:, u, 1], dn_rs[:, u, 0], EPS, None, ALU.add).then_inc(s["pool_step"], 1)
                    pool.wait_ge(s["pool_step"], t * 3 + 2)
                    pool.tensor_tensor(dn_rs[:, u, 1], dn_rs[:, u, 1], mhalf[:, 0:2 * NH], ALU.pow).then_inc(s["pool_step"], 1)
                    hold(pool, s["passed"], s["pool_step"], t * 3 + 3)
                    pool.tensor_scalar(dn_rs[:, u, 1, 0:NH], dn_rs[:, u, 1, 0:NH], DH ** -0.5, None, ALU.mult).then_inc(s["dn_rs_done"], 1)

                def scale(u, t, n):
                    pool.wait_ge(s["qk_scaled"], t + 1)
                    pool.tensor_tensor(qk_g[:, u], qk[:, u], gain[:], ALU.mult).then_inc(s["qk_gained"], 1)
                    pool.wait_ge(s["qk_gained"], t + 1)
                    x = qk_g[:, u].rearrange("p n (h r j) -> p n h r j", h=2, r=2)
                    y = rot_b[:, u].rearrange("p n (h r j) -> p n h r j", h=2, r=2)
                    sin = rope[:, bass.ds(t, 1), 1].rearrange("p a (h r j) -> p (a h) r j", h=2, r=2)
                    for r in range(2):
                        op = pool.tensor_tensor(y[:, :, :, r], x[:, :, :, 1 - r], along(sin[:, :, r], 1, NQK), ALU.mult)
                    op.then_inc(s["rot_b_done"], 1)
                pipeline(pool, turn, scale, none)
                BETA, G, X, E, L, R = range(6)
                pool.wait_ge(s["qkv_copied"], NT + 1)
                pool.tensor_tensor(gates[:, X], ba[:, :, 2 * NH:4 * NH], along(dtb[:], 1, NT), ALU.add).then_inc(s["x_done"], 1)
                pool.wait_ge(s["x_done"], 1)
                pool.tensor_scalar(gates[:, R], gates[:, X], 0.0, None, ALU.max).then_inc(s["x_done"], 1)
                pool.wait_ge(s["gate_step"], 5)
                pool.wait_ge(s["x_done"], 2)
                pool.tensor_tensor(gates[:, R], gates[:, R], gates[:, E], ALU.add).then_inc(s["x_done"], 1)
                pool.tensor_scalar(alog[:, 1], alog[:, 1], -1.0, None, ALU.mult).then_inc(s["x_done"], 1)
                pool.wait_ge(s["x_done"], 4)
                pool.tensor_tensor(gates[:, G], gates[:, R], along(alog[:, 1], 1, NT), ALU.mult).then_inc(s["x_done"], 1)
    end_phase(nc, c)


def attend(nc, io):
    GROUPS = [(0, 0, T0 // P), (4, 0, T0 // P), (T0 // P, T0 // P, T1 // P)]
    NGR = 2 * len(GROUPS)
    group = [(u, *g) for u in range(2) for g in GROUPS]
    TILES = 4 * NGR
    first_key = [sum(g[3] for g in group[:n]) for n in range(NGR + 1)]
    KEYS = first_key[NGR]
    with ExitStack() as ctx:
        c = Core(nc, ctx, "attend")
        q = c.sb("q_head", [P, 2, TOK], F32R)
        k = c.sb("k_head", [P, 2, 2, TOK], F32R)
        v = c.sb("v_head", [P, 2, NT, P], F32R)
        probs = c.sb("probs", [P, 2, 4, T0])
        turned_hi = c.sb("probs_hi", [P, 2, 512], F32R)
        turned_lo = c.sb("probs_lo", [P, 2, 512], F32R)
        neg_max = c.sb("neg_max", [P, 2, 4])
        row_sum = c.sb("row_sum", [P, 3, 4])
        inv_sum = c.sb("inv_sum", [P, 2, 4])
        o_feat = c.sb("o_feat", [P, 2, 512])
        o_tok = c.sb("o_tok", [P, 2, 4, P])
        attn = c.sb("attn_tok", [P, NT, NQH, HD])
        ident = c.sb("ident_c", [P, P])
        score_ps = c.ps("score_ps", [P, 2, 2, 512])
        turn_ps = c.ps("turn_ps", [P, 2, 512])
        out_ps = c.ps("out_ps", [P, 2, 512])

        head_in, head_used = c.sems2("head_in"), c.sems2("head_used")
        names = ("ident_in", "scored", "maxed", "expd", "turned", "hi_done", "lo_done", "pv_done", "o_copied", "o_turned",
                 "inverted", "o_scaled", "o_added", "stored")
        s = {n: c.sem(n) for n in names}

        def schedule(score, keys, copy_out, turn_out, scale_out, lead=0):
            def do(f, *a):
                if f:
                    f(*a)

            def score_at(x):
                if x < TILES:
                    do(score, x // 4, x % 4)
            for x in range(lead):
                score_at(x)
            for j in range(4):
                score_at(j + lead)
            for n in range(NGR):
                per = group[n][3] // 4
                for j in range(4):
                    score_at(4 * n + 4 + j + lead)
                    for kt in range(j * per, (j + 1) * per):
                        do(keys, n, kt)
                    if n and j < 3:
                        do((copy_out, turn_out, scale_out)[j], n - 1)
            for f in (copy_out, turn_out, scale_out):
                do(f, NGR - 1)

        with nc.Block("attend") as block:
            @block.sync
            def _(sp):
                sp.dma_start(ident[:], io["ident"]).then_inc(s["ident_in"], 16)
                with sp.Fori(0, NKVH) as kv:
                    with sp.Fori(0, 2) as pair:
                        for u in range(2):
                            sp.wait_ge(head_used[u], kv * 2 + pair + 1)
                            sp.dma_start(f32(q[:, u]), io["q_s"][bass.ds(kv * 4 + pair * 2 + u, 1)].rearrange("a p t -> p (a t)")).then_inc(head_in[u], 16)
                            sp.dma_start(f32(k[:, u]), io["k_s"][bass.ds(kv * 2, 2)].rearrange("a p t -> p a t")).then_inc(head_in[u], 16)
                            sp.dma_start(f32(v[:, u]), io["v_s"][bass.ds(kv, 1)].rearrange("a p t d -> p (a t) d")).then_inc(head_in[u], 16)
                sp.wait_ge(s["o_added"], 4 * NGR + 2)
                sp.dma_start(io["at_s"], attn[:].rearrange("p t h d -> p (t h d)")).then_inc(s["stored"], 16)
                sp.wait_ge(s["stored"], 16)

            @block.tensor
            def _(pe):
                for u in range(2):
                    pe.sem_inc(head_used[u], 1)
                pe.sem_inc(s["pv_done"], 2)
                pe.wait_ge(s["ident_in"], 16)
                with pe.Fori(0, NQH // 2) as it:
                    def score(n, j):
                        u, q0, k0, nk = group[n]
                        if n % 3 == 0 and j == 0:
                            pe.wait_ge(head_in[u], it * 48 + 48)
                        pe.wait_ge(s["expd"], it * TILES + (4 * n + j + 1))
                        for b in range(nk // 4):
                            for half in range(2):
                                mm = pe.matmul(score_ps[:, j % 2, b], q[:, u, (q0 + j) * P:(q0 + j + 1) * P],
                                               k[:, u, half, (k0 + 4 * b) * P:(k0 + 4 * b + 4) * P], start=half == 0, stop=half == 1)
                        mm.then_inc(s["scored"], 1)

                    def product(n, kt):
                        u, q0, k0, nk = group[n]
                        m = first_key[n] + kt
                        pe.wait_ge(s["lo_done"], it * KEYS + (m + 3))
                        if kt == 0:
                            pe.wait_ge(s["o_scaled"], it * NGR + (n + 1))
                        for half, x in enumerate((turned_hi, turned_lo)):
                            mm = pe.matmul(out_ps[:, n % 2], v[:, u, k0 + kt], x[:, m % 2], start=kt == 0 and half == 0,
                                           stop=kt == nk - 1 and half == 1)
                        mm.then_inc(s["pv_done"], 1)
                        if n % 3 == 2 and kt == nk - 1:
                            pe.wait_ge(s["pv_done"], it * KEYS + (m + 3))
                            pe.sem_inc(head_used[u], 1)

                    def keys(n, kt):
                        u, q0, k0, nk = group[n]
                        m = first_key[n] + kt
                        if kt == 0:
                            pe.wait_ge(s["expd"], it * TILES + (4 * n + 6))
                        pe.wait_ge(s["lo_done"], it * KEYS + (m + 1))
                        for j in range(4):
                            tr = pe.transpose(turn_ps[:, m % 2, j * P:(j + 1) * P], probs[:, n % 2, j, kt * P:(kt + 1) * P], ident[:])
                        tr.then_inc(s["turned"], 1)
                        if kt:
                            product(n, kt - 1)
                        if kt == nk - 1:
                            product(n, kt)

                    def turn_out(n):
                        pe.wait_ge(s["o_copied"], it * NGR + (n + 1))
                        for j in range(4):
                            tr = pe.transpose(out_ps[:, n % 2, j * P:(j + 1) * P], o_feat[:, n % 2, j * P:(j + 1) * P], ident[:])
                        tr.then_inc(s["o_turned"], 1)
                    schedule(score, keys, None, turn_out, None, lead=1)

            @block.scalar
            def _(act):
                act.sem_inc(s["expd"], 2)
                with act.Fori(0, NQH // 2) as it:
                    def score(n, j):
                        u, q0, k0, nk = group[n]
                        act.wait_ge(s["maxed"], it * TILES + (4 * n + j + 1))
                        act.activation(probs[:, n % 2, j, 0:nk * P], score_ps[:, j % 2, 0:nk // 4].rearrange("p b t -> p (b t)"), ACT.Exp,
                                       bias=neg_max[:, n % 2, j:j + 1], accum_out=row_sum[:, n % 3, j:j + 1]).then_inc(s["expd"], 1)

                    def keys(n, kt):
                        m = first_key[n] + kt
                        act.wait_ge(s["turned"], it * KEYS + (m + 1))
                        act.wait_ge(s["pv_done"], it * KEYS + (m + 1))
                        act.activation(turned_hi[:, m % 2], turn_ps[:, m % 2], ACT.Copy).then_inc(s["hi_done"], 1)

                    def copy_out(n):
                        act.wait_ge(s["pv_done"], it * KEYS + (first_key[n + 1] + 2))
                        act.activation(o_feat[:, n % 2], out_ps[:, n % 2], ACT.Copy).then_inc(s["o_copied"], 1)
                    schedule(score, keys, copy_out, None, None)

            @block.vector
            def _(dve):
                dve.sem_inc(s["lo_done"], 2)
                dve.sem_inc(s["o_scaled"], 2)
                with dve.Fori(0, NQH // 2) as it:
                    def score(n, j):
                        u, q0, k0, nk = group[n]
                        dve.wait_ge(s["scored"], it * TILES + (4 * n + j + 1))
                        dve.tensor_reduce(neg_max[:, n % 2, j:j + 1], score_ps[:, j % 2, 0:nk // 4].rearrange("p b t -> p (b t)"),
                                          AX.X, ALU.max, negate=True).then_inc(s["maxed"], 1)

                    def keys(n, kt):
                        m = first_key[n] + kt
                        dve.wait_ge(s["hi_done"], it * KEYS + (m + 1))
                        dve.tensor_tensor(turned_lo[:, m % 2], turn_ps[:, m % 2], f32(turned_hi[:, m % 2]), ALU.subtract).then_inc(s["lo_done"], 1)

                    def scale_out(n):
                        dve.wait_ge(s["expd"], it * TILES + (4 * n + 6))
                        dve.reciprocal(inv_sum[:, n % 2], row_sum[:, n % 3]).then_inc(s["inverted"], 1)
                        dve.wait_ge(s["inverted"], it * NGR + (n + 1))
                        dve.wait_ge(s["o_turned"], it * NGR + (n + 1))
                        dve.wait_ge(s["o_added"], it * NGR + (n + 1))
                        dve.tensor_tensor(o_tok[:, n % 2], out_ps[:, n % 2].rearrange("p (j d) -> p j d", j=4),
                                          along(inv_sum[:, n % 2], 2, P), ALU.mult).then_inc(s["o_scaled"], 1)
                    schedule(score, keys, None, None, scale_out, lead=1)

            @block.gpsimd
            def _(pool):
                pool.sem_inc(s["o_added"], 2)
                with pool.Fori(0, NQH // 2) as it:
                    for n in range(NGR):
                        u, q0, k0, nk = group[n]
                        pool.wait_ge(s["o_scaled"], it * NGR + (n + 3))
                        pool.tensor_tensor(attn[:, q0:q0 + 4, bass.ds(it * 2 + u, 1), :].rearrange("p t a d -> p t (a d)"),
                                           o_tok[:, n % 2, :, 0:HD], o_tok[:, n % 2, :, HD:P], ALU.add).then_inc(s["o_added"], 1)
    end_phase(nc, c)


LEVELS = [2 ** n for n in range(1, 7)]
FWD, BWD = range(2)


def deltanet(nc, io):
    NM = 3 + len(LEVELS)
    INCL, STRICT, NEG_M1 = range(3)
    EGC, TAIL, TOTAL = range(3)
    K_TOK, V_TOK, K_T, Q_T = range(4)
    NL = len(LEVELS)
    with ExitStack() as ctx:
        c = Core(nc, ctx, "deltanet")
        masks = c.sb("masks", [P, 2, NM, P])
        ident = c.sb("ident_d", [P, P])
        ones = c.sb("ones_d", [P, P])
        bg = c.sb("bg", [P, 2, NT, 2 * NH])
        pack = c.sb("pack_in", [P, 2, 2, 4, DNW])
        out = c.sb("dn_out", [P, 2, 2, DNW])

        def work(name):
            return c.sb(name, [P, 2, NH, P])

        def work2(name):
            return c.sb(name, [P, 2, 2, NH, P])
        g_cut, decay, decay_m, decay_b = (work(n) for n in ("g_cut", "decay", "decay_m", "decay_b"))
        low_t, qk_d, r = (work2(n) for n in ("low_t", "qk_d", "r_inv"))
        t_inv, x_m, k_dec, z, v_new, state, q_state = (work(n) for n in ("t_inv", "x_m", "k_dec", "z_in", "v_new", "state", "q_state"))
        small = c.sb("beta_g", [P, 2, 2, 2, NH])
        exps = c.sb("g_exps", [P, 2, 2, 3, NH])
        neg_egc = c.sb("neg_egc", [P, 2, 2, NH])
        ps = c.ps("dn_ps", [P, 2, 4, 512])
        BA, BB, BC, BD = range(4)

        names = ("small_done", "cut_done", "sums_mm", "sums_exp", "gates_mm", "exp_done", "decay_m_done", "decay_b_done", "neg_done", "kk_mm", "qk_mm",
                 "low_done", "qk_done", "r_masked", "r_init", "r_turned", "turned", "t_init", "t_upd", "r_upd", "r_final", "x_mm", "x_done", "tx_mm",
                 "k_dec_done", "ks_mm", "qs_mm", "z_done", "q_state_done", "y_mm", "v_new_done", "o_mm", "ktv_mm", "state_scaled",
                 "state_ready", "out_done")
        s = {n: c.sems2(n) for n in names}
        pack_in, out_stored = ([c.sems2(f"{n}{d}_") for d in range(2)] for n in ("pack_in", "out_stored"))
        const_in, ones_done, passed = c.sem("const_in"), c.sem("ones_done"), c.sem("passed")

        def steps(eng, stages, before=None):
            def step(now, after):
                for stage, of_next in stages:
                    at = after if of_next else now
                    if at is not None:
                        q, p, i = at
                        base, n = SEQS[q]
                        for d in range(2):
                            stage(d, p, i + base, i + base if d == FWD else i * -1 + (base + n - 1), q)
            if before:
                before(0, 0)
            step(None, (0, 0, 0))
            for q, (base, n) in enumerate(SEQS):
                if before and q:
                    before(q, base)
                with eng.Fori(0, n // 2 - 1) as i:
                    for p in range(2):
                        step((q, p, i * 2 + p), (q, 1 - p, i * 2 + (p + 1)))
                step((q, 0, n - 2), (q, 1, n - 1))
                step((q, 1, n - 1), (q + 1, 0, 0) if q + 1 < len(SEQS) else None)

        with nc.Block("deltanet") as block:
            @block.sync
            def _(sp):
                sp.dma_start(masks[:].rearrange("p a m j -> p (a m j)"), io["masks"]).then_inc(const_in, 16)
                sp.dma_start(ident[:], io["ident"]).then_inc(const_in, 16)
                sp.dma_start(bg[:].rearrange("p a t n -> p (a t n)"), io["bg_s"]).then_inc(const_in, 16)

                def load(d, p, g, tile, q):
                    sp.wait_ge(s["ktv_mm"][d], g + 1)
                    sp.dma_start(pack[:, d, p].rearrange("p a n -> p (a n)"),
                                 io["dn_s"][bass.ds(tile, 1)].rearrange("a p n -> p (a n)")[:, 0:4 * DNW]).then_inc(pack_in[d][p], 16)

                def store(d, p, g, tile, q):
                    sp.wait_ge(s["out_done"][d], g + 1)
                    sp.dma_start(io["do_s"][d][bass.ds(tile, 1)].rearrange("a p n -> p (a n)"), out[:, d, p]).then_inc(out_stored[d][p], 16)
                steps(sp, [(load, True), (store, False)])
                for d in range(2):
                    for u in range(2):
                        sp.wait_ge(out_stored[d][u], 16 * (NT // 2 + 1))

            @block.tensor
            def _(pe):
                pe.wait_ge(const_in, 48)
                pe.wait_ge(ones_done, 1)
                for d in range(2):
                    pe.sem_inc(s["ktv_mm"][d], 2)

                def heads(dst, lhs, rhs):
                    for h in range(NH):
                        mm = pe.matmul(dst[:, h * P:(h + 1) * P], lhs(h), rhs(h), start=True, stop=True)
                    return mm

                def block_of(a, d, p, which):
                    return lambda h: a[:, d, p, which, h * P:(h + 1) * P]

                def gate_sums(d, p, g, tile, q):
                    pe.wait_ge(s["small_done"][d], g + 1)
                    if not isinstance(g, int) or g:
                        pe.wait_ge(s["q_state_done"][d], g)
                    for n, lhs in enumerate((masks[:, d, INCL], masks[:, d, STRICT], ones[:])):
                        mm = pe.matmul(ps[:, d, BD, n * NH:(n + 1) * NH], lhs, small[:, d, p, 1], start=True, stop=True)
                    mm.then_inc(s["sums_mm"][d], 1)

                def gates(d, p, g, tile, q):
                    pe.wait_ge(s["cut_done"][d], g + 1)
                    pe.wait_ge(s["sums_exp"][d], g + 1)
                    heads(ps[:, d, BD], lambda h: g_cut[:, d, h], lambda h: masks[:, d, INCL]).then_inc(s["gates_mm"][d], 1)

                def key_products(d, p, g, tile, q):
                    pe.wait_ge(pack_in[d][p], uses(p, g, 16))
                    pe.wait_ge(s["exp_done"][d], g + 1)
                    heads(ps[:, d, BD], block_of(pack, d, p, K_T), block_of(pack, d, p, K_T)).then_inc(s["kk_mm"][d], 1)

                def query_products(d, p, g, tile, q):
                    pe.wait_ge(s["low_done"][d], g + 1)
                    heads(ps[:, d, BD], block_of(pack, d, p, K_T), block_of(pack, d, p, Q_T)).then_inc(s["qk_mm"][d], 1)

                def turn(d, src):
                    for h in range(NH):
                        tr = pe.transpose(ps[:, d, BA, h * P:(h + 1) * P], src[:, h], ident[:])
                    return tr

                def turn_r(d, p, g, tile, q):
                    pe.wait_ge(s["r_init"][d], g + 1)
                    turn(d, r[:, d, p]).then_inc(s["r_turned"][d], 1)

                def grow_x(n):
                    def stage(d, p, g, tile, q):
                        if n == 0:
                            pe.wait_ge(s["t_init"][d], g + 1)
                            pe.wait_ge(s["state_ready"][d], g + (q + 1))
                        else:
                            pe.wait_ge(s["t_upd"][d], g * (NL - 1) + n)
                            turn(d, t_inv[:, d]).then_inc(s["turned"][d], 1)
                        heads(ps[:, d, BB], lambda h: low_t[:, d, p, h], lambda h: t_inv[:, d, h]).then_inc(s["x_mm"][d], 1)
                    return stage

                def grow_t(n):
                    def stage(d, p, g, tile, q):
                        pe.wait_ge(s["x_done"][d], g * NL + (n + 1))
                        if n:
                            pe.wait_ge(s["r_upd"][d], g * (NL - 1) + n)
                        if n < NL - 1:
                            heads(ps[:, d, BC], lambda h: r[:, d, p, h], lambda h: x_m[:, d, h]).then_inc(s["tx_mm"][d], 1)
                        else:
                            heads(ps[:, d, BC], lambda h: x_m[:, d, h], lambda h: r[:, d, p, h]).then_inc(s["tx_mm"][d], 1)
                    return stage

                def state_products(d, p, g, tile, q):
                    pe.wait_ge(s["qk_done"][d], NT if isinstance(g, int) and g == NT - 1 else g + 2)
                    pe.wait_ge(s["q_state_done"][d], g + 1)
                    pe.wait_ge(s["state_ready"][d], g + (q + 1))
                    heads(ps[:, d, BB], block_of(pack, d, p, K_T), lambda h: state[:, d, h]).then_inc(s["ks_mm"][d], 1)
                    heads(ps[:, d, BD], block_of(pack, d, p, Q_T), lambda h: state[:, d, h]).then_inc(s["qs_mm"][d], 1)

                def solve(d, p, g, tile, q):
                    pe.wait_ge(s["r_final"][d], g + 1)
                    pe.wait_ge(s["z_done"][d], g + 1)
                    heads(ps[:, d, BC], lambda h: r[:, d, p, h], lambda h: z[:, d, h]).then_inc(s["y_mm"][d], 1)

                def new_products(d, p, g, tile, q):
                    pe.wait_ge(s["v_new_done"][d], g + 1)
                    pe.wait_ge(s["k_dec_done"][d], g + 1)
                    heads(ps[:, d, BB], lambda h: k_dec[:, d, h], lambda h: v_new[:, d, h]).then_inc(s["ktv_mm"][d], 1)
                    pe.wait_ge(s["t_init"][d], NT if isinstance(g, int) and g == NT - 1 else g + 2)
                    heads(ps[:, d, BA], lambda h: qk_d[:, d, p, h], lambda h: v_new[:, d, h]).then_inc(s["o_mm"][d], 1)

                before_t = {0: gate_sums, 3: key_products, 4: query_products}
                after_t = {0: gates, NL - 1: turn_r}
                stages = []
                for n in range(NL):
                    stages.append((grow_x(n), False))
                    if n in before_t:
                        stages.append((before_t[n], True))
                    stages.append((grow_t(n), False))
                    if n in after_t:
                        stages.append((after_t[n], True))
                steps(pe, stages + [(f, False) for f in (state_products, solve, new_products)])

            @block.scalar
            def _(act):
                for d in range(2):
                    act.sem_inc(s["q_state_done"][d], 1)

                def exp_sums(d, p, g, tile, q):
                    act.wait_ge(s["sums_mm"][d], g + 1)
                    act.activation(exps[:, d, p].rearrange("p a h -> p (a h)"), ps[:, d, BD, 0:3 * NH], ACT.Exp).then_inc(s["sums_exp"][d], 1)

                def exp_decay(d, p, g, tile, q):
                    act.wait_ge(s["gates_mm"][d], g + 1)
                    act.activation(decay[:, d].rearrange("p h t -> p (h t)"), ps[:, d, BD], ACT.Exp).then_inc(s["exp_done"][d], 1)

                def first_t(d, p, g, tile, q):
                    act.wait_ge(s["r_turned"][d], g + 1)
                    act.activation(t_inv[:, d].rearrange("p h t -> p (h t)"), ps[:, d, BA], ACT.Copy).then_inc(s["t_init"][d], 1)

                def copy_turned(n):
                    def stage(d, p, g, tile, q):
                        act.wait_ge(s["turned"][d], g * (NL - 1) + n)
                        act.activation(r[:, d, p].rearrange("p h t -> p (h t)"), ps[:, d, BA], ACT.Copy).then_inc(s["r_upd"][d], 1)
                    return stage

                def scale_q_state(d, p, g, tile, q):
                    act.wait_ge(s["qs_mm"][d], g + 1)
                    for h in range(NH):
                        op = act.activation(q_state[:, d, h], ps[:, d, BD, h * P:(h + 1) * P], ACT.Copy, scale=exps[:, d, p, EGC, h:h + 1])
                    op.then_inc(s["q_state_done"][d], 1)
                steps(act, [(exp_sums, True), (exp_decay, True)] + [(copy_turned(n), False) for n in range(1, NL)] +
                      [(first_t, True), (scale_q_state, False)])

            @block.vector
            def _(dve):
                dve.wait_ge(const_in, 48)

                def take_gates(d, p, g, tile, q):
                    dve.tensor_copy(small[:, d, p], bg[:, :, bass.ds(tile, 1), d * NH:(d + 1) * NH].rearrange("p a t n -> p a (t n)")).then_inc(s["small_done"][d], 1)

                def decay_kk(d, p, g, tile, q):
                    dve.wait_ge(s["kk_mm"][d], g + 1)
                    dve.wait_ge(s["decay_b_done"][d], g + 1)
                    dve.tensor_tensor(low_t[:, d, p], ps[:, d, BD].rearrange("p (h t) -> p h t", h=NH), decay_b[:, d], ALU.mult).then_inc(s["low_done"][d], 1)

                def decay_qk(d, p, g, tile, q):
                    dve.wait_ge(s["qk_mm"][d], g + 1)
                    dve.tensor_tensor(qk_d[:, d, p], ps[:, d, BD].rearrange("p (h t) -> p h t", h=NH), decay_m[:, d], ALU.mult).then_inc(s["qk_done"][d], 1)

                def mask_x(n):
                    def stage(d, p, g, tile, q):
                        dve.wait_ge(s["x_mm"][d], g * NL + (n + 1))
                        dve.tensor_tensor(x_m[:, d], ps[:, d, BB].rearrange("p (h t) -> p h t", h=NH), along(masks[:, d, 3 + n], 1, NH),
                                          ALU.mult).then_inc(s["x_done"][d], 1)
                    return stage

                def subtract(n):
                    def stage(d, p, g, tile, q):
                        dve.wait_ge(s["tx_mm"][d], g * NL + (n + 1))
                        dst, done = (t_inv[:, d], "t_upd") if n < NL - 1 else (r[:, d, p], "r_final")
                        dve.tensor_tensor(dst, dst, ps[:, d, BC].rearrange("p (h t) -> p h t", h=NH), ALU.subtract).then_inc(s[done][d], 1)
                    return stage

                def make_z(d, p, g, tile, q):
                    dve.wait_ge(s["neg_done"][d], g + 1)
                    dve.wait_ge(s["ks_mm"][d], g + 1)
                    for h in range(NH):
                        op = dve.scalar_tensor_tensor(z[:, d, h], ps[:, d, BB, h * P:(h + 1) * P], neg_egc[:, d, p, h:h + 1],
                                                      pack[:, d, p, V_TOK, h * P:(h + 1) * P], ALU.mult, ALU.add)
                    op.then_inc(s["z_done"][d], 1)

                def make_v_new(d, p, g, tile, q):
                    dve.wait_ge(s["y_mm"][d], g + 1)
                    dve.tensor_tensor(v_new[:, d], ps[:, d, BC].rearrange("p (h t) -> p h t", h=NH), along(small[:, d, p, 0], 2, P),
                                      ALU.mult).then_inc(s["v_new_done"][d], 1)

                def update_state(d, p, g, tile, q):
                    dve.wait_ge(s["ktv_mm"][d], g + 3)
                    dve.wait_ge(s["state_scaled"][d], g + 1)
                    dve.tensor_tensor(state[:, d], state[:, d], ps[:, d, BB].rearrange("p (h t) -> p h t", h=NH), ALU.add).then_inc(s["state_ready"][d], 1)

                def outputs(d, p, g, tile, q):
                    dve.wait_ge(s["o_mm"][d], g + 1)
                    dve.wait_ge(s["q_state_done"][d], g + 2)
                    dve.wait_ge(out_stored[d][p], uses(p, g, 16))
                    dve.tensor_tensor(out[:, d, p], q_state[:, d].rearrange("p h t -> p (h t)"), ps[:, d, BA], ALU.add).then_inc(s["out_done"][d], 1)
                woven = {3: decay_kk, 4: decay_qk}
                stages = [(take_gates, True)]
                for n in range(NL):
                    stages.append((mask_x(n), False))
                    if n in woven:
                        stages.append((woven[n], True))
                    stages.append((subtract(n), False))
                steps(dve, stages + [(f, False) for f in (make_z, make_v_new, update_state, outputs)])

            @block.gpsimd
            def _(pool):
                pool.memset(ones[:], 1.0).then_inc(ones_done, 1)
                for d in range(2):
                    for u in range(2):
                        pool.sem_inc(out_stored[d][u], 16)
                pool.wait_ge(const_in, 48)

                def clear_state(q, base):
                    for d in range(2):
                        if q:
                            pool.wait_ge(s["state_ready"][d], base + q)
                        pool.memset(state[:, d], 0.0).then_inc(s["state_ready"][d], 1)

                def cut_gates(d, p, g, tile, q):
                    pool.wait_ge(s["small_done"][d], g + 1)
                    pool.tensor_tensor(g_cut[:, d], along(masks[:, d, STRICT], 1, NH), along(small[:, d, p, 1], 2, P), ALU.mult).then_inc(s["cut_done"][d], 1)

                def mask_decay(d, p, g, tile, q):
                    pool.wait_ge(s["exp_done"][d], g + 1)
                    pool.tensor_tensor(decay_m[:, d], decay[:, d], along(masks[:, d, INCL], 1, NH), ALU.mult).then_inc(s["decay_m_done"][d], 1)
                    pool.wait_ge(s["decay_m_done"][d], g + 1)
                    pool.tensor_tensor(decay_b[:, d], decay_m[:, d], along(small[:, d, p, 0], 2, P), ALU.mult).then_inc(s["decay_b_done"][d], 1)

                def first_r(d, p, g, tile, q):
                    pool.wait_ge(s["low_done"][d], g + 1)
                    pool.tensor_tensor(r[:, d, p], low_t[:, d, p], along(masks[:, d, NEG_M1], 1, NH), ALU.mult).then_inc(s["r_masked"][d], 1)
                    pool.wait_ge(s["r_masked"][d], g + 1)
                    pool.tensor_tensor(r[:, d, p], r[:, d, p], along(ident[:], 1, NH), ALU.add).then_inc(s["r_init"][d], 1)

                def decay_keys(d, p, g, tile, q):
                    pool.wait_ge(pack_in[d][p], uses(p, g, 16))
                    pool.wait_ge(s["ktv_mm"][d], g + 2)
                    pool.tensor_tensor(k_dec[:, d], pack[:, d, p, K_TOK].rearrange("p (h t) -> p h t", h=NH), along(exps[:, d, p, TAIL], 2, P),
                                       ALU.mult).then_inc(s["k_dec_done"][d], 1)
                    pool.tensor_scalar(neg_egc[:, d, p], exps[:, d, p, EGC], -1.0, None, ALU.mult).then_inc(s["neg_done"][d], 1)

                def scale_state(d, p, g, tile, q):
                    pool.wait_ge(s["qs_mm"][d], g + 1)
                    pool.tensor_tensor(state[:, d], state[:, d], along(exps[:, d, p, TOTAL], 2, P), ALU.mult).then_inc(s["state_scaled"][d], 1)
                steps(pool, [(cut_gates, True), (mask_decay, True), (decay_keys, False), (first_r, True), (scale_state, False)], clear_state)
    end_phase(nc, c)


def merge(nc, io):
    KB = NQH * HD // P
    with ExitStack() as ctx:
        c = Core(nc, ctx, "merge")
        x_hi = c.sb("branch_hi", [P, 2, KB, TOK], F32R)
        x_lo = c.sb("branch_lo", [P, 2, KB, TOK], F32R)
        dirs = c.sb("dn_dirs", [P, 2, 2, DNW])
        zt = c.sb("z_tok", [P, 2, DNW])
        at = c.sb("attn_in", [P, 2, DNW])
        osum = c.sb("dn_sum", [P, 2, NH, DH])
        osq = c.sb("dn_square", [P, 2, NH, DH])
        stat = c.sb("dn_stat", [P, 2, 3, NH])
        gain = c.sb("dn_gain", [P, DH])
        mhalf = c.sb("mhalf_e", [P, NH])
        ident = c.sb("ident_e", [P, P])
        raw = c.sb("wb_raw", [P, 2, 2, KB, P])
        whi = c.sb("wb_hi", [P, 2, 2, KB, P], F32R)
        wlo = c.sb("wb_lo", [P, 2, 2, KB, P], F32R)
        sig = c.sb("gate_sig", [P, 2, TOK])
        part = c.sb("branch_out", [P, 2, 2, TOK])
        turn_ps = c.ps("branch_turn", [P, 2, 512])
        acc = c.ps("branch_ps", [P, 2, NG, 512])

        tile_in, dirs_in = c.sems2("tile_in"), c.sems2("dirs_in")
        names = ("const_in", "mhalf_done", "passed", "summed", "squared", "reduced", "ms_done", "rstd_done", "normed", "gained",
                 "gated", "turned", "hi_done", "lo_done")
        s = {n: c.sem(n) for n in names}
        w_in, w_hi, w_ready, stored, added, sig_in, acc_done, acc_used = (c.sems2(n) for n in (
            "w_in", "w_hi", "w_ready", "stored", "added", "sig_in", "acc_done", "acc_used"))

        with nc.Block("merge") as block:
            @block.sync
            def _(sp):
                sp.dma_start(gain[:], io["dn_out_norm_g"][0].partition_broadcast(P)).then_inc(s["const_in"], 16)
                sp.dma_start(ident[:], io["ident"]).then_inc(s["const_in"], 16)

                def load_weights(u, i):
                    sp.wait_ge(w_ready[u], i + 1)
                    for b, w in enumerate(("w_attn_branch", "w_dn_branch")):
                        sp.dma_start(raw[:, u, b], io[w].rearrange("(k p) n -> p k n", p=P)[:, :, bass.ds(i * 256 + u * P, P)]).then_inc(w_in[u], 16)

                def load_gates(u, i):
                    for b in range(2):
                        sp.wait_ge(acc_used[b], i * 2 + (u + 1))
                        sp.dma_start(sig[:, b], io["gate_s"][bass.ds(i * 256 + (u * P + b * D), P), :]).then_inc(sig_in[b], 16)

                with sp.Fori(0, NT // 2) as i:
                    for u in range(2):
                        row = bass.ds(i * 2 + u, 1)
                        sp.wait_ge(s["summed"], i * 2 + (u + 1))
                        for d in range(2):
                            sp.dma_start(dirs[:, u, d], io["do_s"][d][row].rearrange("a p n -> p (a n)")).then_inc(dirs_in[u], 16)
                        sp.wait_ge(s["turned"], i * 2 + (u + 1))
                        sp.dma_start(zt[:, u], io["dn_s"][row].rearrange("a p n -> p (a n)")[:, 4 * DNW:5 * DNW]).then_inc(tile_in[u], 16)
                        sp.dma_start(at[:, u], io["at_s"][:, bass.ds(i * (2 * DNW) + u * DNW, DNW)]).then_inc(tile_in[u], 16)
                for u in range(2):
                    load_weights(u, 0)
                with sp.Fori(0, KD // 2 - 1) as i:
                    for u in range(2):
                        load_gates(u, i)
                        load_weights(u, i + 1)
                for u in range(2):
                    load_gates(u, KD // 2 - 1)

            @block.gpsimd
            def _(pool):
                for u in range(2):
                    pool.sem_inc(w_ready[u], 1)
                pool.memset(mhalf[:], -0.5).then_inc(s["mhalf_done"], 1)
                pool.wait_ge(s["mhalf_done"], 1)
                pool.wait_ge(s["const_in"], 32)

                def root(u, t):
                    hold(pool, s["passed"], s["reduced"], t + 1)
                    pool.tensor_scalar(stat[:, u, 1], stat[:, u, 0], 1.0 / DH, EPS, ALU.mult, ALU.add).then_inc(s["ms_done"], 1)
                    pool.wait_ge(s["ms_done"], t + 1)
                    pool.tensor_tensor(stat[:, u, 2], stat[:, u, 1], mhalf[:], ALU.pow).then_inc(s["rstd_done"], 1)
                    pool.wait_ge(tile_in[u], uses(u, t, 32))
                    zh = zt[:, u].rearrange("p (h d) -> p h d", h=NH)
                    pool.tensor_tensor(zh, zh, along(gain[:], 1, NH), ALU.mult).then_inc(s["gained"], 1)
                ahead(pool, NT, root, lambda u, t: None)

                def split(u, i):
                    pool.wait_ge(w_in[u], i * 32 + 32)
                    hold(pool, s["passed"], acc_done[u], i * 2 + 2)
                    pool.tensor_copy(whi[:, u], raw[:, u]).then_inc(w_hi[u], 1)
                    pool.wait_ge(w_hi[u], i + 1)
                    pool.tensor_tensor(wlo[:, u], raw[:, u], f32(whi[:, u]), ALU.subtract).then_inc(w_ready[u], 1)
                with pool.Fori(0, KD // 2) as i:
                    for u in range(2):
                        split(u, i)

            @block.tensor
            def _(pe):
                for u in range(2):
                    pe.sem_inc(acc_done[u], 2)
                pe.sem_inc(s["turned"], 2)
                pe.wait_ge(s["const_in"], 32)
                with pe.Fori(0, NT // 2) as i:
                    for u in range(2):
                        t = i * 2 + u
                        pe.wait_ge(s["lo_done"], t + 2)
                        pe.wait_ge(tile_in[u], i * 32 + 32)
                        for k in range(KB):
                            pe.transpose(turn_ps[:, 0, k * P:(k + 1) * P], at[:, u, k * P:(k + 1) * P], ident[:])
                        pe.wait_ge(s["gated"], t + 1)
                        for k in range(KB):
                            tr = pe.transpose(turn_ps[:, 1, k * P:(k + 1) * P], osum[:, u, k], ident[:])
                        tr.then_inc(s["turned"], 1)
                pe.wait_ge(s["lo_done"], NT + 2)
                with pe.Fori(0, KD // 2) as i:
                    for u in range(2):
                        pe.wait_ge(w_ready[u], i + 2)
                        for b in range(2):
                            pe.wait_ge(acc_used[b], i * 2 + (u + 1))
                            split_matmuls(pe, [acc[:, b, g] for g in range(NG)],
                                          lambda k, g: (whi[:, u, b, k], wlo[:, u, b, k], x_hi[:, b, k, g * 512:(g + 1) * 512],
                                                        x_lo[:, b, k, g * 512:(g + 1) * 512]), KB).then_inc(acc_done[u], 1)

            @block.scalar
            def _(act):
                for u in range(2):
                    act.sem_inc(stored[u], 16)

                def square(u, t):
                    act.wait_ge(s["summed"], t + 3)
                    act.activation(osq[:, u], osum[:, u], ACT.Square).then_inc(s["squared"], 1)

                def copy_hi(u, t):
                    act.wait_ge(s["turned"], t + 3)
                    act.activation(x_hi[:, :, :, bass.ds(t * P, P)].rearrange("p b k t -> p (b k) t"),
                                   turn_ps[:].rearrange("p b (k t) -> p (b k) t", k=KB), ACT.Copy).then_inc(s["hi_done"], 1)
                ahead(act, NT, square, copy_hi)
                with act.Fori(0, KD // 2) as i:
                    for u in range(2):
                        act.wait_ge(added[u], i + 1)
                        act.dma_start(io["m_s"][:, :, bass.ds(i * 2 + u, 1), :].rearrange("t p a j -> p t (a j)"),
                                      part[:, u, 0].rearrange("p (t j) -> p t j", j=P)).then_inc(stored[u], 16)
                for u in range(2):
                    act.wait_ge(stored[u], 16 * (KD // 2 + 1))

            @block.vector
            def _(dve):
                dve.sem_inc(s["lo_done"], 2)
                dve.sem_inc(s["summed"], 2)
                for b in range(2):
                    dve.sem_inc(acc_used[b], 1)

                def sum_directions(u, t):
                    dve.wait_ge(dirs_in[u], uses(u, t, 32))
                    dve.wait_ge(s["turned"], t + 1)
                    dve.tensor_tensor(osum[:, u].rearrange("p h d -> p (h d)"), dirs[:, u, 0], dirs[:, u, 1], ALU.add).then_inc(s["summed"], 1)
                    dve.wait_ge(s["squared"], t + 1)
                    dve.tensor_reduce(stat[:, u, 0], osq[:, u], AX.X, ALU.add).then_inc(s["reduced"], 1)

                def norm_and_gate(u, t):
                    dve.wait_ge(s["rstd_done"], t + 1)
                    dve.tensor_tensor(osum[:, u], osum[:, u], along(stat[:, u, 2], 2, DH), ALU.mult).then_inc(s["normed"], 1)
                    dve.wait_ge(s["gained"], t + 1)
                    dve.wait_ge(s["normed"], t + 1)
                    dve.tensor_tensor(osum[:, u].rearrange("p h d -> p (h d)"), osum[:, u].rearrange("p h d -> p (h d)"), zt[:, u],
                                      ALU.mult).then_inc(s["gated"], 1)

                def subtract_hi(u, t):
                    dve.wait_ge(s["hi_done"], t + 1)
                    tok = bass.ds(t * P, P)
                    dve.tensor_tensor(x_lo[:, :, :, tok].rearrange("p b k t -> p (b k) t"), turn_ps[:].rearrange("p b (k t) -> p (b k) t", k=KB),
                                      f32(x_hi[:, :, :, tok]).rearrange("p b k t -> p (b k) t"), ALU.subtract).then_inc(s["lo_done"], 1)
                ahead(dve, NT, sum_directions, subtract_hi, norm_and_gate)
                with dve.Fori(0, KD // 2) as i:
                    for u in range(2):
                        for b in range(2):
                            dve.wait_ge(acc_done[u], i * 2 + (b + 3))
                            dve.wait_ge(sig_in[b], i * 32 + (u * 16 + 16))
                            if b == 0:
                                dve.wait_ge(stored[u], i * 16 + 16)
                            dve.tensor_tensor(part[:, u, b], acc[:, b].rearrange("p g t -> p (g t)"), sig[:, b], ALU.mult).then_inc(acc_used[b], 1)
                        for b in range(2):
                            dve.wait_ge(acc_used[b], i * 2 + (u + 2))
                        dve.tensor_tensor(part[:, u, 0], part[:, u, 0], part[:, u, 1], ALU.add).then_inc(added[u], 1)
    end_phase(nc, c)


def mix_out(nc, io):
    with ExitStack() as ctx:
        c = Core(nc, ctx, "mix")
        whi = c.sb("wo_hi", [P, KD, D], F32R)
        wlo = c.sb("wo_lo", [P, KD, D], F32R)
        raw = c.sb("wo_raw", [P, KD, D])
        mt = c.sb("merged_in", [P, 2, KD, P])
        mhi = c.sb("merged_hi", [P, 2, KD, P], F32R)
        mlo = c.sb("merged_lo", [P, 2, KD, P], F32R)
        xt = c.sb("x_res", [P, 2, D])
        h = c.sb("h_tok", [P, 2, D])
        hn = c.sb("h_normed", [P, 2, D])
        junk = c.sb("squares_f", [P, 2, D])
        ht = c.sb("h_turned", [P, 2, KD, P])
        gains = c.sb("gains_f", [P, 2, D])
        stat = c.sb("stat_f", [P, 2, 2, 3])
        mhalf = c.sb("mhalf_f", [P, 1])
        ident = c.sb("ident_f", [P, P])
        acc = c.ps("mix_ps", [P, 2, 2, 512])
        turn_ps = c.ps("h_turn", [P, 2, 2, 512])
        tile_in, stored, raw_in = c.sems2("tile_in"), c.sems2("stored"), [c.sem(f"raw_in{k}") for k in range(KD)]
        names = ("const_in", "mhalf_done", "passed", "w_hi", "w_lo", "m_hi", "m_lo", "products", "post_sq", "post_ms", "post_rstd",
                 "post_normed", "h_done", "pre_sq", "pre_ms", "pre_rstd", "pre_normed", "turned", "copied")
        s = {n: c.sem(n) for n in names}

        with nc.Block("mix_out") as block:
            @block.sync
            def _(sp):
                sp.dma_start(gains[:, 0], io["ln1_post_g"][0].partition_broadcast(P)).then_inc(s["const_in"], 16)
                sp.dma_start(gains[:, 1], io["ln2_pre_g"][0].partition_broadcast(P)).then_inc(s["const_in"], 16)
                sp.dma_start(ident[:], io["ident"]).then_inc(s["const_in"], 16)

                def load(u, t):
                    sp.wait_ge(s["h_done"], t + 1)
                    sp.dma_start(mt[:, u].rearrange("p k t -> p (k t)"), io["m_s"][bass.ds(t, 1)].rearrange("a p k t -> p (a k t)")).then_inc(tile_in[u], 16)
                    sp.dma_start(xt[:, u], io["x"][bass.ds(t * P, P), :]).then_inc(tile_in[u], 16)
                load(0, 0)
                for k in range(KD):
                    sp.dma_start(raw[:, k], io["w_out"][k * P:(k + 1) * P, :]).then_inc(raw_in[k], 16)
                load(1, 1)
                with sp.Fori(1, NT // 2) as i:
                    for u in range(2):
                        load(u, i * 2 + u)

            @block.gpsimd
            def _(pool):
                pool.sem_inc(s["products"], 2)
                pool.memset(mhalf[:], -0.5).then_inc(s["mhalf_done"], 1)
                pool.wait_ge(s["mhalf_done"], 1)

                def split(u, t):
                    pool.wait_ge(tile_in[u], uses(u, t, 32))
                    hold(pool, s["passed"], s["products"], t + 1)
                    pool.tensor_copy(mhi[:, u], mt[:, u]).then_inc(s["m_hi"], 1)
                    pool.wait_ge(s["m_hi"], t + 1)
                    pool.tensor_tensor(mlo[:, u], mt[:, u], f32(mhi[:, u]), ALU.subtract).then_inc(s["m_lo"], 1)

                def norms(u, t):
                    for n, name in enumerate(("post", "pre")):
                        hold(pool, s["passed"], s[name + "_sq"], t + 1)
                        pool.tensor_scalar(stat[:, u, n, 1:2], stat[:, u, n, 0:1], 1.0 / D, EPS, ALU.mult, ALU.add).then_inc(s[name + "_ms"], 1)
                        pool.wait_ge(s[name + "_ms"], t + 1)
                        pool.tensor_tensor(stat[:, u, n, 2:3], stat[:, u, n, 1:2], mhalf[:], ALU.pow).then_inc(s[name + "_rstd"], 1)
                ahead(pool, NT, split, norms)

            @block.tensor
            def _(pe):
                pe.wait_ge(s["const_in"], 48)

                def products(u, t):
                    pe.wait_ge(s["m_lo"], t + 1)
                    pe.wait_ge(s["post_normed"], t + 1)
                    for k in range(KD):
                        if isinstance(t, int) and t == 0:
                            pe.wait_ge(s["w_lo"], k + 1)
                        for first, (x, w) in enumerate(((mhi, whi), (mhi, wlo), (mlo, whi))):
                            for b in range(2):
                                mm = pe.matmul(acc[:, u, b], x[:, u, k], w[:, k, b * 512:(b + 1) * 512], start=k == 0 and first == 0,
                                               stop=k == KD - 1 and first == 2)
                    mm.then_inc(s["products"], 1)

                def turn(u, t):
                    pe.wait_ge(s["pre_normed"], t + 1)
                    pe.wait_ge(s["copied"], t + 1)
                    for k in range(KD):
                        tr = pe.transpose(turn_ps[:, u, k // 4, (k % 4) * P:(k % 4 + 1) * P], hn[:, u, k * P:(k + 1) * P], ident[:])
                    tr.then_inc(s["turned"], 1)
                ahead(pe, NT, products, turn)

            @block.scalar
            def _(act):
                for u in range(2):
                    act.sem_inc(stored[u], 32)
                act.sem_inc(s["copied"], 2)
                for k in range(KD):
                    act.wait_ge(raw_in[k], 16)
                    act.activation(whi[:, k], raw[:, k], ACT.Copy).then_inc(s["w_hi"], 1)

                def squares(u, t):
                    act.wait_ge(s["products"], t + 3)
                    act.activation(junk[:, 0], acc[:, u].rearrange("p b n -> p (b n)"), ACT.Square, accum_out=stat[:, u, 0, 0:1]).then_inc(s["post_sq"], 1)
                    act.wait_ge(s["h_done"], t + 3)
                    act.activation(junk[:, 1], h[:, u], ACT.Square, accum_out=stat[:, u, 1, 0:1]).then_inc(s["pre_sq"], 1)

                def store(u, t):
                    act.wait_ge(s["turned"], t + 1)
                    act.wait_ge(stored[u], uses(u, t, 32))
                    act.activation(ht[:, u].rearrange("p k t -> p (k t)"), turn_ps[:, u].rearrange("p b n -> p (b n)"), ACT.Copy).then_inc(s["copied"], 1)
                    act.wait_ge(s["copied"], t + 3)
                    act.dma_start(io["ht_s"][:, :, bass.ds(t * P, P)].rearrange("k p t -> p k t"), ht[:, u]).then_inc(stored[u], 16)
                    act.dma_start(io["h_s"][bass.ds(t * P, P), :], h[:, u]).then_inc(stored[u], 16)
                ahead(act, NT, squares, store)
                for u in range(2):
                    act.wait_ge(stored[u], 32 * (NT // 2 + 1))

            @block.vector
            def _(dve):
                dve.sem_inc(s["h_done"], 2)
                dve.sem_inc(s["post_normed"], 2)
                for k in range(KD):
                    dve.wait_ge(s["w_hi"], k + 1)
                    dve.tensor_tensor(wlo[:, k], raw[:, k], f32(whi[:, k]), ALU.subtract).then_inc(s["w_lo"], 1)
                dve.wait_ge(s["const_in"], 48)
                with dve.Fori(0, NT // 2) as i:
                    for u in range(2):
                        t = i * 2 + u
                        dve.wait_ge(s["post_rstd"], t + 1)
                        dve.wait_ge(stored[u], i * 32 + 32)
                        dve.scalar_tensor_tensor(h[:, u], acc[:, u].rearrange("p b n -> p (b n)"), stat[:, u, 0, 2:3], gains[:, 0],
                                                 ALU.mult, ALU.mult).then_inc(s["post_normed"], 1)
                        dve.wait_ge(s["post_normed"], t + 3)
                        dve.tensor_tensor(h[:, u], h[:, u], xt[:, u], ALU.add).then_inc(s["h_done"], 1)
                        dve.wait_ge(s["pre_rstd"], t + 1)
                        dve.scalar_tensor_tensor(hn[:, u], h[:, u], stat[:, u, 1, 2:3], gains[:, 1], ALU.mult, ALU.mult).then_inc(s["pre_normed"], 1)
    end_phase(nc, c)


def ff_in(nc, io):
    with ExitStack() as ctx:
        c = Core(nc, ctx, "ff_in")
        x_hi = c.sb("ffx_hi", [P, KD, TOK], F32R)
        x_lo = c.sb("ffx_lo", [P, KD, TOK], F32R)
        xraw = c.sb("ffx_raw", [P, KD, TOK])
        raw = c.sb("w1_raw", [P, 2, KD, P])
        whi = c.sb("w1_hi", [P, 2, KD, P], F32R)
        wlo = c.sb("w1_lo", [P, 2, KD, P], F32R)
        stage = c.sb("ff_stage", [P, 2, TOK])
        acc = c.ps("ff_ps", [P, 2, NG, 512])
        names = ("passed", "x_hi", "x_lo")
        s = {n: c.sem(n) for n in names}
        x_in = [c.sem(f"x_in{k}") for k in range(KD)]
        w_in, w_hi, w_ready, acc_done, acc_used, squared, stored = (c.sems2(n) for n in (
            "w_in", "w_hi", "w_ready", "acc_done", "acc_used", "squared", "stored"))

        with nc.Block("ff_in") as block:
            @block.sync
            def _(sp):
                def load(u, i):
                    sp.wait_ge(w_ready[u], i + 1)
                    sp.dma_start(raw[:, u], io["w_ff_in"].rearrange("(k p) n -> p k n", p=P)[:, :, bass.ds(i * 256 + u * P, P)]).then_inc(w_in[u], 16)
                load(0, 0)
                for k in range(KD):
                    sp.dma_start(xraw[:, k], io["ht_s"][k]).then_inc(x_in[k], 16)
                load(1, 0)
                with sp.Fori(1, DFF // 256) as i:
                    for u in range(2):
                        load(u, i)

            @block.gpsimd
            def _(pool):
                for u in range(2):
                    pool.sem_inc(w_ready[u], 1)
                with pool.Fori(0, DFF // 256) as i:
                    for u in range(2):
                        pool.wait_ge(w_in[u], i * 16 + 16)
                        hold(pool, s["passed"], acc_done[u], i + 1)
                        pool.tensor_copy(whi[:, u], raw[:, u]).then_inc(w_hi[u], 1)
                        pool.wait_ge(w_hi[u], i + 1)
                        pool.tensor_tensor(wlo[:, u], raw[:, u], f32(whi[:, u]), ALU.subtract).then_inc(w_ready[u], 1)

            @block.tensor
            def _(pe):
                for u in range(2):
                    pe.sem_inc(acc_done[u], 1)

                def products(u, i, ahead_of_k=None):
                    pe.wait_ge(w_ready[u], i + 2)
                    pe.wait_ge(acc_used[u], i + 1)
                    split_matmuls(pe, [acc[:, u, g] for g in range(NG)],
                                  lambda k, g: (whi[:, u, k], wlo[:, u, k], x_hi[:, k, g * 512:(g + 1) * 512],
                                                x_lo[:, k, g * 512:(g + 1) * 512]), KD, ahead_of_k).then_inc(acc_done[u], 1)
                products(0, 0, lambda k: pe.wait_ge(s["x_lo"], k + 1))
                products(1, 0)
                with pe.Fori(1, DFF // 256) as i:
                    for u in range(2):
                        products(u, i)

            @block.scalar
            def _(act):
                for u in range(2):
                    act.sem_inc(acc_used[u], 1)
                    act.sem_inc(stored[u], 16)
                for k in range(KD):
                    act.wait_ge(x_in[k], 16)
                    act.activation(x_hi[:, k], xraw[:, k], ACT.Copy).then_inc(s["x_hi"], 1)
                with act.Fori(0, DFF // 256) as i:
                    for u in range(2):
                        act.wait_ge(acc_done[u], i + 2)
                        act.wait_ge(stored[u], i * 16 + 16)
                        act.activation(stage[:, u], acc[:, u].rearrange("p g t -> p (g t)"), ACT.Relu).then_inc(acc_used[u], 1)
                        act.wait_ge(acc_used[u], i + 2)
                        act.activation(stage[:, u], stage[:, u], ACT.Square).then_inc(squared[u], 1)
                        act.wait_ge(squared[u], i + 1)
                        act.dma_start(io["hid_s"][:, :, bass.ds(i * 2 + u, 1), :].rearrange("t p a j -> p t (a j)"),
                                      stage[:, u].rearrange("p (t j) -> p t j", j=P)).then_inc(stored[u], 16)
                for u in range(2):
                    act.wait_ge(stored[u], 16 * (DFF // 256 + 1))

            @block.vector
            def _(dve):
                for k in range(KD):
                    dve.wait_ge(s["x_hi"], k + 1)
                    dve.tensor_tensor(x_lo[:, k], xraw[:, k], f32(x_hi[:, k]), ALU.subtract).then_inc(s["x_lo"], 1)
    end_phase(nc, c)


def ff_out(nc, io):
    KF = DFF // P
    HC = D // 2
    UNIT = 1024
    RING = 4
    WK, HK = UNIT // HC, UNIT // P
    PARTS = KF // WK
    UNITS = PARTS + 4 * NT
    MID = PARTS // 2
    w_parts = [("w", n) for n in range(PARTS)]
    h_chunks = [("h", n) for n in range(4)]
    OPENING = (h_chunks[0:1] + w_parts[:MID] + h_chunks[1:3] + w_parts[MID:] + h_chunks[3:],
               w_parts[:MID] + h_chunks[0:1] + w_parts[MID:] + h_chunks[1:])
    ARRIVED = []
    for order in OPENING:
        sizes = [1 if kind == "w" else 2 for kind, _ in order]
        ARRIVED.append({item: sum(sizes[:n + 1]) for n, item in enumerate(order)})
    with ExitStack() as ctx:
        c = Core(nc, ctx, "ff_out")
        whi = c.sb("w2_hi", [P, KF, HC], F32R)
        wlo = c.sb("w2_lo", [P, KF, HC], F32R)
        raw = c.sb("ff_raw", [P, RING, UNIT])
        hhi = c.sb("hid_hi", [P, 2, KF // 2, P], F32R)
        hlo = c.sb("hid_lo", [P, 2, KF // 2, P], F32R)
        y0 = c.sb("y_half", [P, 2, HC])
        h = c.sb("h_in", [P, 2, D])
        out = c.sb("y_out", [P, D])
        gain = c.sb("gain_g", [P, D])
        stat = c.sb("stat_g", [P, 2, 4])
        mhalf = c.sb("mhalf_g", [P, 1])
        acc = c.ps("y_ps", [P, 4, 512])
        junk = c.ps("squares_g", [P, 2, HC])
        raw_in = [c.sem(f"raw_in{n}") for n in range(RING)]
        y_stored, h_in = c.sems2("y_stored"), c.sems2("h_in")
        names = ("const_in", "mhalf_done", "passed", "hi_done", "lo_done", "products", "w_passed", "squared", "sum_done", "ms_done",
                 "rstd_done", "acc_used", "normed", "added", "out_stored")
        s = {n: c.sem(n) for n in names}

        def opens(t):
            return isinstance(t, int) and t < 2

        def bank(u, t):
            return 2 + t if opens(t) else u

        def ring(eng, w_unit, h_unit, done):
            def opening(half):
                for kind, n in OPENING[half]:
                    first = half * UNITS + ARRIVED[half][kind, n] - (1 if kind == "w" else 2)
                    if kind == "w":
                        w_unit(half, n, first)
                        if half and n == PARTS - 1:
                            done(0, 1, NT - 1)
                    else:
                        for part in range(2):
                            h_unit(half, n % 2, n // 2, part, n, (first + part) % RING, first + part)

            def hidden(half, t):
                for kh in range(2):
                    for part in range(2):
                        r = 2 * kh + part
                        h_unit(half, t, kh, part, t * 2 + kh, r, t * 4 + (half * UNITS + PARTS + r))
            for half in range(2):
                opening(half)
                hidden(half, 2)
                done(half, 0, 0)
                done(half, 1, 1)
                with eng.Fori(1, NT // 2 - 1) as i:
                    for u in range(2):
                        hidden(half, i * 2 + (u + 1))
                        done(half, u, i * 2 + u)
                hidden(half, NT - 1)
                done(half, 0, NT - 2)
            done(1, 1, NT - 1)

        with nc.Block("ff_out") as block:
            @block.sync
            def _(sp):
                def load_part(half, n, unit):
                    sp.wait_ge(s["lo_done"], unit + 1)
                    sp.dma_start(raw[:, unit % RING].rearrange("p (k j) -> p k j", k=WK),
                                 io["w_ff_out"].rearrange("(k p) n -> p k n", p=P)[:, WK * n:WK * (n + 1), half * HC:(half + 1) * HC]).then_inc(raw_in[unit % RING], 16)

                def load_hidden(half, t, kh, part, chunk, r, unit):
                    sp.wait_ge(s["lo_done"], unit + 1)
                    k0 = kh * KF // 2 + part * HK
                    sp.dma_start(raw[:, r].rearrange("p (k j) -> p k j", j=P),
                                 io["hid_s"][bass.ds(t, 1)].rearrange("a p k j -> p (a k) j")[:, k0:k0 + HK, :]).then_inc(raw_in[r], 16)

                def load_rest(half, u, t):
                    if half:
                        if opens(t):
                            sp.wait_ge(y_stored[u], 16 * (NT // 2 + 1))
                        else:
                            sp.wait_ge(s["added"], t + 1)
                        sp.dma_start(y0[:, u], io["y0_s"][bass.ds(t * P, P), :]).then_inc(h_in[u], 16)
                        sp.dma_start(h[:, u], io["h_s"][bass.ds(t * P, P), :]).then_inc(h_in[u], 16)
                sp.dma_start(gain[:], io["ln2_post_g"][0].partition_broadcast(P)).then_inc(s["const_in"], 16)
                ring(sp, load_part, load_hidden, load_rest)

            @block.tensor
            def _(pe):
                pe.sem_inc(s["products"], 2)

                def products(u, t, kh, parts=None, passed=False):
                    for n in range(kh * MID, (kh + 1) * MID):
                        if parts:
                            pe.wait_ge(s["lo_done"], parts[n] + RING)
                        for w in range(WK * n, WK * (n + 1)):
                            k = w - kh * KF // 2
                            for first, (x, y) in enumerate(((hhi, whi), (hhi, wlo), (hlo, whi))):
                                mm = pe.matmul(acc[:, bank(u, t)], x[:, (t if opens(t) else kh), k], y[:, w], start=w == 0 and first == 0,
                                               stop=w == KF - 1 and first == 2)
                        if passed:
                            mm.then_inc(s["w_passed"], 1)
                    if passed:
                        pe.wait_ge(s["w_passed"], (kh + 1) * MID)
                        pe.sem_inc(s["products"], 1)
                    else:
                        mm.then_inc(s["products"], 1)

                def tile(half, u, t, used, passed=False):
                    pe.wait_ge(s["acc_used"], used)
                    for kh in range(2):
                        pe.wait_ge(s["lo_done"], t * 4 + (half * UNITS + PARTS + 2 * kh + 2 + RING))
                        products(u, t, kh, passed=passed)

                for half in range(2):
                    come = ARRIVED[half]
                    for kh in range(2):
                        for t in range(2):
                            pe.wait_ge(s["lo_done"], half * UNITS + come["h", 2 * kh + t] + RING)
                            products(t, t, kh, None if t else {n: half * UNITS + come["w", n] for n in range(PARTS)})
                    for u in range(2):
                        tile(half, u, 2 + u, half * NT + 2)
                    last = NT // 2 if half else NT // 2 - 1
                    with pe.Fori(2, last) as i:
                        for u in range(2):
                            tile(half, u, i * 2 + u, i * 2 + (u + half * NT + 1))
                    if not half:
                        for u in range(2):
                            tile(half, u, NT - 2 + u, NT - 1 + u, passed=u == 1)

            @block.scalar
            def _(act):
                for u in range(2):
                    act.sem_inc(y_stored[u], 16)
                act.sem_inc(s["out_stored"], 16)

                def part_hi(half, n, unit):
                    act.wait_ge(raw_in[unit % RING], (unit // RING + 1) * 16)
                    if half:
                        act.wait_ge(s["w_passed"], n + 1)
                    act.activation(whi[:, WK * n:WK * (n + 1)].rearrange("p k j -> p (k j)"), raw[:, unit % RING], ACT.Copy).then_inc(s["hi_done"], 1)

                def hidden_hi(half, t, kh, part, chunk, r, unit):
                    if isinstance(unit, int):
                        act.wait_ge(raw_in[r], (unit // RING + 1) * 16)
                    else:
                        act.wait_ge(raw_in[r], (t + (half * UNITS + PARTS) // RING + 1) * 16)
                    act.wait_ge(s["products"], chunk + (half * 2 * NT + 1))
                    act.activation(hhi[:, t if opens(t) else kh, part * HK:(part + 1) * HK].rearrange("p k j -> p (k j)"), raw[:, r],
                                   ACT.Copy).then_inc(s["hi_done"], 1)

                def keep(u, t):
                    act.wait_ge(s["products"], 6 if opens(t) else t * 2 + 4)
                    act.wait_ge(y_stored[u], uses(u, t, 16))
                    act.activation(y0[:, u], acc[:, bank(u, t)], ACT.Copy).then_inc(s["acc_used"], 1)
                    act.wait_ge(s["acc_used"], t + 3)
                    act.dma_start(io["y0_s"][bass.ds(t * P, P), :], y0[:, u]).then_inc(y_stored[u], 16)

                def finish(u, t):
                    act.wait_ge(s["products"], 2 * NT + 6 if opens(t) else t * 2 + (2 * NT + 4))
                    act.activation(junk[:, 0], acc[:, bank(u, t)], ACT.Square, accum_out=stat[:, u, 0:1])
                    act.wait_ge(h_in[u], uses(u, t, 32))
                    act.activation(junk[:, 1], y0[:, u], ACT.Square, accum_out=stat[:, u, 1:2]).then_inc(s["squared"], 1)
                    act.wait_ge(s["added"], t + 3)
                    act.dma_start(io["y"][bass.ds(t * P, P), :], out[:]).then_inc(s["out_stored"], 16)
                ring(act, part_hi, hidden_hi, lambda half, u, t: (finish if half else keep)(u, t))
                act.wait_ge(s["out_stored"], 16 * (NT + 1))

            @block.vector
            def _(dve):
                dve.sem_inc(s["lo_done"], RING)
                dve.sem_inc(s["acc_used"], 2)
                dve.sem_inc(s["added"], 2)
                dve.wait_ge(s["const_in"], 16)

                def part_lo(half, n, unit):
                    dve.wait_ge(s["hi_done"], unit + 1)
                    dve.tensor_tensor(wlo[:, WK * n:WK * (n + 1)].rearrange("p k j -> p (k j)"), raw[:, unit % RING],
                                      f32(whi[:, WK * n:WK * (n + 1)]).rearrange("p k j -> p (k j)"), ALU.subtract).then_inc(s["lo_done"], 1)

                def hidden_lo(half, t, kh, part, chunk, r, unit):
                    dve.wait_ge(s["hi_done"], unit + 1)
                    b, ks = (t if opens(t) else kh), slice(part * HK, (part + 1) * HK)
                    dve.tensor_tensor(hlo[:, b, ks].rearrange("p k j -> p (k j)"), raw[:, r],
                                      f32(hhi[:, b, ks]).rearrange("p k j -> p (k j)"), ALU.subtract).then_inc(s["lo_done"], 1)

                def finish(half, u, t):
                    if half:
                        dve.wait_ge(s["rstd_done"], t + 1)
                        dve.wait_ge(s["out_stored"], t * 16 + 16)
                        dve.scalar_tensor_tensor(out[:, 0:HC], y0[:, u], stat[:, u, 3:4], gain[:, 0:HC], ALU.mult, ALU.mult).then_inc(s["normed"], 1)
                        dve.scalar_tensor_tensor(out[:, HC:D], acc[:, bank(u, t)], stat[:, u, 3:4], gain[:, HC:D], ALU.mult, ALU.mult).then_inc(s["acc_used"], 1)
                        dve.wait_ge(s["normed"], t + 1)
                        dve.wait_ge(s["acc_used"], t + (NT + 3))
                        dve.tensor_tensor(out[:], out[:], h[:, u], ALU.add).then_inc(s["added"], 1)
                ring(dve, part_lo, hidden_lo, finish)

            @block.gpsimd
            def _(pool):
                pool.memset(mhalf[:], -0.5).then_inc(s["mhalf_done"], 1)
                pool.wait_ge(s["mhalf_done"], 1)
                with pool.Fori(0, NT // 2) as i:
                    for u in range(2):
                        t = i * 2 + u
                        pool.wait_ge(s["squared"], t + 1)
                        pool.tensor_tensor(stat[:, u, 2:3], stat[:, u, 0:1], stat[:, u, 1:2], ALU.add).then_inc(s["sum_done"], 1)
                        hold(pool, s["passed"], s["sum_done"], t + 1)
                        pool.tensor_scalar(stat[:, u, 2:3], stat[:, u, 2:3], 1.0 / D, EPS, ALU.mult, ALU.add).then_inc(s["ms_done"], 1)
                        pool.wait_ge(s["ms_done"], t + 1)
                        pool.tensor_tensor(stat[:, u, 3:4], stat[:, u, 2:3], mhalf[:], ALU.pow).then_inc(s["rstd_done"], 1)
    end_phase(nc, c)


PHASES = [project, prepare, attend, deltanet, merge, mix_out, ff_in, ff_out]
SCRATCH = {"qkv_s": (QKV_W, TOK), "dqkv_s": (3 * DNW, TOK), "z_s": (DNW, TOK), "ba_s": (4 * NH, TOK),
           "gate_s": (2 * D, TOK), "q_s": (NQH, P, TOK), "k_s": (2 * NKVH, P, TOK), "v_s": (NKVH, P, NT, P),
           "dn_s": (NT, P, 5 * DNW), "bg_s": (P, 2 * NT * 2 * NH), "at_s": (P, NT * NQH * HD), "do_s": (2, NT, P, DNW),
           "m_s": (NT, P, KD, P), "h_s": (TOK, D), "ht_s": (KD, P, TOK), "hid_s": (NT, P, DFF // P, P), "y0_s": (TOK, D // 2)}


def program(nc, io):
    for phase in PHASES:
        phase(nc, io)


def constants():
    tok = np.concatenate([np.arange(T0), np.arange(T1)]).astype(np.float32)
    inv = (np.float32(10000.0) ** (-np.arange(0, 32, 2, dtype=np.float32) / np.float32(32))).astype(np.float32)
    angles = [np.floor(tok / GRID_W)[:, None] * inv, (tok % GRID_W)[:, None] * inv]
    cos = np.concatenate([np.cos(a) for a in angles for _ in range(2)], 1)
    sin = np.concatenate([sign * np.sin(a) for a in angles for sign in (-1, 1)], 1)
    a, b = np.arange(P)[:, None], np.arange(P)[None]
    level = {w: (a // (2 * w) == b // (2 * w)) & (a % (2 * w) >= w) & (b % (2 * w) < w) for w in [1] + LEVELS}
    fwd = [a <= b, a > b, -1.0 * level[1].T] + [level[w] for w in LEVELS]
    bwd = [a >= b, a < b, -1.0 * level[1]] + [level[w].T for w in LEVELS]
    masks = np.stack([np.asarray(m, np.float32) for m in fwd + bwd], 1).reshape(P, -1)
    return {"masks": masks, "ident": np.eye(P, dtype=np.float32), "rope": np.concatenate([cos, sin], 1).astype(np.float32)}


def kernel(**inputs):
    import concourse.bacc as bacc
    from concourse.bass_utils import run_bass_kernel_spmd

    nc = bacc.Bacc("TRN2", target_bir_lowering=False, num_devices=1)
    arrays = {k: np.ascontiguousarray(v) for k, v in inputs.items() if k not in ("x_prompt", "x_sample", "dn_conv_w")}
    arrays = {k: v[0] if v.shape[0] == 1 and v.ndim == 3 else v for k, v in arrays.items()}
    arrays["x"] = np.concatenate([np.asarray(inputs["x_prompt"])[0], np.asarray(inputs["x_sample"])[0]])
    arrays["conv_w"] = np.ascontiguousarray(np.asarray(inputs["dn_conv_w"])[0].T)
    arrays |= constants()
    io = {k: nc.dram_tensor(f"in_{k}", v.shape, F32, kind="ExternalInput").ap() for k, v in arrays.items()}
    for k, shape in SCRATCH.items():
        io[k] = nc.dram_tensor(f"s_{k}", shape, F32, kind="Internal").ap()
    io["y"] = nc.dram_tensor("y", (TOK, D), F32, kind="ExternalOutput").ap()
    program(nc, io)
    r = run_bass_kernel_spmd(nc, [{f"in_{k}": v for k, v in arrays.items()}], core_ids=[0]).results[0]
    return r["y"][None, :T0], r["y"][None, T0:]
```

```python
from contextlib import ExitStack

import concourse.bass as bass
from concourse import mybir
import numpy as np

F32 = mybir.dt.float32
F32R = mybir.dt.float32r
ACT = mybir.ActivationFunctionType
ALU = mybir.AluOpType
AX = mybir.AxisListType

P = 128
D = 1024
KD = D // P
T0, T1 = 1024, 512
TOK = T0 + T1
NT = TOK // P
SEQS = [(0, T0 // P), (T0 // P, T1 // P)]
NG = TOK // 512
GRID_W = 64
NQH, NKVH, HD = 8, 2, 64
NH, DH = 4, 128
DNW = NH * DH
DFF = 4 * D
EPS = 1e-6
QKV_W = NQH * HD + 2 * NKVH * HD
DQKV_COL = QKV_W
DZ_COL = DQKV_COL + 3 * DNW
BA_COL = DZ_COL + DNW
GATE_COL = BA_COL + 4 * NH
PROJ_W = GATE_COL + 2 * D


def f32(ap):
    return ap.bitcast(F32)


def along(ap, axis, n):
    a = ap.unsqueeze(axis)
    shape = list(a.shape)
    shape[axis] = n
    return a.to_broadcast(shape)


def hold(pool, passed, sem, value):
    pool.wait_ge(sem, value)
    pool.sem_inc(passed, 1)


class Core:

    def __init__(self, nc, ctx, phase):
        self.nc, self.ctx, self.phase = nc, ctx, phase
        self.sems = []

    def sb(self, name, shape, dt=F32):
        return self.ctx.enter_context(self.nc.sbuf_tensor(name, shape, dt))

    def ps(self, name, shape):
        return self.ctx.enter_context(self.nc.psum_tensor(name, shape, F32))

    def sem(self, name):
        s = self.nc.alloc_semaphore(f"{self.phase}_{name}")
        self.sems.append(s)
        return s

    def sems2(self, name):
        return [self.sem(f"{name}{u}") for u in range(2)]


def end_phase(nc, core):
    nc.clear_and_free_semaphores(core.sems)
    nc.all_engine_barrier()


def split_matmuls(pe, out, pairs, n_k, ahead_of_k=None):
    for k in range(n_k):
        if ahead_of_k:
            ahead_of_k(k)
        for first, (wi, xi) in enumerate(((0, 2), (0, 3), (1, 2))):
            for g, bank in enumerate(out):
                ops = pairs(k, g)
                mm = pe.matmul(bank, ops[wi], ops[xi], start=(k == 0 and first == 0),
                               stop=(k == n_k - 1 and first == 2))
    return mm


def uses(u, t, per):
    return (t + (2 - u)) * (per // 2)


def ahead(eng, n, stage1, stage2, early=None, peel=1):
    def step(u, t):
        if early:
            early(u, t)
        if not isinstance(t, int) or t + 1 < n:
            stage1(1 - u, t + 1)
        stage2(u, t)
    stage1(0, 0)
    with eng.Fori(0, n // 2 - peel) as i:
        for u in range(2):
            step(u, i * 2 + u)
    for t in range(n - 2 * peel, n):
        step(t % 2, t)


def project(nc, io):
    with ExitStack() as ctx:
        c = Core(nc, ctx, "project")
        ht_hi = c.sb("ht_hi", [P, KD, TOK], F32R)
        ht_lo = c.sb("ht_lo", [P, KD, TOK], F32R)
        xt = c.sb("xt", [P, 2, D])
        gain = c.sb("ln1_gain", [P, D])
        ident = c.sb("ident_a", [P, P])
        stat = c.sb("x_stat", [P, 2, 3])
        mhalf = c.sb("mhalf_a", [P, 1])
        raw = c.sb("win_raw", [P, 2, KD, P])
        whi = c.sb("win_hi", [P, 2, KD, P], F32R)
        wlo = c.sb("win_lo", [P, 2, KD, P], F32R)
        stage = c.sb("proj_stage", [P, 2, TOK])
        conv = c.sb("conv_out", [P, TOK])
        taps = c.sb("conv_taps", [P, 2, 3])
        junk = c.sb("squares_a", [P, 2, D])
        xn = [stage[:, u, 0:D] for u in range(2)]
        acc = c.ps("proj_ps", [P, 2, NG, 512])
        xps = c.ps("xt_ps", [P, 2, 512])

        x_in = c.sems2("x_in")
        const_in, ss_done, ms_done, rstd_done = (c.sem(n) for n in ("const_in", "ss_done", "ms_done", "rstd_done"))
        xn_done, xt_done, hi_done, lo_done = (c.sem(n) for n in ("xn_done", "xt_done", "hi_done", "lo_done"))
        mhalf_done, passed = c.sem("mhalf_done"), c.sem("passed")
        w_in, w_hi, w_ready, acc_done = (c.sems2(n) for n in ("w_in", "w_hi", "w_ready", "acc_done"))
        acc_used, stage_done, stored = (c.sems2(n) for n in ("acc_used", "stage_done", "stored"))
        taps_in, conv_step, sig_done, silu_done = c.sems2("taps_in"), c.sem("conv_step"), c.sems2("sig_done"), c.sems2("silu_done")

        w_cols = io["w_in"].rearrange("(ko p) n -> p ko n", p=P)
        groups = [("plain", 0, QKV_W // 256, io["qkv_s"], 0),
                  ("conv", DQKV_COL, 3 * DNW // 256, io["dqkv_s"], 0),
                  ("silu", DZ_COL, DNW // 256, io["z_s"], 0),
                  ("gate", GATE_COL, 2 * D // 256, io["gate_s"], 0),
                  ("ba", BA_COL, 0.5, io["ba_s"], 0)]

        def tiles(eng, body, kinds=("plain", "conv", "silu", "ba", "gate"), start=0):
            done = [0, 0]
            for kind, col0, pairs, dst, row0 in groups:
                if kind not in kinds:
                    done = [d + (pairs if pairs != 0.5 else 1 - u) for u, d in enumerate(done)]
                    continue
                if pairs == 0.5:
                    body(0, done[0] + 1, kind, col0, dst, row0)
                    done[0] += 1
                    continue
                with eng.Fori(start if kind == "plain" else 0, pairs) as i:
                    for u in range(2):
                        body(u, i + done[u] + 1, kind, i * 256 + (col0 + u * P), dst, i * 256 + (row0 + u * P))
                done = [d + pairs for d in done]
            return done

        block = ctx.enter_context(nc.Block("project"))

        @block.sync
        def _(sp):
            sp.dma_start(gain[:], io["ln1_pre_g"][0].partition_broadcast(P)).then_inc(const_in, 16)
            sp.dma_start(ident[:], io["ident"]).then_inc(const_in, 16)
            def load(u, n, kind, col, dst, row):
                sp.wait_ge(w_ready[u], n)
                sp.dma_start(raw[:, u], w_cols[:, :, bass.ds(col, P)]).then_inc(w_in[u], 16)
                if kind == "conv":
                    sp.wait_ge(silu_done[u], n - QKV_W // 256)
                    sp.dma_start(taps[:, u, :], io["conv_w"][bass.ds(row, P), :]).then_inc(taps_in[u], 16)

            def load_x(u, t):
                tok = bass.ds(t * P, P)
                sp.wait_ge(xn_done, t + 1)
                sp.dma_start(xt[:, u, :], io["x"][tok, :]).then_inc(x_in[u], 16)
            for u in range(2):
                load_x(u, u)
            for u in range(2):
                load(u, 1, "plain", u * P, io["qkv_s"], 0)
            with sp.Fori(1, NT // 2) as i:
                for u in range(2):
                    load_x(u, i * 2 + u)
            tiles(sp, load, start=1)

        @block.gpsimd
        def _(pool):
            pool.memset(mhalf[:], -0.5).then_inc(mhalf_done, 1)
            for u in range(2):
                pool.sem_inc(w_ready[u], 1)
            pool.wait_ge(mhalf_done, 1)

            def root(u, t):
                hold(pool, passed, ss_done, t + 1)
                pool.tensor_scalar(stat[:, u, 1:2], stat[:, u, 0:1], 1.0 / D, EPS, ALU.mult, ALU.add).then_inc(ms_done, 1)
                pool.wait_ge(ms_done, t + 1)
                pool.tensor_tensor(stat[:, u, 2:3], stat[:, u, 1:2], mhalf[:], ALU.pow).then_inc(rstd_done, 1)

            def copy_hi(u, n):
                pool.wait_ge(w_in[u], n * 16)
                hold(pool, passed, acc_done[u], n)
                pool.tensor_copy(whi[:, u], raw[:, u]).then_inc(w_hi[u], 1)

            def subtract_hi(u, n):
                pool.wait_ge(w_hi[u], n)
                pool.tensor_tensor(wlo[:, u], raw[:, u], f32(whi[:, u]), ALU.subtract).then_inc(w_ready[u], 1)

            def split(u, n, kind, col, dst, row):
                copy_hi(u, n)
                subtract_hi(u, n)
            root(0, 0)
            for u, t, step in ((0, 1, copy_hi), (0, 2, subtract_hi), (1, 3, copy_hi), (1, 4, subtract_hi)):
                root(t % 2, t)
                step(u, 1)
            root(1, 5)
            with pool.Fori(3, NT // 2) as i:
                for u in range(2):
                    root(u, i * 2 + u)
            tiles(pool, split, start=1)

        @block.tensor
        def _(pe):
            for u in range(2):
                pe.sem_inc(acc_done[u], 1)
            pe.wait_ge(const_in, 32)

            def quarter(g, j):
                u, half = j // 2, j % 2
                pe.wait_ge(lo_done, 8 * g + 10)
                pe.wait_ge(w_ready[u], 2)
                tok = slice(g * 512, (g + 1) * 512)
                for k in range(4 * half, 4 * half + 4):
                    for first, (w, x) in enumerate(((whi, ht_hi), (whi, ht_lo), (wlo, ht_hi))):
                        mm = pe.matmul(acc[:, u, g], w[:, u, k], x[:, k, tok], start=k == 0 and first == 0, stop=k == KD - 1 and first == 2)
                if g == NG - 1 and half:
                    mm.then_inc(acc_done[u], 1)

            for u in range(2):
                pe.wait_ge(acc_used[u], 1)
            for t in range(NT):
                pe.wait_ge(xn_done, t + 3)
                for half in range(2):
                    pe.wait_ge(lo_done, t * 2 + (half + 1))
                    for k in range(4):
                        tr = pe.transpose(xps[:, half, k * P:(k + 1) * P], xn[t % 2][:, (4 * half + k) * P:(4 * half + k + 1) * P], ident[:])
                    tr.then_inc(xt_done, 1)
                if t >= 4:
                    quarter(t // 4 - 1, t % 4)
            for j in range(4):
                quarter(NG - 1, j)

            def products(u, n, kind, col, dst, row):
                pe.wait_ge(w_ready[u], n + 1)
                pe.wait_ge(acc_used[u], n)
                split_matmuls(pe, [acc[:, u, g] for g in range(NG)],
                              lambda k, g: (whi[:, u, k], wlo[:, u, k], ht_hi[:, k, g * 512:(g + 1) * 512],
                                            ht_lo[:, k, g * 512:(g + 1) * 512]), KD).then_inc(acc_done[u], 1)
            tiles(pe, products, start=1)

        @block.scalar
        def _(act):
            for u in range(2):
                act.sem_inc(acc_used[u], 1)
                act.sem_inc(stored[u], 16)

            def square(u, t):
                act.wait_ge(x_in[u], uses(u, t, 16))
                act.activation(junk[:, u], xt[:, u, :], ACT.Square, accum_out=stat[:, u, 0:1]).then_inc(ss_done, 1)

            def copy_hi(u, t):
                for half in range(2):
                    act.wait_ge(xt_done, t * 2 + (half + 1))
                    act.activation(ht_hi[:, 4 * half:4 * half + 4, bass.ds(t * P, P)],
                                   xps[:, half].rearrange("p (k t) -> p k t", k=4), ACT.Copy).then_inc(hi_done, 1)
            ahead(act, NT, square, copy_hi)

            def evacuate(u, n, kind, col, dst, row):
                act.wait_ge(acc_done[u], n + 1)
                act.wait_ge(stored[u], n * 16)
                banks = acc[:, u].rearrange("p g t -> p (g t)")
                if kind in ("plain", "ba", "conv", "silu"):
                    act.activation(stage[:, u], banks, ACT.Copy).then_inc(acc_used[u], 1)
                if kind == "gate":
                    act.activation(stage[:, u], banks, ACT.Sigmoid).then_inc(acc_used[u], 1)
                if kind == "conv":
                    act.wait_ge(conv_step, (n - QKV_W // 256 - 1) * 6 + 3 * u + 3)
                    act.activation(stage[:, u], conv[:], ACT.Sigmoid).then_inc(sig_done[u], 1)
                if kind == "silu":
                    act.wait_ge(acc_used[u], n + 1)
                    act.activation(conv[:], stage[:, u], ACT.Sigmoid).then_inc(sig_done[u], 1)
                if kind in ("conv", "silu"):
                    act.wait_ge(silu_done[u], n - QKV_W // 256 + 1)
                else:
                    act.wait_ge(acc_used[u], n + 1)
                if kind == "ba":
                    act.dma_start(dst, stage[0:4 * NH, u]).then_inc(stored[u], 16)
                else:
                    act.dma_start(dst[bass.ds(row, P), :], stage[:, u]).then_inc(stored[u], 16)
            done = tiles(act, evacuate)
            for u in range(2):
                act.wait_ge(stored[u], 16 * done[u] + 16)

        @block.vector
        def _(dve):
            for u in range(2):
                dve.sem_inc(silu_done[u], 1)
            dve.sem_inc(lo_done, 2)
            dve.sem_inc(xn_done, 2)
            dve.wait_ge(const_in, 32)

            def normalise(u, t):
                dve.wait_ge(rstd_done, t + 1)
                dve.scalar_tensor_tensor(xn[u], xt[:, u, :], stat[:, u, 2:3], gain[:], ALU.mult, ALU.mult).then_inc(xn_done, 1)

            def subtract_hi(u, t):
                for half in range(2):
                    dve.wait_ge(hi_done, t * 2 + (half + 1))
                    out = ht_lo[:, 4 * half:4 * half + 4, bass.ds(t * P, P)]
                    hi = f32(ht_hi[:, 4 * half:4 * half + 4, bass.ds(t * P, P)])
                    dve.tensor_tensor(out, xps[:, half].rearrange("p (k t) -> p k t", k=4), hi, ALU.subtract).then_inc(lo_done, 1)
            ahead(dve, NT, normalise, subtract_hi)

            def act_on(u, n, kind, col, dst, row):
                m = n - QKV_W // 256
                if kind == "conv":
                    x, s = stage[:, u], (m - 1) * 6 + 3 * u
                    dve.wait_ge(taps_in[u], m * 16)
                    dve.wait_ge(acc_used[u], n + 1)
                    dve.tensor_scalar(conv[:], x, taps[:, u, 1:2], None, ALU.mult).then_inc(conv_step, 1)
                    dve.wait_ge(conv_step, s + 1)
                    for a, b in ((0, T0), (T0, TOK)):
                        op = dve.scalar_tensor_tensor(conv[:, a + 1:b], x[:, a:b - 1], taps[:, u, 0:1],
                                                      conv[:, a + 1:b], ALU.mult, ALU.add)
                    op.then_inc(conv_step, 1)
                    dve.wait_ge(conv_step, s + 2)
                    for a, b in ((0, T0), (T0, TOK)):
                        op = dve.scalar_tensor_tensor(conv[:, a:b - 1], x[:, a + 1:b], taps[:, u, 2:3],
                                                      conv[:, a:b - 1], ALU.mult, ALU.add)
                    op.then_inc(conv_step, 1)
                if kind in ("conv", "silu"):
                    dve.wait_ge(sig_done[u], m)
                    dve.tensor_tensor(stage[:, u], stage[:, u], conv[:], ALU.mult).then_inc(silu_done[u], 1)
            tiles(dve, act_on, ("conv", "silu"))
    end_phase(nc, c)


def prepare(nc, io):
    B = 3
    NQK = NQH + NKVH
    QK = NQK * HD
    with ExitStack() as ctx:
        c = Core(nc, ctx, "prepare")
        feat = c.sb("feat", [P, B, 22, P])
        feat_ba = c.sb("feat_ba", [4 * NH, B, P])
        rope = c.sb("rope", [P, NT, 2, HD])
        qk = c.sb("qk_tok", [P, B, NQK, HD])
        qk_sq = c.sb("qk_sq", [P, B, NQK, HD])
        qk_g = c.sb("qk_gained", [P, B, NQK, HD])
        rot_a = c.sb("rot_a", [P, B, NQK, HD])
        rot_b = c.sb("rot_b", [P, B, NQK, HD])
        rstd = c.sb("qk_rstd", [P, B, 2, NQK])
        q_split = c.sb("q_split", [P, B, NQH, 2, HD], F32R)
        k_split = c.sb("k_split", [P, B, NKVH, 2, 2, HD], F32R)
        v_split = c.sb("v_split", [P, B, NKVH, 2, HD], F32R)
        dn_sq = c.sb("dn_sq", [P, B, 2 * NH, DH])
        dn_rs = c.sb("dn_rs", [P, B, 2, 2 * NH])
        dn_q = c.sb("dn_q", [P, B, DNW])
        pack = c.sb("dn_pack", [P, B, 5, DNW])
        qt = c.sb("q_t", [P, B, NQH, P])
        kt = c.sb("k_t", [P, B, 2 * NKVH, P])
        ba = c.sb("ba_tok", [P, NT, 4 * NH])
        gain = c.sb("qk_gain", [P, NQK, HD])
        ident = c.sb("ident_b", [P, P])
        mhalf = c.sb("mhalf_b", [P, NQK])
        gates = c.sb("dn_gates", [P, 6, NT, 2 * NH])
        alog = c.sb("alog_row", [P, 2, 2 * NH])
        dtb = c.sb("dtb_row", [P, 2 * NH])
        one = c.sb("one_b", [P, 1])
        ps = c.ps("prep_ps", [P, 8, 512])
        K_TOK, V_TOK, K_T, Q_T, Z_TOK = range(5)

        tile_in, stored = ([c.sem(f"{n}{u}") for u in range(B)] for n in ("tile_in", "p_stored"))
        names = ("const_in", "rope_in", "const_done", "qkv_turned", "dn_turned", "qkv_copied", "qk_squared", "dn_copied",
                 "v_lo_done", "qk_summed", "dn_summed", "qk_rms", "dn_rs_done", "qk_scaled", "dn_scaled", "qk_gained",
                 "rot_b_done", "rot_step", "split_done", "back_turned", "back_copied", "gate_step", "x_done", "bg_stored", "dn_squared", "qk_mean", "dn_mean")
        s = {n: c.sem(n) for n in names}

        def pipeline(eng, turn, scale, finish, late=None):
            def step(u, t, n):
                after = (u + 1) % B, t + 1, n + (u + 1) // B
                more = not isinstance(t, int) or t + 1 < NT
                scale(u, t, n)
                if more:
                    turn(*after)
                finish(u, t, n)
                if more and late:
                    late(*after)
            turn(0, 0, 0)
            if late:
                late(0, 0, 0)
            with eng.Fori(0, NT // B - 1) as i:
                for u in range(B):
                    step(u, i * B + u, i)
            for t in range(NT - B, NT):
                step(t % B, t, t // B)

        def none(u, t, n):
            pass

        with nc.Block("prepare") as block:
            @block.sync
            def _(sp):
                for dst, src in ((gain[:, 0], "attn_q_norm_g"), (gain[:, NQH], "attn_k_norm_g")):
                    sp.dma_start(dst, io[src][0].partition_broadcast(P)).then_inc(s["const_in"], 16)
                sp.dma_start(ident[:], io["ident"]).then_inc(s["const_in"], 16)
                sp.dma_start(alog[:, 0], io["dn_A_log"].rearrange("a b -> (a b)").partition_broadcast(P)).then_inc(s["const_in"], 16)
                sp.dma_start(dtb[:], io["dn_dt_bias"].rearrange("a b -> (a b)").partition_broadcast(P)).then_inc(s["const_in"], 16)
                sp.dma_start(rope[:], io["rope"].rearrange("(t p) (a d) -> p t a d", p=P, a=2)).then_inc(s["rope_in"], 16)

                def load(u, t, turned=None):
                    tok = bass.ds(t * P, P)
                    if turned is not None:
                        sp.wait_ge(s["dn_turned"], turned)
                    for a, b, src in ((0, 6, "qkv_s"), (6, 18, "dqkv_s"), (18, 22, "z_s")):
                        sp.dma_start(feat[:, u, a:b], io[src].rearrange("(n p) t -> p n t", p=P)[:, :, tok]).then_inc(tile_in[u], 16)
                    sp.dma_start(feat_ba[:, u], io["ba_s"][:, tok]).then_inc(tile_in[u], 16)

                def store(u, t):
                    tok, row = bass.ds(t * P, P), bass.ds(t, 1)
                    sp.wait_ge(s["back_copied"], t * 5 + 7)
                    sp.dma_start(io["q_s"][:, :, tok].rearrange("h p t -> p h t"), qt[:, u]).then_inc(stored[u], 16)
                    sp.dma_start(io["k_s"][:, :, tok].rearrange("h p t -> p h t"), kt[:, u]).then_inc(stored[u], 16)
                    sp.wait_ge(s["v_lo_done"], t + 2)
                    sp.dma_start(io["v_s"][:, :, row, :].rearrange("h p a d -> p h (a d)"),
                                 f32(v_split[:, u]).rearrange("p h s d -> p h (s d)")).then_inc(stored[u], 16)
                    sp.dma_start(io["dn_s"][row].rearrange("a p n -> p (a n)"),
                                 pack[:, u].rearrange("p a n -> p (a n)")).then_inc(stored[u], 16)
                for t in range(B):
                    load(t, t)
                with sp.Fori(0, NT // B - 1) as i:
                    for u in range(B):
                        load(u, i * B + (u + B), i * B + (u + B + 1))
                        store(u, i * B + u)
                for t in range(NT - B, NT):
                    store(t % B, t)
                for u in range(B):
                    sp.wait_ge(stored[u], 64 * (NT // B + 1))

            @block.tensor
            def _(pe):
                pe.sem_inc(s["dn_turned"], B)
                pe.wait_ge(s["const_in"], 80)

                def turn(u, t, n):
                    pe.wait_ge(tile_in[u], n * 64 + 64)
                    pe.wait_ge(s["qkv_copied"], t + 1)
                    pe.wait_ge(s["v_lo_done"], t + 1)
                    for k in range(6):
                        pe.transpose(ps[:, k // 4, (k % 4) * P:(k % 4 + 1) * P], feat[:, u, k], ident[:])
                    pe.transpose(ps[:, 1, 256:256 + 4 * NH], feat_ba[:, u], ident[0:4 * NH, 0:4 * NH]).then_inc(s["qkv_turned"], 1)
                    pe.wait_ge(s["dn_copied"], t + 1)
                    pe.wait_ge(s["dn_scaled"], t + 1)
                    for k in range(16):
                        tr = pe.transpose(ps[:, 2 + k // 4, (k % 4) * P:(k % 4 + 1) * P], feat[:, u, 6 + k], ident[:])
                    tr.then_inc(s["dn_turned"], 1)

                def finish(u, t, n):
                    sources = [dn_q[:, u].rearrange("p (h d) -> p h d", h=NH),
                               pack[:, u, K_TOK].rearrange("p (h d) -> p h d", h=NH),
                               f32(q_split[:, u, 0:4]).rearrange("p h s d -> p h (s d)"),
                               f32(q_split[:, u, 4:8]).rearrange("p h s d -> p h (s d)"),
                               f32(k_split[:, u]).rearrange("p h s r d -> p (h s) (r d)")]
                    pe.wait_ge(s["dn_scaled"], t + 2)
                    for g, src in enumerate(sources):
                        if g == 2:
                            pe.wait_ge(s["split_done"], t + 1)
                        pe.wait_ge(s["back_copied"], t * 5 + max(g + 1, 2))
                        for k in range(4):
                            tr = pe.transpose(ps[:, 6 + g % 2, k * P:(k + 1) * P], src[:, k], ident[:])
                        tr.then_inc(s["back_turned"], 1)
                pipeline(pe, turn, none, finish)

            @block.scalar
            def _(act):
                for u in range(B):
                    act.sem_inc(stored[u], 64)
                for n in ("qkv_copied", "dn_copied"):
                    act.sem_inc(s[n], 1)
                act.sem_inc(s["back_copied"], 2)

                def turn(u, t, n):
                    act.wait_ge(s["qkv_turned"], t + 1)
                    act.wait_ge(stored[u], n * 64 + 64)
                    act.activation(qk[:, u, 0:NQH], ps[:, 0].rearrange("p (n d) -> p n d", d=HD), ACT.Copy)
                    act.activation(qk[:, u, NQH:NQK], ps[:, 1, 0:P].rearrange("p (n d) -> p n d", d=HD), ACT.Copy)
                    act.activation(v_split[:, u, :, 0], ps[:, 1, P:2 * P].rearrange("p (n d) -> p n d", d=HD), ACT.Copy)
                    act.activation(ba[:, bass.ds(t, 1), :].rearrange("p a n -> p (a n)"), ps[:, 1, 256:256 + 4 * NH], ACT.Copy).then_inc(s["qkv_copied"], 1)
                    act.wait_ge(s["qkv_copied"], t + 2)
                    act.activation(qk_sq[:, u], qk[:, u], ACT.Square).then_inc(s["qk_squared"], 1)
                    act.wait_ge(s["dn_turned"], t + (B + 1))
                    act.activation(dn_sq[:, u], ps[:, 2:4].rearrange("p b (n d) -> p (b n) d", d=DH), ACT.Square).then_inc(s["dn_squared"], 1)
                    act.activation(pack[:, u, V_TOK], ps[:, 4], ACT.Copy)
                    act.activation(pack[:, u, Z_TOK], ps[:, 5], ACT.Copy).then_inc(s["dn_copied"], 1)

                def finish(u, t, n):
                    targets = [pack[:, u, Q_T].rearrange("p (h d) -> p h d", h=NH),
                               pack[:, u, K_T].rearrange("p (h d) -> p h d", h=NH), qt[:, u, 0:4], qt[:, u, 4:8], kt[:, u]]
                    for g, dst in enumerate(targets):
                        act.wait_ge(s["back_turned"], t * 5 + (g + 1))
                        act.activation(dst, ps[:, 6 + g % 2].rearrange("p (n d) -> p n d", n=4), ACT.Copy).then_inc(s["back_copied"], 1)
                pipeline(act, turn, none, finish)
                BETA, G, X, E, L, R = range(6)
                act.activation(gates[:, BETA], ba[:, :, 0:2 * NH], ACT.Sigmoid).then_inc(s["gate_step"], 1)
                act.activation(alog[:, 1], alog[:, 0], ACT.Exp).then_inc(s["gate_step"], 1)
                act.wait_ge(s["x_done"], 1)
                act.activation(gates[:, E], gates[:, X], ACT.Abs).then_inc(s["gate_step"], 1)
                act.wait_ge(s["gate_step"], 3)
                act.activation(gates[:, L], gates[:, E], ACT.Exp, scale=-1.0).then_inc(s["gate_step"], 1)
                act.wait_ge(s["gate_step"], 4)
                act.activation(gates[:, E], gates[:, L], ACT.Ln, bias=one[:]).then_inc(s["gate_step"], 1)
                act.wait_ge(s["x_done"], 5)
                act.dma_start(io["bg_s"], gates[:, 0:2].rearrange("p a t n -> p (a t n)")).then_inc(s["bg_stored"], 16)
                act.wait_ge(s["bg_stored"], 16)

            @block.vector
            def _(dve):
                dve.sem_inc(s["v_lo_done"], 1)
                dve.sem_inc(s["dn_scaled"], 1)
                dve.wait_ge(s["rope_in"], 16)

                def turn(u, t, n):
                    dve.wait_ge(s["qkv_copied"], t + 2)
                    dve.tensor_tensor(v_split[:, u, :, 1], ps[:, 1, P:2 * P].rearrange("p (n d) -> p n d", d=HD),
                                      f32(v_split[:, u, :, 0]), ALU.subtract).then_inc(s["v_lo_done"], 1)
                    dve.wait_ge(s["qk_squared"], t + 1)
                    dve.tensor_reduce(rstd[:, u, 0], qk_sq[:, u], AX.X, ALU.add).then_inc(s["qk_summed"], 1)
                    dve.wait_ge(s["qk_summed"], t + 1)
                    dve.tensor_scalar(rstd[:, u, 0], rstd[:, u, 0], 1.0 / HD, EPS, ALU.mult, ALU.add).then_inc(s["qk_mean"], 1)

                def sum_dn(u, t, n):
                    dve.wait_ge(s["dn_squared"], t + 1)
                    dve.tensor_reduce(dn_rs[:, u, 0], dn_sq[:, u], AX.X, ALU.add).then_inc(s["dn_summed"], 1)
                    dve.wait_ge(s["dn_summed"], t + 1)
                    dve.tensor_scalar(dn_rs[:, u, 0, 0:NH], dn_rs[:, u, 0, 0:NH], DH, DH * EPS, ALU.mult, ALU.add)
                    dve.tensor_scalar(dn_rs[:, u, 0, NH:2 * NH], dn_rs[:, u, 0, NH:2 * NH], EPS, None, ALU.add).then_inc(s["dn_mean"], 1)

                def scale(u, t, n):
                    dve.wait_ge(s["qk_rms"], t + 1)
                    dve.tensor_tensor(qk[:, u], qk[:, u], along(rstd[:, u, 1], 2, HD), ALU.mult).then_inc(s["qk_scaled"], 1)
                    dve.wait_ge(s["dn_rs_done"], t + 1)
                    dve.tensor_tensor(dn_q[:, u].rearrange("p (h d) -> p h d", h=NH), ps[:, 2].rearrange("p (h d) -> p h d", h=NH),
                                      along(dn_rs[:, u, 1, 0:NH], 2, DH), ALU.mult)
                    dve.tensor_tensor(pack[:, u, K_TOK].rearrange("p (h d) -> p h d", h=NH), ps[:, 3].rearrange("p (h d) -> p h d", h=NH),
                                      along(dn_rs[:, u, 1, NH:2 * NH], 2, DH), ALU.mult).then_inc(s["dn_scaled"], 1)

                def finish(u, t, n):
                    dve.wait_ge(s["qk_gained"], t + 1)
                    dve.tensor_tensor(rot_a[:, u], qk_g[:, u], along(rope[:, bass.ds(t, 1), 0].rearrange("p a d -> p (a d)"), 1, NQK),
                                      ALU.mult).then_inc(s["rot_step"], 1)
                    dve.wait_ge(s["rot_b_done"], t + 1)
                    dve.wait_ge(s["rot_step"], t * 3 + 1)
                    dve.tensor_tensor(rot_a[:, u], rot_a[:, u], rot_b[:, u], ALU.add).then_inc(s["rot_step"], 1)
                    dve.wait_ge(s["rot_step"], t * 3 + 2)
                    k_rot = along(rot_a[:, u, NQH:NQK], 2, 2)
                    dve.tensor_copy(q_split[:, u, :, 0], rot_a[:, u, 0:NQH])
                    dve.tensor_copy(k_split[:, u, :, 0], k_rot).then_inc(s["rot_step"], 1)
                    dve.wait_ge(s["rot_step"], t * 3 + 3)
                    dve.tensor_tensor(q_split[:, u, :, 1], rot_a[:, u, 0:NQH], f32(q_split[:, u, :, 0]), ALU.subtract)
                    dve.tensor_tensor(k_split[:, u, :, 1], k_rot, f32(k_split[:, u, :, 0]), ALU.subtract).then_inc(s["split_done"], 1)
                pipeline(dve, turn, scale, finish, sum_dn)

            @block.gpsimd
            def _(pool):
                pool.memset(mhalf[:], -0.5)
                pool.memset(one[:], 1.0)
                pool.wait_ge(s["const_in"], 80)
                pool.wait_ge(s["rope_in"], 16)
                for h in range(1, NQH):
                    pool.tensor_copy(gain[:, h], gain[:, 0])
                pool.tensor_copy(gain[:, NQH + 1], gain[:, NQH]).then_inc(s["const_done"], 1)
                pool.wait_ge(s["const_done"], 1)
                pool.tensor_scalar(gain[:, 0:NQH], gain[:, 0:NQH], HD ** -0.5, None, ALU.mult).then_inc(s["const_done"], 1)
                pool.wait_ge(s["const_done"], 2)

                def turn(u, t, n):
                    pool.wait_ge(s["qk_mean"], t + 1)
                    pool.tensor_tensor(rstd[:, u, 1], rstd[:, u, 0], mhalf[:], ALU.pow).then_inc(s["qk_rms"], 1)
                    pool.wait_ge(s["dn_mean"], t + 1)
                    pool.tensor_tensor(dn_rs[:, u, 1], dn_rs[:, u, 0], mhalf[:, 0:2 * NH], ALU.pow).then_inc(s["dn_rs_done"], 1)

                def scale(u, t, n):
                    pool.wait_ge(s["qk_scaled"], t + 1)
                    pool.tensor_tensor(qk_g[:, u], qk[:, u], gain[:], ALU.mult).then_inc(s["qk_gained"], 1)
                    pool.wait_ge(s["qk_gained"], t + 1)
                    x = qk_g[:, u].rearrange("p n (h r j) -> p n h r j", h=2, r=2)
                    y = rot_b[:, u].rearrange("p n (h r j) -> p n h r j", h=2, r=2)
                    sin = rope[:, bass.ds(t, 1), 1].rearrange("p a (h r j) -> p (a h) r j", h=2, r=2)
                    for r in range(2):
                        op = pool.tensor_tensor(y[:, :, :, r], x[:, :, :, 1 - r], along(sin[:, :, r], 1, NQK), ALU.mult)
                    op.then_inc(s["rot_b_done"], 1)
                pipeline(pool, turn, scale, none)
                BETA, G, X, E, L, R = range(6)
                pool.wait_ge(s["qkv_copied"], NT + 1)
                pool.tensor_tensor(gates[:, X], ba[:, :, 2 * NH:4 * NH], along(dtb[:], 1, NT), ALU.add).then_inc(s["x_done"], 1)
                pool.wait_ge(s["x_done"], 1)
                pool.tensor_scalar(gates[:, R], gates[:, X], 0.0, None, ALU.max).then_inc(s["x_done"], 1)
                pool.wait_ge(s["gate_step"], 5)
                pool.wait_ge(s["x_done"], 2)
                pool.tensor_tensor(gates[:, R], gates[:, R], gates[:, E], ALU.add).then_inc(s["x_done"], 1)
                pool.tensor_scalar(alog[:, 1], alog[:, 1], -1.0, None, ALU.mult).then_inc(s["x_done"], 1)
                pool.wait_ge(s["x_done"], 4)
                pool.tensor_tensor(gates[:, G], gates[:, R], along(alog[:, 1], 1, NT), ALU.mult).then_inc(s["x_done"], 1)
    end_phase(nc, c)


def attend(nc, io):
    GROUPS = [(0, 0, T0 // P), (4, 0, T0 // P), (T0 // P, T0 // P, T1 // P)]
    NGR = 2 * len(GROUPS)
    group = [(u, *g) for u in range(2) for g in GROUPS]
    TILES = 4 * NGR
    first_key = [sum(g[3] for g in group[:n]) for n in range(NGR + 1)]
    KEYS = first_key[NGR]
    key_tile = [(n, kt) for n in range(NGR) for kt in range(group[n][3])]
    TURNS = NQH // 2
    LAG = 2
    with ExitStack() as ctx:
        c = Core(nc, ctx, "attend")
        q = c.sb("q_head", [P, 2, TOK], F32R)
        k = c.sb("k_head", [P, 2, 2, TOK], F32R)
        v = c.sb("v_head", [P, 2, NT, P], F32R)
        probs = c.sb("probs", [P, 2, 4, T0])
        turned_hi = c.sb("probs_hi", [P, 4, 512], F32R)
        turned_lo = c.sb("probs_lo", [P, 4, 512], F32R)
        neg_max = c.sb("neg_max", [P, 2, 4])
        row_sum = c.sb("row_sum", [P, NGR, 4])
        inv_sum = c.sb("inv_sum", [P, 2, 4])
        o_feat = c.sb("o_feat", [P, 2, 512])
        o_tok = c.sb("o_tok", [P, 2, 4, P])
        attn = c.sb("attn_tok", [P, NT, NQH, HD])
        ident = c.sb("ident_c", [P, P])
        score_ps = c.ps("score_ps", [P, 2, 2, 512])
        turn_ps = c.ps("turn_ps", [P, 2, 512])
        out_ps = c.ps("out_ps", [P, 2, 512])

        head_in, v_in, head_used = c.sems2("head_in"), c.sems2("v_in"), c.sems2("head_used")
        names = ("ident_in", "scored", "maxed", "expd", "turned", "hi_done", "lo_done", "pv_done", "o_copied", "o_turned",
                 "inverted", "o_scaled", "o_added", "stored")
        s = {n: c.sem(n) for n in names}

        def schedule(eng, score, keys, copy_out, turn_out, scale_out, lead=0, flush=None):
            outs = (copy_out, turn_out, scale_out)

            def turn(it, first, last):
                for n in range(NGR):
                    per = group[n][3] // 4
                    for j in range(4):
                        x = 4 * n + 4 + j + lead
                        for i in range(per):
                            if keys:
                                keys(it, first_key[n] + j * per + i)
                            if i == 0 and score and not (last and x >= TILES):
                                score(it, x)
                        if j and outs[j - 1] and not (first and n == 0):
                            outs[j - 1](it, n - 1)
            if score:
                for x in range(4 + lead):
                    score(0, x)
            turn(0, True, False)
            with eng.Fori(1, TURNS - 1) as it:
                turn(it, False, False)
            turn(TURNS - 1, False, True)
            if flush:
                flush()
            for f in outs:
                if f:
                    f(TURNS - 1, NGR - 1)

        with nc.Block("attend") as block:
            @block.sync
            def _(sp):
                sp.dma_start(ident[:], io["ident"]).then_inc(s["ident_in"], 16)
                with sp.Fori(0, NKVH) as kv:
                    with sp.Fori(0, 2) as pair:
                        for u in range(2):
                            sp.wait_ge(head_used[u], kv * 2 + pair + 1)
                            sp.dma_start(f32(q[:, u]), io["q_s"][bass.ds(kv * 4 + pair * 2 + u, 1)].rearrange("a p t -> p (a t)")).then_inc(head_in[u], 16)
                            sp.dma_start(f32(k[:, u]), io["k_s"][bass.ds(kv * 2, 2)].rearrange("a p t -> p a t")).then_inc(head_in[u], 16)
                            sp.dma_start(f32(v[:, u]), io["v_s"][bass.ds(kv, 1)].rearrange("a p t d -> p (a t) d")).then_inc(v_in[u], 16)

            @block.tensor
            def _(pe):
                for u in range(2):
                    pe.sem_inc(head_used[u], 1)
                pe.sem_inc(s["pv_done"], 4)
                pe.wait_ge(s["ident_in"], 16)

                def score(it, x):
                    j = x % 4
                    u, q0, k0, nk = group[x // 4 % NGR]
                    if x % 12 == 0:
                        pe.wait_ge(head_in[u], it * 32 + (64 if x >= TILES else 32))
                    pe.wait_ge(s["expd"], it * TILES + (x + 1))
                    for b in range(nk // 4):
                        for half in range(2):
                            mm = pe.matmul(score_ps[:, j % 2, b], q[:, u, (q0 + j) * P:(q0 + j + 1) * P],
                                           k[:, u, half, (k0 + 4 * b) * P:(k0 + 4 * b + 4) * P], start=half == 0, stop=half == 1)
                    mm.then_inc(s["scored"], 1)

                def product(it, m):
                    n, kt = key_tile[m]
                    u, q0, k0, nk = group[n]
                    pe.wait_ge(s["lo_done"], it * KEYS + (m + 3))
                    if m >= 0 and kt == 0 and n % 3 == 0:
                        pe.wait_ge(v_in[u], it * 16 + 16)
                    if m >= 0 and kt == 0:
                        pe.wait_ge(s["o_scaled"], it * NGR + (n + 1))
                    for half, x in enumerate((turned_hi, turned_lo)):
                        mm = pe.matmul(out_ps[:, n % 2], v[:, u, k0 + kt], x[:, m % 4], start=kt == 0 and half == 0,
                                       stop=kt == nk - 1 and half == 1)
                    mm.then_inc(s["pv_done"], 1)
                    if n % 3 == 2 and kt == nk - 1:
                        pe.wait_ge(s["pv_done"], it * KEYS + (m + 5))
                        pe.sem_inc(head_used[u], 1)

                def keys(it, m):
                    n, kt = key_tile[m]
                    if kt == 0:
                        pe.wait_ge(s["expd"], it * TILES + (4 * n + 6))
                    pe.wait_ge(s["lo_done"], it * KEYS + (m + 1))
                    for j in range(4):
                        tr = pe.transpose(turn_ps[:, m % 2, j * P:(j + 1) * P], probs[:, n % 2, j, kt * P:(kt + 1) * P], ident[:])
                    tr.then_inc(s["turned"], 1)
                    if m >= LAG or not isinstance(it, int) or it:
                        product(it, m - LAG)

                def flush():
                    for m in range(KEYS - LAG, KEYS):
                        product(TURNS - 1, m)

                def turn_out(it, n):
                    pe.wait_ge(s["o_copied"], it * NGR + (n + 1))
                    for j in range(4):
                        tr = pe.transpose(out_ps[:, n % 2, j * P:(j + 1) * P], o_feat[:, n % 2, j * P:(j + 1) * P], ident[:])
                    tr.then_inc(s["o_turned"], 1)
                schedule(pe, score, keys, None, turn_out, None, lead=1, flush=flush)

            @block.scalar
            def _(act):
                act.sem_inc(s["expd"], 2)

                def score(it, x):
                    n, j = x // 4, x % 4
                    nk = group[n % NGR][3]
                    act.wait_ge(s["maxed"], it * TILES + (x + 1))
                    act.activation(probs[:, n % 2, j, 0:nk * P], score_ps[:, j % 2, 0:nk // 4].rearrange("p b t -> p (b t)"), ACT.Exp,
                                   bias=neg_max[:, n % 2, j:j + 1], accum_out=row_sum[:, n % NGR, j:j + 1]).then_inc(s["expd"], 1)

                def keys(it, m):
                    act.wait_ge(s["turned"], it * KEYS + (m + 1))
                    act.wait_ge(s["pv_done"], it * KEYS + (m + 1))
                    act.activation(turned_hi[:, m % 4], turn_ps[:, m % 2], ACT.Copy).then_inc(s["hi_done"], 1)

                def copy_out(it, n):
                    act.wait_ge(s["pv_done"], it * KEYS + (first_key[n + 1] + 4))
                    act.activation(o_feat[:, n % 2], out_ps[:, n % 2], ACT.Copy).then_inc(s["o_copied"], 1)
                    if n == 1 and not (isinstance(it, int) and it == 0):
                        store(it - 1)

                def store(it):
                    heads = bass.ds(it * 2, 2)
                    act.wait_ge(s["o_added"], it * NGR + (NGR + 2))
                    act.dma_start(io["at_s"].rearrange("p (t h d) -> p t h d", h=NQH, d=HD)[:, :, heads], attn[:, :, heads]).then_inc(s["stored"], 16)
                schedule(act, score, keys, copy_out, None, None)
                store(TURNS - 1)
                act.wait_ge(s["stored"], 16 * TURNS)

            @block.vector
            def _(dve):
                dve.sem_inc(s["lo_done"], 2)
                dve.sem_inc(s["o_scaled"], 2)

                def score(it, x):
                    n, j = x // 4, x % 4
                    dve.wait_ge(s["scored"], it * TILES + (x + 1))
                    dve.tensor_reduce(neg_max[:, n % 2, j:j + 1], score_ps[:, j % 2, 0:group[n % NGR][3] // 4].rearrange("p b t -> p (b t)"),
                                      AX.X, ALU.max, negate=True).then_inc(s["maxed"], 1)

                def keys(it, m):
                    dve.wait_ge(s["hi_done"], it * KEYS + (m + 1))
                    dve.tensor_tensor(turned_lo[:, m % 4], turn_ps[:, m % 2], f32(turned_hi[:, m % 4]), ALU.subtract).then_inc(s["lo_done"], 1)

                def scale_out(it, n):
                    dve.wait_ge(s["expd"], it * TILES + (4 * n + 6))
                    dve.reciprocal(inv_sum[:, n % 2], row_sum[:, n % NGR]).then_inc(s["inverted"], 1)
                    dve.wait_ge(s["inverted"], it * NGR + (n + 1))
                    dve.wait_ge(s["o_turned"], it * NGR + (n + 1))
                    dve.wait_ge(s["o_added"], it * NGR + (n + 1))
                    dve.tensor_tensor(o_tok[:, n % 2], out_ps[:, n % 2].rearrange("p (j d) -> p j d", j=4),
                                      along(inv_sum[:, n % 2], 2, P), ALU.mult).then_inc(s["o_scaled"], 1)
                schedule(dve, score, keys, None, None, scale_out, lead=1)

            @block.gpsimd
            def _(pool):
                pool.sem_inc(s["o_added"], 2)
                with pool.Fori(0, NQH // 2) as it:
                    for n in range(NGR):
                        u, q0, k0, nk = group[n]
                        pool.wait_ge(s["o_scaled"], it * NGR + (n + 3))
                        pool.tensor_tensor(attn[:, q0:q0 + 4, bass.ds(it * 2 + u, 1), :].rearrange("p t a d -> p t (a d)"),
                                           o_tok[:, n % 2, :, 0:HD], o_tok[:, n % 2, :, HD:P], ALU.add).then_inc(s["o_added"], 1)
    end_phase(nc, c)


LEVELS = [2 ** n for n in range(1, 7)]
FWD, BWD = range(2)


def deltanet(nc, io):
    NM = 3 + len(LEVELS)
    INCL, STRICT, NEG_M1 = range(3)
    EGC, TAIL, TOTAL = range(3)
    K_TOK, V_TOK, K_T, Q_T = range(4)
    NL = len(LEVELS)
    with ExitStack() as ctx:
        c = Core(nc, ctx, "deltanet")
        masks = c.sb("masks", [P, 2, NM, P])
        ident = c.sb("ident_d", [P, P])
        ones = c.sb("ones_d", [P, P])
        bg = c.sb("bg", [P, 2, NT, 2 * NH])
        pack = c.sb("pack_in", [P, 2, 2, 4, DNW])
        out = c.sb("dn_out", [P, 2, 2, DNW])

        def work(name):
            return c.sb(name, [P, 2, NH, P])

        def work2(name):
            return c.sb(name, [P, 2, 2, NH, P])
        g_cut, decay, decay_m, decay_b = (work(n) for n in ("g_cut", "decay", "decay_m", "decay_b"))
        low_t, qk_d, r = (work2(n) for n in ("low_t", "qk_d", "r_inv"))
        x_m = c.sb("x_m", [P, 2, NH, P // 2])
        t_inv, k_dec, z, v_new, state, q_state = (work(n) for n in ("t_inv", "k_dec", "z_in", "v_new", "state", "q_state"))
        x_last = c.sb("x_last", [P, 2, NH, P])
        small = c.sb("beta_g", [P, 2, 2, 2, NH])
        exps = c.sb("g_exps", [P, 2, 2, 3, NH])
        neg_egc = c.sb("neg_egc", [P, 2, 2, NH])
        ps = c.ps("dn_ps", [P, 2, 4, 512])
        BA, BB, BC, BD = range(4)

        names = ("small_done", "cut_done", "sums_mm", "sums_exp", "gates_mm", "exp_done", "decay_m_done", "decay_b_done", "neg_done", "kk_mm", "qk_mm",
                 "low_done", "qk_done", "r_masked", "r_init", "r_turned", "turned", "t_init", "t_upd", "r_upd", "r_final", "x_mm", "x_done", "tx_mm",
                 "k_dec_done", "ks_mm", "qs_mm", "z_done", "q_state_done", "y_mm", "v_new_done", "o_mm", "ktv_mm", "state_scaled",
                 "state_ready", "out_done")
        s = {n: c.sems2(n) for n in names}
        pack_in, out_stored = ([c.sems2(f"{n}{d}_") for d in range(2)] for n in ("pack_in", "out_stored"))
        const_in, set_done = c.sem("const_in"), c.sem("set_done")

        HALF = P // 2

        def side(a, which, b):
            return a.rearrange("p h (n s b) -> p h n s b", s=2, b=b)[:, :, :, which]

        def compact(bank, b):
            return bank[:, 0:NH * HALF].rearrange("p (h n b) -> p h n b", h=NH, b=b)

        def steps(eng, stages, before=None):
            def step(now, after):
                for stage, of_next in stages:
                    at = after if of_next else now
                    if at is not None:
                        q, p, i = at
                        base, n = SEQS[q]
                        for d in range(2):
                            stage(d, p, i + base, i + base if d == FWD else i * -1 + (base + n - 1), q)
            if before:
                before(0, 0)
            step(None, (0, 0, 0))
            for q, (base, n) in enumerate(SEQS):
                if before and q:
                    before(q, base)
                with eng.Fori(0, n // 2 - 1) as i:
                    for p in range(2):
                        step((q, p, i * 2 + p), (q, 1 - p, i * 2 + (p + 1)))
                step((q, 0, n - 2), (q, 1, n - 1))
                step((q, 1, n - 1), (q + 1, 0, 0) if q + 1 < len(SEQS) else None)

        with nc.Block("deltanet") as block:
            @block.sync
            def _(sp):
                sp.dma_start(masks[:].rearrange("p a m j -> p (a m j)"), io["masks"]).then_inc(const_in, 16)
                sp.dma_start(ident[:], io["ident"]).then_inc(const_in, 16)
                sp.dma_start(bg[:].rearrange("p a t n -> p (a t n)"), io["bg_s"]).then_inc(const_in, 16)

                def load(d, p, g, tile, q):
                    sp.wait_ge(s["ktv_mm"][d], g + 1)
                    sp.dma_start(pack[:, d, p].rearrange("p a n -> p (a n)"),
                                 io["dn_s"][bass.ds(tile, 1)].rearrange("a p n -> p (a n)")[:, 0:4 * DNW]).then_inc(pack_in[d][p], 16)

                def store(d, p, g, tile, q):
                    sp.wait_ge(s["out_done"][d], g + 1)
                    sp.dma_start(io["do_s"][d][bass.ds(tile, 1)].rearrange("a p n -> p (a n)"), out[:, d, p]).then_inc(out_stored[d][p], 16)
                steps(sp, [(load, True), (store, False)])
                for d in range(2):
                    for u in range(2):
                        sp.wait_ge(out_stored[d][u], 16 * (NT // 2 + 1))

            @block.tensor
            def _(pe):
                pe.wait_ge(const_in, 48)
                pe.wait_ge(set_done, 2)
                for d in range(2):
                    pe.sem_inc(s["ktv_mm"][d], 2)

                def heads(dst, lhs, rhs, width=P):
                    for h in range(NH):
                        mm = pe.matmul(dst[:, h * width:(h + 1) * width], lhs(h), rhs(h), start=True, stop=True)
                    return mm

                def block_of(a, d, p, which):
                    return lambda h: a[:, d, p, which, h * P:(h + 1) * P]

                def gate_sums(d, p, g, tile, q):
                    pe.wait_ge(s["small_done"][d], g + 1)
                    if not isinstance(g, int) or g:
                        pe.wait_ge(s["q_state_done"][d], g)
                    for n, lhs in enumerate((masks[:, d, INCL], masks[:, d, STRICT], ones[:])):
                        mm = pe.matmul(ps[:, d, BD, n * NH:(n + 1) * NH], lhs, small[:, d, p, 1], start=True, stop=True)
                    mm.then_inc(s["sums_mm"][d], 1)

                def gates(d, p, g, tile, q):
                    pe.wait_ge(s["cut_done"][d], g + 1)
                    pe.wait_ge(s["sums_exp"][d], g + 1)
                    heads(ps[:, d, BD], lambda h: g_cut[:, d, h], lambda h: masks[:, d, INCL]).then_inc(s["gates_mm"][d], 1)

                def key_products(d, p, g, tile, q):
                    pe.wait_ge(pack_in[d][p], uses(p, g, 16))
                    pe.wait_ge(s["exp_done"][d], g + 1)
                    heads(ps[:, d, BD], block_of(pack, d, p, K_T), block_of(pack, d, p, K_T)).then_inc(s["kk_mm"][d], 1)

                def query_products(d, p, g, tile, q):
                    pe.wait_ge(s["low_done"][d], g + 1)
                    heads(ps[:, d, BD], block_of(pack, d, p, K_T), block_of(pack, d, p, Q_T)).then_inc(s["qk_mm"][d], 1)

                def turn(d, src):
                    for h in range(NH):
                        tr = pe.transpose(ps[:, d, BA, h * P:(h + 1) * P], src[:, h], ident[:])
                    return tr

                def turn_r(d, p, g, tile, q):
                    pe.wait_ge(s["r_init"][d], g + 1)
                    turn(d, r[:, d, p]).then_inc(s["r_turned"][d], 1)

                def grow_x(n):
                    def stage(d, p, g, tile, q):
                        if n == 0:
                            pe.wait_ge(s["t_init"][d], g + 1)
                            pe.wait_ge(s["state_ready"][d], g + (q + 1))
                        else:
                            pe.wait_ge(s["t_upd"][d], g * (NL - 1) + n)
                            turn(d, t_inv[:, d]).then_inc(s["turned"][d], 1)
                        heads(ps[:, d, BB], lambda h: low_t[:, d, p, h],
                              lambda h: side(t_inv[:, d], d, LEVELS[n])[:, h], HALF).then_inc(s["x_mm"][d], 1)
                    return stage

                def grow_t(n):
                    def stage(d, p, g, tile, q):
                        pe.wait_ge(s["x_done"][d], g * NL + (n + 1))
                        if n:
                            pe.wait_ge(s["r_upd"][d], g * (NL - 1) + n)
                        if n < NL - 1:
                            heads(ps[:, d, BC], lambda h: r[:, d, p, h], lambda h: x_m[:, d, h], HALF).then_inc(s["tx_mm"][d], 1)
                        else:
                            heads(ps[:, d, BC], lambda h: x_last[:, d, h], lambda h: side(r[:, d, p], 1 - d, HALF)[:, h],
                                  HALF).then_inc(s["tx_mm"][d], 1)
                    return stage

                def state_products(d, p, g, tile, q):
                    pe.wait_ge(s["qk_done"][d], NT if isinstance(g, int) and g == NT - 1 else g + 2)
                    pe.wait_ge(s["q_state_done"][d], g + 1)
                    pe.wait_ge(s["state_ready"][d], g + (q + 1))
                    heads(ps[:, d, BB], block_of(pack, d, p, K_T), lambda h: state[:, d, h]).then_inc(s["ks_mm"][d], 1)
                    heads(ps[:, d, BD], block_of(pack, d, p, Q_T), lambda h: state[:, d, h]).then_inc(s["qs_mm"][d], 1)

                def solve(d, p, g, tile, q):
                    pe.wait_ge(s["r_final"][d], g + 1)
                    pe.wait_ge(s["z_done"][d], g + 1)
                    heads(ps[:, d, BC], lambda h: r[:, d, p, h], lambda h: z[:, d, h]).then_inc(s["y_mm"][d], 1)

                def new_products(d, p, g, tile, q):
                    pe.wait_ge(s["v_new_done"][d], g + 1)
                    pe.wait_ge(s["k_dec_done"][d], g + 1)
                    heads(ps[:, d, BB], lambda h: k_dec[:, d, h], lambda h: v_new[:, d, h]).then_inc(s["ktv_mm"][d], 1)
                    pe.wait_ge(s["t_init"][d], NT if isinstance(g, int) and g == NT - 1 else g + 2)
                    heads(ps[:, d, BA], lambda h: qk_d[:, d, p, h], lambda h: v_new[:, d, h]).then_inc(s["o_mm"][d], 1)

                before_t = {0: gate_sums, 3: key_products, 4: query_products}
                after_t = {0: gates, NL - 1: turn_r}
                stages = []
                for n in range(NL):
                    stages.append((grow_x(n), False))
                    if n in before_t:
                        stages.append((before_t[n], True))
                    stages.append((grow_t(n), False))
                    if n in after_t:
                        stages.append((after_t[n], True))
                steps(pe, stages + [(f, False) for f in (state_products, solve, new_products)])

            @block.scalar
            def _(act):
                for d in range(2):
                    act.sem_inc(s["q_state_done"][d], 1)

                def exp_sums(d, p, g, tile, q):
                    act.wait_ge(s["sums_mm"][d], g + 1)
                    act.activation(exps[:, d, p].rearrange("p a h -> p (a h)"), ps[:, d, BD, 0:3 * NH], ACT.Exp).then_inc(s["sums_exp"][d], 1)

                def exp_decay(d, p, g, tile, q):
                    act.wait_ge(s["gates_mm"][d], g + 1)
                    act.activation(decay[:, d].rearrange("p h t -> p (h t)"), ps[:, d, BD], ACT.Exp).then_inc(s["exp_done"][d], 1)

                def first_t(d, p, g, tile, q):
                    act.wait_ge(s["r_turned"][d], g + 1)
                    act.activation(t_inv[:, d].rearrange("p h t -> p (h t)"), ps[:, d, BA], ACT.Copy).then_inc(s["t_init"][d], 1)

                def copy_turned(n):
                    def stage(d, p, g, tile, q):
                        act.wait_ge(s["turned"][d], g * (NL - 1) + n)
                        act.activation(r[:, d, p].rearrange("p h t -> p (h t)"), ps[:, d, BA], ACT.Copy).then_inc(s["r_upd"][d], 1)
                    return stage

                def scale_q_state(d, p, g, tile, q):
                    act.wait_ge(s["qs_mm"][d], g + 1)
                    for h in range(NH):
                        op = act.activation(q_state[:, d, h], ps[:, d, BD, h * P:(h + 1) * P], ACT.Copy, scale=exps[:, d, p, EGC, h:h + 1])
                    op.then_inc(s["q_state_done"][d], 1)
                steps(act, [(exp_sums, True), (exp_decay, True)] + [(copy_turned(n), False) for n in range(1, NL)] +
                      [(first_t, True), (scale_q_state, False)])

            @block.vector
            def _(dve):
                dve.wait_ge(const_in, 48)

                def take_gates(d, p, g, tile, q):
                    dve.tensor_copy(small[:, d, p], bg[:, :, bass.ds(tile, 1), d * NH:(d + 1) * NH].rearrange("p a t n -> p a (t n)")).then_inc(s["small_done"][d], 1)

                def decay_kk(d, p, g, tile, q):
                    dve.wait_ge(s["kk_mm"][d], g + 1)
                    dve.wait_ge(s["decay_b_done"][d], g + 1)
                    dve.tensor_tensor(low_t[:, d, p], ps[:, d, BD].rearrange("p (h t) -> p h t", h=NH), decay_b[:, d], ALU.mult).then_inc(s["low_done"][d], 1)

                def decay_qk(d, p, g, tile, q):
                    dve.wait_ge(s["qk_mm"][d], g + 1)
                    dve.tensor_tensor(qk_d[:, d, p], ps[:, d, BD].rearrange("p (h t) -> p h t", h=NH), decay_m[:, d], ALU.mult).then_inc(s["qk_done"][d], 1)

                def mask_x(n):
                    def stage(d, p, g, tile, q):
                        dve.wait_ge(s["x_mm"][d], g * NL + (n + 1))
                        b = LEVELS[n]
                        dst = x_m[:, d].rearrange("p h (n b) -> p h n b", b=b) if n < NL - 1 else side(x_last[:, d], d, b)
                        mask = side(masks[:, d, 3 + n:4 + n], d, b).rearrange("p a n b -> p (a n) b")
                        dve.tensor_tensor(dst, compact(ps[:, d, BB], b), along(mask, 1, NH), ALU.mult).then_inc(s["x_done"][d], 1)
                    return stage

                def subtract(n):
                    def stage(d, p, g, tile, q):
                        dve.wait_ge(s["tx_mm"][d], g * NL + (n + 1))
                        if n < NL - 1:
                            dst, done = side(t_inv[:, d], d, LEVELS[n]), "t_upd"
                        else:
                            dst, done = side(r[:, d, p], 1 - d, HALF), "r_final"
                        dve.tensor_tensor(dst, dst, compact(ps[:, d, BC], LEVELS[n]), ALU.subtract).then_inc(s[done][d], 1)
                    return stage

                def make_z(d, p, g, tile, q):
                    dve.wait_ge(s["neg_done"][d], g + 1)
                    dve.wait_ge(s["ks_mm"][d], g + 1)
                    for h in range(NH):
                        op = dve.scalar_tensor_tensor(z[:, d, h], ps[:, d, BB, h * P:(h + 1) * P], neg_egc[:, d, p, h:h + 1],
                                                      pack[:, d, p, V_TOK, h * P:(h + 1) * P], ALU.mult, ALU.add)
                    op.then_inc(s["z_done"][d], 1)

                def make_v_new(d, p, g, tile, q):
                    dve.wait_ge(s["y_mm"][d], g + 1)
                    dve.tensor_tensor(v_new[:, d], ps[:, d, BC].rearrange("p (h t) -> p h t", h=NH), along(small[:, d, p, 0], 2, P),
                                      ALU.mult).then_inc(s["v_new_done"][d], 1)

                def update_state(d, p, g, tile, q):
                    dve.wait_ge(s["ktv_mm"][d], g + 3)
                    dve.wait_ge(s["state_scaled"][d], g + 1)
                    dve.tensor_tensor(state[:, d], state[:, d], ps[:, d, BB].rearrange("p (h t) -> p h t", h=NH), ALU.add).then_inc(s["state_ready"][d], 1)

                def outputs(d, p, g, tile, q):
                    dve.wait_ge(s["o_mm"][d], g + 1)
                    dve.wait_ge(s["q_state_done"][d], g + 2)
                    dve.wait_ge(out_stored[d][p], uses(p, g, 16))
                    dve.tensor_tensor(out[:, d, p], q_state[:, d].rearrange("p h t -> p (h t)"), ps[:, d, BA], ALU.add).then_inc(s["out_done"][d], 1)
                woven = {3: decay_kk, 4: decay_qk}
                stages = [(take_gates, True)]
                for n in range(NL):
                    stages.append((mask_x(n), False))
                    if n in woven:
                        stages.append((woven[n], True))
                    stages.append((subtract(n), False))
                steps(dve, stages + [(f, False) for f in (make_z, make_v_new, update_state, outputs)])

            @block.gpsimd
            def _(pool):
                pool.memset(ones[:], 1.0).then_inc(set_done, 1)
                pool.memset(x_last[:], 0.0).then_inc(set_done, 1)
                for d in range(2):
                    for u in range(2):
                        pool.sem_inc(out_stored[d][u], 16)
                pool.wait_ge(const_in, 48)

                def clear_state(q, base):
                    for d in range(2):
                        if q:
                            pool.wait_ge(s["state_ready"][d], base + q)
                        pool.memset(state[:, d], 0.0).then_inc(s["state_ready"][d], 1)

                def cut_gates(d, p, g, tile, q):
                    pool.wait_ge(s["small_done"][d], g + 1)
                    pool.tensor_tensor(g_cut[:, d], along(masks[:, d, STRICT], 1, NH), along(small[:, d, p, 1], 2, P), ALU.mult).then_inc(s["cut_done"][d], 1)

                def mask_decay(d, p, g, tile, q):
                    pool.wait_ge(s["exp_done"][d], g + 1)
                    pool.tensor_tensor(decay_m[:, d], decay[:, d], along(masks[:, d, INCL], 1, NH), ALU.mult).then_inc(s["decay_m_done"][d], 1)
                    pool.wait_ge(s["decay_m_done"][d], g + 1)
                    pool.tensor_tensor(decay_b[:, d], decay_m[:, d], along(small[:, d, p, 0], 2, P), ALU.mult).then_inc(s["decay_b_done"][d], 1)

                def first_r(d, p, g, tile, q):
                    pool.wait_ge(s["low_done"][d], g + 1)
                    pool.tensor_tensor(r[:, d, p], low_t[:, d, p], along(masks[:, d, NEG_M1], 1, NH), ALU.mult).then_inc(s["r_masked"][d], 1)
                    pool.wait_ge(s["r_masked"][d], g + 1)
                    pool.tensor_tensor(r[:, d, p], r[:, d, p], along(ident[:], 1, NH), ALU.add).then_inc(s["r_init"][d], 1)

                def decay_keys(d, p, g, tile, q):
                    pool.wait_ge(pack_in[d][p], uses(p, g, 16))
                    pool.wait_ge(s["ktv_mm"][d], g + 2)
                    pool.tensor_tensor(k_dec[:, d], pack[:, d, p, K_TOK].rearrange("p (h t) -> p h t", h=NH), along(exps[:, d, p, TAIL], 2, P),
                                       ALU.mult).then_inc(s["k_dec_done"][d], 1)
                    pool.tensor_scalar(neg_egc[:, d, p], exps[:, d, p, EGC], -1.0, None, ALU.mult).then_inc(s["neg_done"][d], 1)

                def scale_state(d, p, g, tile, q):
                    pool.wait_ge(s["qs_mm"][d], g + 1)
                    pool.tensor_tensor(state[:, d], state[:, d], along(exps[:, d, p, TOTAL], 2, P), ALU.mult).then_inc(s["state_scaled"][d], 1)
                steps(pool, [(cut_gates, True), (mask_decay, True), (decay_keys, False), (first_r, True), (scale_state, False)], clear_state)
    end_phase(nc, c)


def merge(nc, io):
    KB = NQH * HD // P
    with ExitStack() as ctx:
        c = Core(nc, ctx, "merge")
        x_hi = c.sb("branch_hi", [P, 2, KB, TOK], F32R)
        x_lo = c.sb("branch_lo", [P, 2, KB, TOK], F32R)
        dirs = c.sb("dn_dirs", [P, 2, 2, DNW])
        zt = c.sb("z_tok", [P, 2, DNW])
        at = c.sb("attn_in", [P, 2, DNW])
        osum = c.sb("dn_sum", [P, 2, NH, DH])
        osq = c.sb("dn_square", [P, 2, NH, DH])
        stat = c.sb("dn_stat", [P, 2, 3, NH])
        gain = c.sb("dn_gain", [P, DH])
        mhalf = c.sb("mhalf_e", [P, NH])
        ident = c.sb("ident_e", [P, P])
        raw = c.sb("wb_raw", [P, 2, 2, KB, P])
        whi = c.sb("wb_hi", [P, 2, 2, KB, P], F32R)
        wlo = c.sb("wb_lo", [P, 2, 2, KB, P], F32R)
        sig = c.sb("gate_sig", [P, 2, TOK])
        part = c.sb("branch_out", [P, 2, 2, TOK])
        turn_ps = c.ps("branch_turn", [P, 2, 512])
        acc = c.ps("branch_ps", [P, 2, NG, 512])

        tile_in, dirs_in = c.sems2("tile_in"), c.sems2("dirs_in")
        names = ("const_in", "mhalf_done", "passed", "summed", "squared", "reduced", "ms_done", "rstd_done", "normed", "gained",
                 "gated", "at_turned", "turned", "at_hi", "hi_done", "at_lo", "lo_done")
        s = {n: c.sem(n) for n in names}
        w_in, w_hi, w_ready, stored, added, sig_in, acc_done, acc_used = (c.sems2(n) for n in (
            "w_in", "w_hi", "w_ready", "stored", "added", "sig_in", "acc_done", "acc_used"))

        with nc.Block("merge") as block:
            @block.sync
            def _(sp):
                sp.dma_start(gain[:], io["dn_out_norm_g"][0].partition_broadcast(P)).then_inc(s["const_in"], 16)
                sp.dma_start(ident[:], io["ident"]).then_inc(s["const_in"], 16)

                def load_weights(u, i):
                    sp.wait_ge(w_ready[u], i + 1)
                    for b, w in enumerate(("w_attn_branch", "w_dn_branch")):
                        sp.dma_start(raw[:, u, b], io[w].rearrange("(k p) n -> p k n", p=P)[:, :, bass.ds(i * 256 + u * P, P)]).then_inc(w_in[u], 16)

                def load_gates(u, i):
                    for b in range(2):
                        sp.wait_ge(acc_used[b], i * 2 + (u + 1))
                        sp.dma_start(sig[:, b], io["gate_s"][bass.ds(i * 256 + (u * P + b * D), P), :]).then_inc(sig_in[b], 16)

                with sp.Fori(0, NT // 2) as i:
                    for u in range(2):
                        row = bass.ds(i * 2 + u, 1)
                        sp.wait_ge(s["summed"], i * 2 + (u + 1))
                        for d in range(2):
                            sp.dma_start(dirs[:, u, d], io["do_s"][d][row].rearrange("a p n -> p (a n)")).then_inc(dirs_in[u], 16)
                        sp.wait_ge(s["turned"], i * 2 + (u + 1))
                        sp.dma_start(zt[:, u], io["dn_s"][row].rearrange("a p n -> p (a n)")[:, 4 * DNW:5 * DNW]).then_inc(tile_in[u], 16)
                        sp.dma_start(at[:, u], io["at_s"][:, bass.ds(i * (2 * DNW) + u * DNW, DNW)]).then_inc(tile_in[u], 16)
                for u in range(2):
                    load_weights(u, 0)
                with sp.Fori(0, KD // 2 - 1) as i:
                    for u in range(2):
                        load_gates(u, i)
                        load_weights(u, i + 1)
                for u in range(2):
                    load_gates(u, KD // 2 - 1)

            @block.gpsimd
            def _(pool):
                for u in range(2):
                    pool.sem_inc(w_ready[u], 1)
                pool.memset(mhalf[:], -0.5).then_inc(s["mhalf_done"], 1)
                pool.wait_ge(s["mhalf_done"], 1)
                pool.wait_ge(s["const_in"], 32)

                def root(u, t):
                    pool.wait_ge(tile_in[u], uses(u, t, 32))
                    zh = zt[:, u].rearrange("p (h d) -> p h d", h=NH)
                    pool.tensor_tensor(zh, zh, along(gain[:], 1, NH), ALU.mult).then_inc(s["gained"], 1)
                    hold(pool, s["passed"], s["reduced"], t + 1)
                    pool.tensor_scalar(stat[:, u, 1], stat[:, u, 0], 1.0 / DH, EPS, ALU.mult, ALU.add).then_inc(s["ms_done"], 1)
                    pool.wait_ge(s["ms_done"], t + 1)
                    pool.tensor_tensor(stat[:, u, 2], stat[:, u, 1], mhalf[:], ALU.pow).then_inc(s["rstd_done"], 1)
                ahead(pool, NT, root, lambda u, t: None)

                def split(u, i):
                    pool.wait_ge(w_in[u], i * 32 + 32)
                    hold(pool, s["passed"], acc_done[u], i * 2 + 2)
                    pool.tensor_copy(whi[:, u], raw[:, u]).then_inc(w_hi[u], 1)
                    pool.wait_ge(w_hi[u], i + 1)
                    pool.tensor_tensor(wlo[:, u], raw[:, u], f32(whi[:, u]), ALU.subtract).then_inc(w_ready[u], 1)
                with pool.Fori(0, KD // 2) as i:
                    for u in range(2):
                        split(u, i)

            @block.tensor
            def _(pe):
                for u in range(2):
                    pe.sem_inc(acc_done[u], 2)
                pe.sem_inc(s["turned"], 2)
                pe.wait_ge(s["const_in"], 32)
                with pe.Fori(0, NT // 2) as i:
                    for u in range(2):
                        t = i * 2 + u
                        pe.wait_ge(s["lo_done"], t + 2)
                        pe.wait_ge(tile_in[u], i * 32 + 32)
                        for k in range(KB):
                            tr = pe.transpose(turn_ps[:, 0, k * P:(k + 1) * P], at[:, u, k * P:(k + 1) * P], ident[:])
                        tr.then_inc(s["at_turned"], 1)
                        pe.wait_ge(s["gated"], t + 1)
                        for k in range(KB):
                            tr = pe.transpose(turn_ps[:, 1, k * P:(k + 1) * P], osum[:, u, k], ident[:])
                        tr.then_inc(s["turned"], 1)
                pe.wait_ge(s["lo_done"], NT + 2)
                with pe.Fori(0, KD // 2) as i:
                    for u in range(2):
                        pe.wait_ge(w_ready[u], i + 2)
                        for b in range(2):
                            pe.wait_ge(acc_used[b], i * 2 + (u + 1))
                            split_matmuls(pe, [acc[:, b, g] for g in range(NG)],
                                          lambda k, g: (whi[:, u, b, k], wlo[:, u, b, k], x_hi[:, b, k, g * 512:(g + 1) * 512],
                                                        x_lo[:, b, k, g * 512:(g + 1) * 512]), KB).then_inc(acc_done[u], 1)

            @block.scalar
            def _(act):
                for u in range(2):
                    act.sem_inc(stored[u], 16)

                def square(u, t):
                    act.wait_ge(s["summed"], t + 3)
                    act.activation(osq[:, u], osum[:, u], ACT.Square).then_inc(s["squared"], 1)

                def copy_hi(u, t):
                    tok = bass.ds(t * P, P)
                    act.wait_ge(s["at_turned"], t + 1)
                    act.activation(x_hi[:, 0, :, tok], turn_ps[:, 0].rearrange("p (k t) -> p k t", k=KB), ACT.Copy).then_inc(s["at_hi"], 1)
                    act.wait_ge(s["turned"], t + 3)
                    act.activation(x_hi[:, 1, :, tok], turn_ps[:, 1].rearrange("p (k t) -> p k t", k=KB), ACT.Copy).then_inc(s["hi_done"], 1)
                ahead(act, NT, square, copy_hi)
                with act.Fori(0, KD // 2) as i:
                    for u in range(2):
                        act.wait_ge(added[u], i + 1)
                        act.dma_start(io["m_s"][:, :, bass.ds(i * 2 + u, 1), :].rearrange("t p a j -> p t (a j)"),
                                      part[:, u, 0].rearrange("p (t j) -> p t j", j=P)).then_inc(stored[u], 16)
                for u in range(2):
                    act.wait_ge(stored[u], 16 * (KD // 2 + 1))

            @block.vector
            def _(dve):
                dve.sem_inc(s["lo_done"], 2)
                dve.sem_inc(s["summed"], 2)
                for b in range(2):
                    dve.sem_inc(acc_used[b], 1)

                def sum_directions(u, t):
                    dve.wait_ge(dirs_in[u], uses(u, t, 32))
                    dve.wait_ge(s["turned"], t + 1)
                    dve.tensor_tensor(osum[:, u].rearrange("p h d -> p (h d)"), dirs[:, u, 0], dirs[:, u, 1], ALU.add).then_inc(s["summed"], 1)

                def norm_and_gate(u, t):
                    dve.wait_ge(s["rstd_done"], t + 1)
                    dve.tensor_tensor(osum[:, u], osum[:, u], along(stat[:, u, 2], 2, DH), ALU.mult).then_inc(s["normed"], 1)
                    dve.wait_ge(s["gained"], t + 1)
                    dve.wait_ge(s["normed"], t + 1)
                    dve.tensor_tensor(osum[:, u].rearrange("p h d -> p (h d)"), osum[:, u].rearrange("p h d -> p (h d)"), zt[:, u],
                                      ALU.mult).then_inc(s["gated"], 1)

                def reduce(u, t):
                    dve.wait_ge(s["squared"], t + 1)
                    dve.tensor_reduce(stat[:, u, 0], osq[:, u], AX.X, ALU.add).then_inc(s["reduced"], 1)

                def subtract_hi(u, t):
                    tok = bass.ds(t * P, P)
                    for b, (hi, lo) in enumerate((("at_hi", "at_lo"), ("hi_done", "lo_done"))):
                        dve.wait_ge(s[hi], t + 1)
                        dve.tensor_tensor(x_lo[:, b, :, tok], turn_ps[:, b].rearrange("p (k t) -> p k t", k=KB),
                                          f32(x_hi[:, b, :, tok]), ALU.subtract).then_inc(s[lo], 1)

                def finish(u, t):
                    norm_and_gate(u, t)
                    if not isinstance(t, int) or t + 1 < NT:
                        reduce(1 - u, t + 1)
                    subtract_hi(u, t)
                sum_directions(0, 0)
                reduce(0, 0)
                with dve.Fori(0, NT // 2 - 1) as i:
                    for u in range(2):
                        sum_directions(1 - u, i * 2 + (u + 1))
                        finish(u, i * 2 + u)
                sum_directions(1, NT - 1)
                finish(0, NT - 2)
                finish(1, NT - 1)
                with dve.Fori(0, KD // 2) as i:
                    for u in range(2):
                        for b in range(2):
                            dve.wait_ge(acc_done[u], i * 2 + (b + 3))
                            dve.wait_ge(sig_in[b], i * 32 + (u * 16 + 16))
                            if b == 0:
                                dve.wait_ge(stored[u], i * 16 + 16)
                            dve.tensor_tensor(part[:, u, b], acc[:, b].rearrange("p g t -> p (g t)"), sig[:, b], ALU.mult).then_inc(acc_used[b], 1)
                        for b in range(2):
                            dve.wait_ge(acc_used[b], i * 2 + (u + 2))
                        dve.tensor_tensor(part[:, u, 0], part[:, u, 0], part[:, u, 1], ALU.add).then_inc(added[u], 1)
    end_phase(nc, c)


def mix_out(nc, io):
    with ExitStack() as ctx:
        c = Core(nc, ctx, "mix")
        whi = c.sb("wo_hi", [P, KD, D], F32R)
        wlo = c.sb("wo_lo", [P, KD, D], F32R)
        raw = c.sb("wo_raw", [P, KD, D])
        mt = c.sb("merged_in", [P, 2, KD, P])
        mhi = c.sb("merged_hi", [P, 2, KD, P], F32R)
        mlo = c.sb("merged_lo", [P, 2, KD, P], F32R)
        xt = c.sb("x_res", [P, 2, D])
        h = c.sb("h_tok", [P, 2, D])
        hn = c.sb("h_normed", [P, 2, D])
        junk = c.sb("squares_f", [P, 2, D])
        ht = c.sb("h_turned", [P, 2, KD, P])
        gains = c.sb("gains_f", [P, 2, D])
        stat = c.sb("stat_f", [P, 2, 2, 3])
        mhalf = c.sb("mhalf_f", [P, 1])
        ident = c.sb("ident_f", [P, P])
        acc = c.ps("mix_ps", [P, 2, 2, 512])
        turn_ps = c.ps("h_turn", [P, 2, 2, 512])
        m_in, x_in, stored, raw_in = c.sems2("m_in"), c.sems2("x_in"), c.sems2("stored"), [c.sem(f"raw_in{k}") for k in range(KD)]
        names = ("const_in", "mhalf_done", "passed", "w_hi", "w_lo", "m_hi", "m_lo", "products", "post_sq", "post_ms", "post_rstd",
                 "post_normed", "h_done", "pre_sq", "pre_ms", "pre_rstd", "pre_normed", "turned", "copied")
        s = {n: c.sem(n) for n in names}

        with nc.Block("mix_out") as block:
            @block.sync
            def _(sp):
                sp.dma_start(gains[:, 0], io["ln1_post_g"][0].partition_broadcast(P)).then_inc(s["const_in"], 16)
                sp.dma_start(gains[:, 1], io["ln2_pre_g"][0].partition_broadcast(P)).then_inc(s["const_in"], 16)
                sp.dma_start(ident[:], io["ident"]).then_inc(s["const_in"], 16)

                def load(u, t):
                    row, tok = bass.ds(t, 1), bass.ds(t * P, P)
                    sp.wait_ge(s["m_lo"], t + 1)
                    sp.dma_start(mt[:, u].rearrange("p k t -> p (k t)"), io["m_s"][row].rearrange("a p k t -> p (a k t)")).then_inc(m_in[u], 16)
                    sp.wait_ge(s["h_done"], t + 1)
                    sp.dma_start(xt[:, u], io["x"][tok, :]).then_inc(x_in[u], 16)
                load(0, 0)
                for k in range(KD):
                    sp.dma_start(raw[:, k], io["w_out"][k * P:(k + 1) * P, :]).then_inc(raw_in[k], 16)
                load(1, 1)
                with sp.Fori(1, NT // 2) as i:
                    for u in range(2):
                        load(u, i * 2 + u)

            @block.gpsimd
            def _(pool):
                pool.sem_inc(s["m_lo"], 2)
                pool.memset(mhalf[:], -0.5).then_inc(s["mhalf_done"], 1)
                pool.wait_ge(s["mhalf_done"], 1)

                def subtract_hi(u, t):
                    pool.wait_ge(s["m_hi"], t + 1)
                    pool.tensor_tensor(mlo[:, u], mt[:, u], f32(mhi[:, u]), ALU.subtract).then_inc(s["m_lo"], 1)

                def root(u, t, n, name):
                    hold(pool, s["passed"], s[name + "_sq"], t + 1)
                    pool.tensor_scalar(stat[:, u, n, 1:2], stat[:, u, n, 0:1], 1.0 / D, EPS, ALU.mult, ALU.add).then_inc(s[name + "_ms"], 1)
                    pool.wait_ge(s[name + "_ms"], t + 1)
                    pool.tensor_tensor(stat[:, u, n, 2:3], stat[:, u, n, 1:2], mhalf[:], ALU.pow).then_inc(s[name + "_rstd"], 1)

                def norms(u, t):
                    root(u, t, 0, "post")
                    if not isinstance(t, int) or t + 2 < NT:
                        subtract_hi(u, t + 2)
                    root(u, t, 1, "pre")
                for t in range(2):
                    subtract_hi(t, t)
                ahead(pool, NT, norms, lambda u, t: None, peel=2)

            @block.tensor
            def _(pe):
                pe.wait_ge(s["const_in"], 48)

                def products(u, t):
                    pe.wait_ge(s["m_lo"], t + 3)
                    pe.wait_ge(s["post_normed"], t + 1)
                    for k in range(KD):
                        if isinstance(t, int) and t == 0:
                            pe.wait_ge(s["w_lo"], k + 1)
                        for first, (x, w) in enumerate(((mhi, whi), (mhi, wlo), (mlo, whi))):
                            for b in range(2):
                                mm = pe.matmul(acc[:, u, b], x[:, u, k], w[:, k, b * 512:(b + 1) * 512], start=k == 0 and first == 0,
                                               stop=k == KD - 1 and first == 2)
                    mm.then_inc(s["products"], 1)

                def turn(u, t):
                    pe.wait_ge(s["pre_normed"], t + 1)
                    pe.wait_ge(s["copied"], t + 1)
                    for k in range(KD):
                        tr = pe.transpose(turn_ps[:, u, k // 4, (k % 4) * P:(k % 4 + 1) * P], hn[:, u, k * P:(k + 1) * P], ident[:])
                    tr.then_inc(s["turned"], 1)
                ahead(pe, NT, products, turn)

            @block.scalar
            def _(act):
                for u in range(2):
                    act.sem_inc(stored[u], 32)
                act.sem_inc(s["copied"], 2)

                def merged_hi(u, t):
                    act.wait_ge(m_in[u], uses(u, t, 16))
                    act.activation(mhi[:, u], mt[:, u], ACT.Copy).then_inc(s["m_hi"], 1)
                merged_hi(0, 0)
                for k in range(KD):
                    act.wait_ge(raw_in[k], 16)
                    act.activation(whi[:, k], raw[:, k], ACT.Copy).then_inc(s["w_hi"], 1)
                merged_hi(1, 1)

                def squares(u, t):
                    act.wait_ge(s["products"], t + 1)
                    act.activation(junk[:, 0], acc[:, u].rearrange("p b n -> p (b n)"), ACT.Square, accum_out=stat[:, u, 0, 0:1]).then_inc(s["post_sq"], 1)
                    if not isinstance(t, int) or t + 2 < NT:
                        merged_hi(u, t + 2)
                    act.wait_ge(s["h_done"], t + 3)
                    act.activation(junk[:, 1], h[:, u], ACT.Square, accum_out=stat[:, u, 1, 0:1]).then_inc(s["pre_sq"], 1)

                def store(u, t):
                    act.wait_ge(s["turned"], t + 1)
                    act.wait_ge(stored[u], uses(u, t, 32))
                    act.activation(ht[:, u].rearrange("p k t -> p (k t)"), turn_ps[:, u].rearrange("p b n -> p (b n)"), ACT.Copy).then_inc(s["copied"], 1)
                    act.wait_ge(s["copied"], t + 3)
                    act.dma_start(io["ht_s"][:, :, bass.ds(t * P, P)].rearrange("k p t -> p k t"), ht[:, u]).then_inc(stored[u], 16)
                    act.dma_start(io["h_s"][bass.ds(t * P, P), :], h[:, u]).then_inc(stored[u], 16)
                ahead(act, NT, squares, store, peel=2)
                for u in range(2):
                    act.wait_ge(stored[u], 32 * (NT // 2 + 1))

            @block.vector
            def _(dve):
                dve.sem_inc(s["h_done"], 2)
                dve.sem_inc(s["post_normed"], 2)
                for k in range(KD):
                    dve.wait_ge(s["w_hi"], k + 1)
                    dve.tensor_tensor(wlo[:, k], raw[:, k], f32(whi[:, k]), ALU.subtract).then_inc(s["w_lo"], 1)
                dve.wait_ge(s["const_in"], 48)
                with dve.Fori(0, NT // 2) as i:
                    for u in range(2):
                        t = i * 2 + u
                        dve.wait_ge(s["post_rstd"], t + 1)
                        dve.wait_ge(stored[u], i * 32 + 32)
                        dve.scalar_tensor_tensor(h[:, u], acc[:, u].rearrange("p b n -> p (b n)"), stat[:, u, 0, 2:3], gains[:, 0],
                                                 ALU.mult, ALU.mult).then_inc(s["post_normed"], 1)
                        dve.wait_ge(x_in[u], i * 16 + 16)
                        dve.wait_ge(s["post_normed"], t + 3)
                        dve.tensor_tensor(h[:, u], h[:, u], xt[:, u], ALU.add).then_inc(s["h_done"], 1)
                        dve.wait_ge(s["pre_rstd"], t + 1)
                        dve.scalar_tensor_tensor(hn[:, u], h[:, u], stat[:, u, 1, 2:3], gains[:, 1], ALU.mult, ALU.mult).then_inc(s["pre_normed"], 1)
    end_phase(nc, c)


def ff_in(nc, io):
    with ExitStack() as ctx:
        c = Core(nc, ctx, "ff_in")
        x_hi = c.sb("ffx_hi", [P, KD, TOK], F32R)
        x_lo = c.sb("ffx_lo", [P, KD, TOK], F32R)
        xraw = c.sb("ffx_raw", [P, KD, TOK])
        raw = c.sb("w1_raw", [P, 2, KD, P])
        whi = c.sb("w1_hi", [P, 2, KD, P], F32R)
        wlo = c.sb("w1_lo", [P, 2, KD, P], F32R)
        stage = c.sb("ff_stage", [P, 2, TOK])
        acc = c.ps("ff_ps", [P, 2, NG, 512])
        names = ("passed", "x_hi", "x_lo")
        s = {n: c.sem(n) for n in names}
        x_in = [c.sem(f"x_in{k}") for k in range(KD)]
        w_in, w_hi, w_ready, acc_done, acc_used, squared, stored = (c.sems2(n) for n in (
            "w_in", "w_hi", "w_ready", "acc_done", "acc_used", "squared", "stored"))

        with nc.Block("ff_in") as block:
            @block.sync
            def _(sp):
                def load(u, i):
                    sp.wait_ge(w_ready[u], i + 1)
                    sp.dma_start(raw[:, u], io["w_ff_in"].rearrange("(k p) n -> p k n", p=P)[:, :, bass.ds(i * 256 + u * P, P)]).then_inc(w_in[u], 16)
                load(0, 0)
                for k in range(KD):
                    sp.dma_start(xraw[:, k], io["ht_s"][k]).then_inc(x_in[k], 16)
                load(1, 0)
                with sp.Fori(1, DFF // 256) as i:
                    for u in range(2):
                        load(u, i)

            @block.gpsimd
            def _(pool):
                for u in range(2):
                    pool.sem_inc(w_ready[u], 1)
                with pool.Fori(0, DFF // 256) as i:
                    for u in range(2):
                        pool.wait_ge(w_in[u], i * 16 + 16)
                        hold(pool, s["passed"], acc_done[u], i + 1)
                        pool.tensor_copy(whi[:, u], raw[:, u]).then_inc(w_hi[u], 1)
                        pool.wait_ge(w_hi[u], i + 1)
                        pool.tensor_tensor(wlo[:, u], raw[:, u], f32(whi[:, u]), ALU.subtract).then_inc(w_ready[u], 1)

            @block.tensor
            def _(pe):
                for u in range(2):
                    pe.sem_inc(acc_done[u], 1)

                def products(u, i, ahead_of_k=None):
                    pe.wait_ge(w_ready[u], i + 2)
                    pe.wait_ge(acc_used[u], i + 1)
                    split_matmuls(pe, [acc[:, u, g] for g in range(NG)],
                                  lambda k, g: (whi[:, u, k], wlo[:, u, k], x_hi[:, k, g * 512:(g + 1) * 512],
                                                x_lo[:, k, g * 512:(g + 1) * 512]), KD, ahead_of_k).then_inc(acc_done[u], 1)
                products(0, 0, lambda k: pe.wait_ge(s["x_lo"], k + 1))
                products(1, 0)
                with pe.Fori(1, DFF // 256) as i:
                    for u in range(2):
                        products(u, i)

            @block.scalar
            def _(act):
                for u in range(2):
                    act.sem_inc(acc_used[u], 1)
                    act.sem_inc(stored[u], 16)
                for k in range(KD):
                    act.wait_ge(x_in[k], 16)
                    act.activation(x_hi[:, k], xraw[:, k], ACT.Copy).then_inc(s["x_hi"], 1)
                with act.Fori(0, DFF // 256) as i:
                    for u in range(2):
                        act.wait_ge(acc_done[u], i + 2)
                        act.wait_ge(stored[u], i * 16 + 16)
                        act.activation(stage[:, u], acc[:, u].rearrange("p g t -> p (g t)"), ACT.Relu).then_inc(acc_used[u], 1)
                        act.wait_ge(acc_used[u], i + 2)
                        act.activation(stage[:, u], stage[:, u], ACT.Square).then_inc(squared[u], 1)
                        act.wait_ge(squared[u], i + 1)
                        act.dma_start(io["hid_s"][:, :, bass.ds(i * 2 + u, 1), :].rearrange("t p a j -> p t (a j)"),
                                      stage[:, u].rearrange("p (t j) -> p t j", j=P)).then_inc(stored[u], 16)
                for u in range(2):
                    act.wait_ge(stored[u], 16 * (DFF // 256 + 1))

            @block.vector
            def _(dve):
                for k in range(KD):
                    dve.wait_ge(s["x_hi"], k + 1)
                    dve.tensor_tensor(x_lo[:, k], xraw[:, k], f32(x_hi[:, k]), ALU.subtract).then_inc(s["x_lo"], 1)
    end_phase(nc, c)


def ff_out(nc, io):
    KF = DFF // P
    HC = D // 2
    UNIT = 1024
    RING = 4
    WK, HK = UNIT // HC, UNIT // P
    PARTS = KF // WK
    UNITS = PARTS + 4 * NT
    MID = PARTS // 2
    w_parts = [("w", n) for n in range(PARTS)]
    h_chunks = [("h", n) for n in range(4)]
    OPENING = (h_chunks[0:1] + w_parts[:MID] + h_chunks[1:3] + w_parts[MID:] + h_chunks[3:],
               w_parts[:MID] + h_chunks[0:1] + w_parts[MID:] + h_chunks[1:])
    ARRIVED = []
    for order in OPENING:
        sizes = [1 if kind == "w" else 2 for kind, _ in order]
        ARRIVED.append({item: sum(sizes[:n + 1]) for n, item in enumerate(order)})
    with ExitStack() as ctx:
        c = Core(nc, ctx, "ff_out")
        whi = c.sb("w2_hi", [P, KF, HC], F32R)
        wlo = c.sb("w2_lo", [P, KF, HC], F32R)
        raw = c.sb("ff_raw", [P, RING, UNIT])
        hhi = c.sb("hid_hi", [P, 2, KF // 2, P], F32R)
        hlo = c.sb("hid_lo", [P, 2, KF // 2, P], F32R)
        y0 = c.sb("y_half", [P, 2, HC])
        h = c.sb("h_in", [P, 2, D])
        out = c.sb("y_out", [P, D])
        gain = c.sb("gain_g", [P, D])
        stat = c.sb("stat_g", [P, 2, 4])
        mhalf = c.sb("mhalf_g", [P, 1])
        acc = c.ps("y_ps", [P, 4, 512])
        junk = c.ps("squares_g", [P, 2, HC])
        raw_in = [c.sem(f"raw_in{n}") for n in range(RING)]
        y_stored, h_in = c.sems2("y_stored"), c.sems2("h_in")
        names = ("const_in", "mhalf_done", "passed", "hi_done", "lo_done", "products", "w_passed", "squared", "sum_done", "ms_done",
                 "rstd_done", "acc_used", "normed", "added", "out_stored")
        s = {n: c.sem(n) for n in names}

        def opens(t):
            return isinstance(t, int) and t < 2

        def bank(u, t):
            return 2 + t if opens(t) else u

        def ring(eng, w_unit, h_unit, done):
            def opening(half):
                for kind, n in OPENING[half]:
                    first = half * UNITS + ARRIVED[half][kind, n] - (1 if kind == "w" else 2)
                    if kind == "w":
                        w_unit(half, n, first)
                        if half and n == PARTS - 1:
                            done(0, 1, NT - 1)
                    else:
                        for part in range(2):
                            h_unit(half, n % 2, n // 2, part, n, (first + part) % RING, first + part)

            def hidden(half, t):
                for kh in range(2):
                    for part in range(2):
                        r = 2 * kh + part
                        h_unit(half, t, kh, part, t * 2 + kh, r, t * 4 + (half * UNITS + PARTS + r))
            for half in range(2):
                opening(half)
                hidden(half, 2)
                done(half, 0, 0)
                done(half, 1, 1)
                with eng.Fori(1, NT // 2 - 1) as i:
                    for u in range(2):
                        hidden(half, i * 2 + (u + 1))
                        done(half, u, i * 2 + u)
                hidden(half, NT - 1)
                done(half, 0, NT - 2)
            done(1, 1, NT - 1)

        with nc.Block("ff_out") as block:
            @block.sync
            def _(sp):
                def load_part(half, n, unit):
                    sp.wait_ge(s["lo_done"], unit + 1)
                    sp.dma_start(raw[:, unit % RING].rearrange("p (k j) -> p k j", k=WK),
                                 io["w_ff_out"].rearrange("(k p) n -> p k n", p=P)[:, WK * n:WK * (n + 1), half * HC:(half + 1) * HC]).then_inc(raw_in[unit % RING], 16)

                def load_hidden(half, t, kh, part, chunk, r, unit):
                    sp.wait_ge(s["lo_done"], unit + 1)
                    k0 = kh * KF // 2 + part * HK
                    sp.dma_start(raw[:, r].rearrange("p (k j) -> p k j", j=P),
                                 io["hid_s"][bass.ds(t, 1)].rearrange("a p k j -> p (a k) j")[:, k0:k0 + HK, :]).then_inc(raw_in[r], 16)

                def load_rest(half, u, t):
                    if half:
                        if opens(t):
                            sp.wait_ge(y_stored[u], 16 * (NT // 2 + 1))
                        else:
                            sp.wait_ge(s["added"], t + 1)
                        sp.dma_start(y0[:, u], io["y0_s"][bass.ds(t * P, P), :]).then_inc(h_in[u], 16)
                        sp.dma_start(h[:, u], io["h_s"][bass.ds(t * P, P), :]).then_inc(h_in[u], 16)
                sp.dma_start(gain[:], io["ln2_post_g"][0].partition_broadcast(P)).then_inc(s["const_in"], 16)
                ring(sp, load_part, load_hidden, load_rest)

            @block.tensor
            def _(pe):
                pe.sem_inc(s["products"], 2)

                def products(u, t, kh, parts=None, passed=False):
                    for n in range(kh * MID, (kh + 1) * MID):
                        if parts:
                            pe.wait_ge(s["lo_done"], parts[n] + RING)
                        for w in range(WK * n, WK * (n + 1)):
                            k = w - kh * KF // 2
                            for first, (x, y) in enumerate(((hhi, whi), (hhi, wlo), (hlo, whi))):
                                mm = pe.matmul(acc[:, bank(u, t)], x[:, (t if opens(t) else kh), k], y[:, w], start=w == 0 and first == 0,
                                               stop=w == KF - 1 and first == 2)
                        if passed:
                            mm.then_inc(s["w_passed"], 1)
                    if passed:
                        pe.wait_ge(s["w_passed"], (kh + 1) * MID)
                        pe.sem_inc(s["products"], 1)
                    else:
                        mm.then_inc(s["products"], 1)

                def tile(half, u, t, used, passed=False):
                    pe.wait_ge(s["acc_used"], used)
                    for kh in range(2):
                        pe.wait_ge(s["lo_done"], t * 4 + (half * UNITS + PARTS + 2 * kh + 2 + RING))
                        products(u, t, kh, passed=passed)

                for half in range(2):
                    come = ARRIVED[half]
                    for kh in range(2):
                        for t in range(2):
                            pe.wait_ge(s["lo_done"], half * UNITS + come["h", 2 * kh + t] + RING)
                            products(t, t, kh, None if t else {n: half * UNITS + come["w", n] for n in range(PARTS)})
                    for u in range(2):
                        tile(half, u, 2 + u, half * NT + 2)
                    last = NT // 2 if half else NT // 2 - 1
                    with pe.Fori(2, last) as i:
                        for u in range(2):
                            tile(half, u, i * 2 + u, i * 2 + (u + half * NT + 1))
                    if not half:
                        for u in range(2):
                            tile(half, u, NT - 2 + u, NT - 1 + u, passed=u == 1)

            @block.scalar
            def _(act):
                for u in range(2):
                    act.sem_inc(y_stored[u], 16)
                act.sem_inc(s["out_stored"], 16)

                def part_hi(half, n, unit):
                    act.wait_ge(raw_in[unit % RING], (unit // RING + 1) * 16)
                    if half:
                        act.wait_ge(s["w_passed"], n + 1)
                    act.activation(whi[:, WK * n:WK * (n + 1)].rearrange("p k j -> p (k j)"), raw[:, unit % RING], ACT.Copy).then_inc(s["hi_done"], 1)

                def hidden_hi(half, t, kh, part, chunk, r, unit):
                    if isinstance(unit, int):
                        act.wait_ge(raw_in[r], (unit // RING + 1) * 16)
                    else:
                        act.wait_ge(raw_in[r], (t + (half * UNITS + PARTS) // RING + 1) * 16)
                    act.wait_ge(s["products"], chunk + (half * 2 * NT + 1))
                    act.activation(hhi[:, t if opens(t) else kh, part * HK:(part + 1) * HK].rearrange("p k j -> p (k j)"), raw[:, r],
                                   ACT.Copy).then_inc(s["hi_done"], 1)

                def keep(u, t):
                    act.wait_ge(s["products"], 6 if opens(t) else t * 2 + 4)
                    act.wait_ge(y_stored[u], uses(u, t, 16))
                    act.activation(y0[:, u], acc[:, bank(u, t)], ACT.Copy).then_inc(s["acc_used"], 1)
                    act.wait_ge(s["acc_used"], t + 3)
                    act.dma_start(io["y0_s"][bass.ds(t * P, P), :], y0[:, u]).then_inc(y_stored[u], 16)

                def finish(u, t):
                    act.wait_ge(s["products"], 2 * NT + 6 if opens(t) else t * 2 + (2 * NT + 4))
                    act.activation(junk[:, 0], acc[:, bank(u, t)], ACT.Square, accum_out=stat[:, u, 0:1])
                    act.wait_ge(h_in[u], uses(u, t, 32))
                    act.activation(junk[:, 1], y0[:, u], ACT.Square, accum_out=stat[:, u, 1:2]).then_inc(s["squared"], 1)
                    act.wait_ge(s["added"], t + 3)
                    act.dma_start(io["y"][bass.ds(t * P, P), :], out[:]).then_inc(s["out_stored"], 16)
                ring(act, part_hi, hidden_hi, lambda half, u, t: (finish if half else keep)(u, t))
                act.wait_ge(s["out_stored"], 16 * (NT + 1))

            @block.vector
            def _(dve):
                dve.sem_inc(s["lo_done"], RING)
                dve.sem_inc(s["acc_used"], 2)
                dve.sem_inc(s["added"], 2)
                dve.wait_ge(s["const_in"], 16)

                def part_lo(half, n, unit):
                    dve.wait_ge(s["hi_done"], unit + 1)
                    dve.tensor_tensor(wlo[:, WK * n:WK * (n + 1)].rearrange("p k j -> p (k j)"), raw[:, unit % RING],
                                      f32(whi[:, WK * n:WK * (n + 1)]).rearrange("p k j -> p (k j)"), ALU.subtract).then_inc(s["lo_done"], 1)

                def hidden_lo(half, t, kh, part, chunk, r, unit):
                    dve.wait_ge(s["hi_done"], unit + 1)
                    b, ks = (t if opens(t) else kh), slice(part * HK, (part + 1) * HK)
                    dve.tensor_tensor(hlo[:, b, ks].rearrange("p k j -> p (k j)"), raw[:, r],
                                      f32(hhi[:, b, ks]).rearrange("p k j -> p (k j)"), ALU.subtract).then_inc(s["lo_done"], 1)

                def finish(half, u, t):
                    if half:
                        dve.wait_ge(s["rstd_done"], t + 1)
                        dve.wait_ge(s["out_stored"], t * 16 + 16)
                        dve.scalar_tensor_tensor(out[:, 0:HC], y0[:, u], stat[:, u, 3:4], gain[:, 0:HC], ALU.mult, ALU.mult).then_inc(s["normed"], 1)
                        dve.scalar_tensor_tensor(out[:, HC:D], acc[:, bank(u, t)], stat[:, u, 3:4], gain[:, HC:D], ALU.mult, ALU.mult).then_inc(s["acc_used"], 1)
                        dve.wait_ge(s["normed"], t + 1)
                        dve.wait_ge(s["acc_used"], t + (NT + 3))
                        dve.tensor_tensor(out[:], out[:], h[:, u], ALU.add).then_inc(s["added"], 1)
                ring(dve, part_lo, hidden_lo, finish)

            @block.gpsimd
            def _(pool):
                pool.memset(mhalf[:], -0.5).then_inc(s["mhalf_done"], 1)
                pool.wait_ge(s["mhalf_done"], 1)
                with pool.Fori(0, NT // 2) as i:
                    for u in range(2):
                        t = i * 2 + u
                        pool.wait_ge(s["squared"], t + 1)
                        pool.tensor_tensor(stat[:, u, 2:3], stat[:, u, 0:1], stat[:, u, 1:2], ALU.add).then_inc(s["sum_done"], 1)
                        hold(pool, s["passed"], s["sum_done"], t + 1)
                        pool.tensor_scalar(stat[:, u, 2:3], stat[:, u, 2:3], 1.0 / D, EPS, ALU.mult, ALU.add).then_inc(s["ms_done"], 1)
                        pool.wait_ge(s["ms_done"], t + 1)
                        pool.tensor_tensor(stat[:, u, 3:4], stat[:, u, 2:3], mhalf[:], ALU.pow).then_inc(s["rstd_done"], 1)
    end_phase(nc, c)


PHASES = [project, prepare, attend, deltanet, merge, mix_out, ff_in, ff_out]
SCRATCH = {"qkv_s": (QKV_W, TOK), "dqkv_s": (3 * DNW, TOK), "z_s": (DNW, TOK), "ba_s": (4 * NH, TOK),
           "gate_s": (2 * D, TOK), "q_s": (NQH, P, TOK), "k_s": (2 * NKVH, P, TOK), "v_s": (NKVH, P, NT, P),
           "dn_s": (NT, P, 5 * DNW), "bg_s": (P, 2 * NT * 2 * NH), "at_s": (P, NT * NQH * HD), "do_s": (2, NT, P, DNW),
           "m_s": (NT, P, KD, P), "h_s": (TOK, D), "ht_s": (KD, P, TOK), "hid_s": (NT, P, DFF // P, P), "y0_s": (TOK, D // 2)}


def program(nc, io):
    for phase in PHASES:
        phase(nc, io)


def constants():
    tok = np.concatenate([np.arange(T0), np.arange(T1)]).astype(np.float32)
    inv = (np.float32(10000.0) ** (-np.arange(0, 32, 2, dtype=np.float32) / np.float32(32))).astype(np.float32)
    angles = [np.floor(tok / GRID_W)[:, None] * inv, (tok % GRID_W)[:, None] * inv]
    cos = np.concatenate([np.cos(a) for a in angles for _ in range(2)], 1)
    sin = np.concatenate([sign * np.sin(a) for a in angles for sign in (-1, 1)], 1)
    a, b = np.arange(P)[:, None], np.arange(P)[None]
    level = {w: (a // (2 * w) == b // (2 * w)) & (a % (2 * w) >= w) & (b % (2 * w) < w) for w in [1] + LEVELS}
    fwd = [a <= b, a > b, -1.0 * level[1].T] + [level[w] for w in LEVELS]
    bwd = [a >= b, a < b, -1.0 * level[1]] + [level[w].T for w in LEVELS]
    masks = np.stack([np.asarray(m, np.float32) for m in fwd + bwd], 1).reshape(P, -1)
    return {"masks": masks, "ident": np.eye(P, dtype=np.float32), "rope": np.concatenate([cos, sin], 1).astype(np.float32)}


def kernel(**inputs):
    import concourse.bacc as bacc
    from concourse.bass_utils import run_bass_kernel_spmd

    nc = bacc.Bacc("TRN2", target_bir_lowering=False, num_devices=1)
    arrays = {k: np.ascontiguousarray(v) for k, v in inputs.items() if k not in ("x_prompt", "x_sample", "dn_conv_w")}
    arrays = {k: v[0] if v.shape[0] == 1 and v.ndim == 3 else v for k, v in arrays.items()}
    arrays["x"] = np.concatenate([np.asarray(inputs["x_prompt"])[0], np.asarray(inputs["x_sample"])[0]])
    arrays["conv_w"] = np.ascontiguousarray(np.asarray(inputs["dn_conv_w"])[0].T)
    arrays |= constants()
    io = {k: nc.dram_tensor(f"in_{k}", v.shape, F32, kind="ExternalInput").ap() for k, v in arrays.items()}
    for k, shape in SCRATCH.items():
        io[k] = nc.dram_tensor(f"s_{k}", shape, F32, kind="Internal").ap()
    io["y"] = nc.dram_tensor("y", (TOK, D), F32, kind="ExternalOutput").ap()
    program(nc, io)
    r = run_bass_kernel_spmd(nc, [{f"in_{k}": v for k, v in arrays.items()}], core_ids=[0]).results[0]
    return r["y"][None, :T0], r["y"][None, T0:]
```
